# Optimizing a Trainium2 kernel written in Bass

```python
import math
import jax, jax.numpy as jnp
from jax import lax
import numpy as np

D_MODEL = 1024
BATCH = 1
SEQ = 512
DEPTH = 1
DEC_BATCH = 8
DEC_SEQ = 1
PAST_LEN = 2048
PAGE_SIZE = 128

N_Q_HEADS = 8
N_KV_HEADS = 2
Q_PER_KV = N_Q_HEADS // N_KV_HEADS
HEAD_DIM = 64
WINDOW = 128
Q_BLOCK = 128
N_BUCKETS = 32
MAX_DISTANCE = 128
N_DELTA_HEADS = 4
DK = 128
DV = 128
CONV_W = 4
CHUNK = 64
N_KEYS = 128
N_EXPERTS = N_KEYS * N_KEYS
PEER_HEADS = 8
PEER_KEY_DIM = 256
PEER_HALF = PEER_KEY_DIM // 2
PEER_TOPK = 16
PEER_BLOCK = 256
RMS_EPS = 1e-6
N_ADA = 6

ATTN_Q_W = N_Q_HEADS * HEAD_DIM
ATTN_KV_W = N_KV_HEADS * HEAD_DIM
DELTA_QK_W = N_DELTA_HEADS * DK
DELTA_V_W = N_DELTA_HEADS * DV
CONV_DIM = 2 * DELTA_QK_W + DELTA_V_W
IN_WIDTHS = (ATTN_Q_W, ATTN_KV_W, ATTN_KV_W, CONV_DIM, N_DELTA_HEADS, N_DELTA_HEADS, DELTA_V_W, D_MODEL, D_MODEL)
IN_W = sum(IN_WIDTHS)

kernel_name = 'hybrid_swa_gdn_peer_step'

def _split(x, widths):
    points, acc = [], 0
    for w in widths[:-1]:
        acc += w
        points.append(acc)
    return jnp.split(x, points, axis=-1)

def _rmsnorm(x, g):
    xf = x.astype(jnp.float32)
    y = xf * lax.rsqrt(jnp.mean(xf * xf, axis=-1, keepdims=True) + RMS_EPS)
    return (y * g.astype(jnp.float32)).astype(x.dtype)

def _l2norm(x):
    return x * lax.rsqrt(jnp.sum(x * x, axis=-1, keepdims=True) + RMS_EPS)

def _rel_bucket(dist):
    n = jnp.maximum(dist, 0)
    max_exact = N_BUCKETS // 2
    nf = jnp.maximum(n, 1).astype(jnp.float32)
    large = max_exact + (jnp.log(nf / max_exact) / math.log(MAX_DISTANCE / max_exact)
                         * (N_BUCKETS - max_exact)).astype(jnp.int32)
    return jnp.where(n < max_exact, n, jnp.minimum(large, N_BUCKETS - 1))

def _swa_attend(q, k, v, q_pos, k_pos, sinks, rel_bias):
    nb, nq = q_pos.shape
    nk = k_pos.shape[1]
    dist = q_pos[:, :, None] - k_pos[:, None, :]
    valid = (dist >= 0) & (dist < WINDOW) & (k_pos[:, None, :] >= 0)
    bias = rel_bias.astype(jnp.float32)[_rel_bucket(dist)]
    bias = bias.reshape(nb, nq, nk, N_KV_HEADS, Q_PER_KV).transpose(0, 3, 4, 1, 2)
    logits = jnp.einsum('bnqhgd,bnkhd->bnhgqk', q.astype(jnp.float32), k.astype(jnp.float32)) * (HEAD_DIM ** -0.5)
    logits = jnp.where(valid[None, :, None, None], logits + bias[None], -jnp.inf)
    sink = sinks.astype(jnp.float32).reshape(N_KV_HEADS, Q_PER_KV)[None, None, :, :, None, None]
    m = jnp.maximum(jnp.max(logits, axis=-1, keepdims=True), sink)
    p = jnp.exp(logits - m)
    denom = jnp.sum(p, axis=-1, keepdims=True) + jnp.exp(sink - m)
    o = jnp.einsum('bnhgqk,bnkhd->bnqhgd', p / denom, v.astype(jnp.float32))
    return o.astype(q.dtype)

def _swa_prompt(q, k, v, sinks, rel_bias):
    B, L = q.shape[:2]
    nb = L // Q_BLOCK
    qb = q.reshape(B, nb, Q_BLOCK, N_KV_HEADS, Q_PER_KV, HEAD_DIM)
    def band(t):
        tp = jnp.concatenate([jnp.zeros((B, Q_BLOCK, N_KV_HEADS, HEAD_DIM), t.dtype), t], axis=1)
        prev = tp[:, :L].reshape(B, nb, Q_BLOCK, N_KV_HEADS, HEAD_DIM)
        cur = t.reshape(B, nb, Q_BLOCK, N_KV_HEADS, HEAD_DIM)
        return jnp.concatenate([prev, cur], axis=2)
    blk = jnp.arange(nb, dtype=jnp.int32)[:, None]
    q_pos = blk * Q_BLOCK + jnp.arange(Q_BLOCK, dtype=jnp.int32)[None]
    k_pos = (blk - 1) * Q_BLOCK + jnp.arange(2 * Q_BLOCK, dtype=jnp.int32)[None]
    o = _swa_attend(qb, band(k), band(v), q_pos, k_pos, sinks, rel_bias)
    return o.reshape(B, L, N_KV_HEADS, Q_PER_KV, HEAD_DIM)

def _swa_sample(q, k, v, k_buf, v_buf, sinks, rel_bias):
    T = q.shape[1]
    W = k_buf.shape[1]
    kc = jnp.concatenate([k_buf.astype(k.dtype), k], axis=1)
    vc = jnp.concatenate([v_buf.astype(v.dtype), v], axis=1)
    q_pos = PAST_LEN + jnp.arange(T, dtype=jnp.int32)
    k_pos = PAST_LEN - W + jnp.arange(W + T, dtype=jnp.int32)
    o = _swa_attend(q[:, None], kc[:, None], vc[:, None], q_pos[None], k_pos[None], sinks, rel_bias)[:, 0]
    return o, kc[:, -W:], vc[:, -W:]

def _short_conv(u, buf, w):
    L = u.shape[1]
    full = jnp.concatenate([buf.astype(u.dtype), u], axis=1)
    out = full[:, 0:L] * w[0]
    for i in range(1, CONV_W):
        out = out + full[:, i:i + L] * w[i]
    return jax.nn.silu(out), full[:, L:]

def _gated_delta(q, k, v, g, beta, s0):
    B, L, H, _ = q.shape
    C = min(CHUNK, L)
    n = -(-L // C)
    pad = n * C - L
    q = _l2norm(q) * (DK ** -0.5)
    k = _l2norm(k)
    if pad:
        pw = ((0, 0), (0, pad), (0, 0), (0, 0))
        q, k, v = jnp.pad(q, pw), jnp.pad(k, pw), jnp.pad(v, pw)
        g, beta = jnp.pad(g, pw[:3]), jnp.pad(beta, pw[:3])
    def chunks(t):
        t = t.reshape((B, n, C, H) + t.shape[3:])
        return jnp.moveaxis(t, (1, 3), (0, 2))
    qc, kc, vc, bc = chunks(q), chunks(k), chunks(v), chunks(beta)
    gc = jnp.cumsum(chunks(g), axis=-1)
    causal = jnp.tril(jnp.ones((C, C), bool))
    strict = jnp.tril(jnp.ones((C, C), bool), -1)
    diff = gc[..., :, None] - gc[..., None, :]
    decay = jnp.where(causal, jnp.exp(jnp.where(causal, diff, 0.0)), 0.0)
    kb = kc * bc[..., None]
    vb = vc * bc[..., None]
    lmat = jnp.where(strict, jnp.einsum('nbhcd,nbhsd->nbhcs', kb, kc) * decay, 0.0)
    eye = jnp.eye(C, dtype=jnp.float32)
    tmat = lax.linalg.triangular_solve(lmat + eye, jnp.broadcast_to(eye, lmat.shape),
                                       left_side=True, lower=True, unit_diagonal=True)
    u = jnp.einsum('nbhcs,nbhsd->nbhcd', tmat, vb)
    w = jnp.einsum('nbhcs,nbhsd->nbhcd', tmat, kb * jnp.exp(gc)[..., None])
    a_intra = jnp.where(causal, jnp.einsum('nbhcd,nbhsd->nbhcs', qc, kc) * decay, 0.0)
    def step(S, inp):
        q_i, k_i, u_i, w_i, a_i, g_i = inp
        v_new = u_i - jnp.einsum('bhcd,bhde->bhce', w_i, S)
        o = jnp.einsum('bhcd,bhde->bhce', q_i * jnp.exp(g_i)[..., None], S) + jnp.einsum('bhcs,bhse->bhce', a_i, v_new)
        g_last = g_i[..., -1]
        S = S * jnp.exp(g_last)[..., None, None] + jnp.einsum(
            'bhcd,bhce->bhde', k_i * jnp.exp(g_last[..., None] - g_i)[..., None], v_new)
        return S, o
    S, o = lax.scan(step, s0, (qc, kc, u, w, a_intra, gc))
    o = jnp.moveaxis(o, (0, 2), (1, 3)).reshape(B, n * C, H, DV)[:, :L]
    return o, S

def _peer(h, w_query, sub_keys, expert_u, expert_v):
    B, L, D = h.shape
    T = B * L
    blk = min(PEER_BLOCK, T)
    nblk = -(-T // blk)
    xt = jnp.pad(h.reshape(T, D), ((0, nblk * blk - T), (0, 0))).reshape(nblk, blk, D)
    def one_block(xb):
        qry = (xb @ w_query).reshape(blk, PEER_HEADS, 2, PEER_HALF).astype(jnp.float32)
        s = jnp.einsum('thpd,pkd->thpk', qry, sub_keys.astype(jnp.float32))
        sv, si = lax.top_k(s, PEER_TOPK)
        cand = sv[:, :, 0, :, None] + sv[:, :, 1, None, :]
        cidx = si[:, :, 0, :, None] * N_KEYS + si[:, :, 1, None, :]
        best, pos = lax.top_k(cand.reshape(blk, PEER_HEADS, PEER_TOPK * PEER_TOPK), PEER_TOPK)
        eidx = jnp.take_along_axis(cidx.reshape(blk, PEER_HEADS, PEER_TOPK * PEER_TOPK), pos, axis=-1)
        gate = jax.nn.softmax(best, axis=-1)
        u = expert_u[eidx]
        v = expert_v[eidx]
        act = jax.nn.gelu(jnp.einsum('td,thed->the', xb, u), approximate=False)
        return jnp.einsum('the,thed->td', (gate * act.astype(jnp.float32)).astype(v.dtype), v)
    out = lax.map(one_block, xt)
    return out.reshape(nblk * blk, D)[:T].reshape(B, L, D).astype(h.dtype)

def _layer(x, c, k_buf, v_buf, conv_buf, s0, rel_bias, p):
    B, L, _ = x.shape
    ada = jax.nn.silu(c) @ p['w_ada'] + p['b_ada']
    sh1, sc1, gt1, sh2, sc2, gt2 = [a[:, None, :] for a in jnp.split(ada, N_ADA, axis=-1)]
    h = _rmsnorm(x, p['g_pre_mix']) * (1.0 + sc1) + sh1
    proj = h @ p['w_in']
    aq, ak, av, conv_in, a_dec, b_beta, z, g_a, g_b = _split(proj, IN_WIDTHS)
    q = aq.reshape(B, L, N_KV_HEADS, Q_PER_KV, HEAD_DIM)
    k = ak.reshape(B, L, N_KV_HEADS, HEAD_DIM)
    v = av.reshape(B, L, N_KV_HEADS, HEAD_DIM)
    if k_buf is None:
        o_att = _swa_prompt(q, k, v, p['attn_sinks'], rel_bias)
        new_k, new_v = k[:, -WINDOW:], v[:, -WINDOW:]
        conv_buf = jnp.zeros((B, CONV_W - 1, CONV_DIM), conv_in.dtype)
        s0 = jnp.zeros((B, N_DELTA_HEADS, DK, DV), jnp.float32)
    else:
        o_att, new_k, new_v = _swa_sample(q, k, v, k_buf, v_buf, p['attn_sinks'], rel_bias)
    o_att = o_att.reshape(B, L, ATTN_Q_W)
    conv_out, new_conv = _short_conv(conv_in, conv_buf, p['w_conv'])
    dq, dk_, dv_ = _split(conv_out.astype(jnp.float32), (DELTA_QK_W, DELTA_QK_W, DELTA_V_W))
    g_log = -jnp.exp(p['a_log'].astype(jnp.float32)) * jax.nn.softplus(
        a_dec.astype(jnp.float32) + p['dt_bias'].astype(jnp.float32))
    beta = jax.nn.sigmoid(b_beta.astype(jnp.float32))
    o_d, s_new = _gated_delta(dq.reshape(B, L, N_DELTA_HEADS, DK), dk_.reshape(B, L, N_DELTA_HEADS, DK),
                              dv_.reshape(B, L, N_DELTA_HEADS, DV), g_log, beta, s0.astype(jnp.float32))
    o_d = _rmsnorm(o_d, p['delta_norm']) * jax.nn.silu(z.reshape(B, L, N_DELTA_HEADS, DV).astype(jnp.float32))
    o_d = o_d.reshape(B, L, DELTA_V_W).astype(x.dtype)
    merged = jax.nn.sigmoid(g_a) * (o_att @ p['w_att_out']) + jax.nn.sigmoid(g_b) * (o_d @ p['w_delta_out'])
    mix = merged @ p['w_out']
    x = x + gt1 * _rmsnorm(mix, p['g_post_mix'])
    h2 = _rmsnorm(x, p['g_pre_ffn']) * (1.0 + sc2) + sh2
    f = _peer(h2, p['w_query'], p['sub_keys'], p['expert_u'], p['expert_v'])
    x = x + gt2 * _rmsnorm(f, p['g_post_ffn'])
    return x, new_k, new_v, new_conv, s_new.astype(x.dtype)

def setup_inputs(seed: int = 0) -> dict:
    key = jax.random.key(seed)
    keys = iter(jax.random.split(key, 40))
    def nrm(shape, scale):
        return jax.random.normal(next(keys), shape, jnp.float32) * scale
    def gain(shape):
        return 1.0 + nrm(shape, 0.01)
    w_buf = min(WINDOW, PAST_LEN)
    x_prompt = nrm((BATCH, SEQ, D_MODEL), 1.0)
    x_sample = nrm((DEC_BATCH, DEC_SEQ, D_MODEL), 1.0)
    cache_swa_k = nrm((DEPTH, DEC_BATCH, w_buf, N_KV_HEADS, HEAD_DIM), 1.0)
    cache_swa_v = nrm((DEPTH, DEC_BATCH, w_buf, N_KV_HEADS, HEAD_DIM), 1.0)
    state_conv = nrm((DEPTH, DEC_BATCH, CONV_W - 1, CONV_DIM), 1.0)
    state_delta = nrm((DEPTH, DEC_BATCH, N_DELTA_HEADS, DK, DV), DK ** -0.5)
    c_prompt = nrm((BATCH, D_MODEL), 1.0)
    c_sample = nrm((DEC_BATCH, D_MODEL), 1.0)
    rel_bias = nrm((N_BUCKETS, N_Q_HEADS), 0.5)
    w_ada = nrm((DEPTH, D_MODEL, N_ADA * D_MODEL), 0.5 * D_MODEL ** -0.5)
    b_ada = nrm((DEPTH, N_ADA * D_MODEL), 0.01)
    g_pre_mix = gain((DEPTH, D_MODEL))
    g_post_mix = gain((DEPTH, D_MODEL))
    g_pre_ffn = gain((DEPTH, D_MODEL))
    g_post_ffn = gain((DEPTH, D_MODEL))
    w_in = nrm((DEPTH, D_MODEL, IN_W), D_MODEL ** -0.5)
    attn_sinks = nrm((DEPTH, N_Q_HEADS), 0.5)
    w_conv = nrm((DEPTH, CONV_W, CONV_DIM), CONV_W ** -0.5)
    a_log = jnp.log(jax.random.uniform(next(keys), (DEPTH, N_DELTA_HEADS), jnp.float32, 1.0, 16.0))
    dt_bias = nrm((DEPTH, N_DELTA_HEADS), 0.1)
    delta_norm = gain((DEPTH, DV))
    w_att_out = nrm((DEPTH, ATTN_Q_W, D_MODEL), ATTN_Q_W ** -0.5)
    w_delta_out = nrm((DEPTH, DELTA_V_W, D_MODEL), DELTA_V_W ** -0.5)
    w_out = nrm((DEPTH, D_MODEL, D_MODEL), D_MODEL ** -0.5)
    w_query = nrm((DEPTH, D_MODEL, PEER_HEADS * PEER_KEY_DIM), D_MODEL ** -0.5)
    sub_keys = nrm((DEPTH, 2, N_KEYS, PEER_HALF), PEER_HALF ** -0.5)
    expert_u = nrm((DEPTH, N_EXPERTS, D_MODEL), D_MODEL ** -0.5)
    expert_v = nrm((DEPTH, N_EXPERTS, D_MODEL), D_MODEL ** -0.5)
    return {'x_prompt': x_prompt, 'x_sample': x_sample, 'cache_swa_k': cache_swa_k, 'cache_swa_v': cache_swa_v,
            'state_conv': state_conv, 'state_delta': state_delta, 'c_prompt': c_prompt, 'c_sample': c_sample,
            'rel_bias': rel_bias, 'w_ada': w_ada, 'b_ada': b_ada, 'g_pre_mix': g_pre_mix, 'g_post_mix': g_post_mix,
            'g_pre_ffn': g_pre_ffn, 'g_post_ffn': g_post_ffn, 'w_in': w_in, 'attn_sinks': attn_sinks,
            'w_conv': w_conv, 'a_log': a_log, 'dt_bias': dt_bias, 'delta_norm': delta_norm,
            'w_att_out': w_att_out, 'w_delta_out': w_delta_out, 'w_out': w_out, 'w_query': w_query,
            'sub_keys': sub_keys, 'expert_u': expert_u, 'expert_v': expert_v}

def reference(x_prompt, x_sample, cache_swa_k, cache_swa_v, state_conv, state_delta, c_prompt, c_sample,
              rel_bias, w_ada, b_ada, g_pre_mix, g_post_mix, g_pre_ffn, g_post_ffn, w_in, attn_sinks,
              w_conv, a_log, dt_bias, delta_norm, w_att_out, w_delta_out, w_out, w_query, sub_keys,
              expert_u, expert_v):
    yp, ys = x_prompt, x_sample
    kp_l, vp_l, cp_l, sp_l, ks_l, vs_l, cs_l, ss_l = [], [], [], [], [], [], [], []
    for layer in range(DEPTH):
        p = dict(w_ada=w_ada[layer], b_ada=b_ada[layer], g_pre_mix=g_pre_mix[layer], g_post_mix=g_post_mix[layer],
                 g_pre_ffn=g_pre_ffn[layer], g_post_ffn=g_post_ffn[layer], w_in=w_in[layer],
                 attn_sinks=attn_sinks[layer], w_conv=w_conv[layer], a_log=a_log[layer], dt_bias=dt_bias[layer],
                 delta_norm=delta_norm[layer], w_att_out=w_att_out[layer], w_delta_out=w_delta_out[layer],
                 w_out=w_out[layer], w_query=w_query[layer], sub_keys=sub_keys[layer],
                 expert_u=expert_u[layer], expert_v=expert_v[layer])
        yp, kp, vp, cp, sp = _layer(yp, c_prompt, None, None, None, None, rel_bias, p)
        ys, ks, vs, cs, ss = _layer(ys, c_sample, cache_swa_k[layer], cache_swa_v[layer], state_conv[layer],
                                    state_delta[layer], rel_bias, p)
        kp_l.append(kp); vp_l.append(vp); cp_l.append(cp); sp_l.append(sp)
        ks_l.append(ks); vs_l.append(vs); cs_l.append(cs); ss_l.append(ss)
    new_k_prompt = jnp.stack(kp_l)
    new_v_prompt = jnp.stack(vp_l)
    new_conv_prompt = jnp.stack(cp_l)
    new_delta_prompt = jnp.stack(sp_l)
    new_k_sample = jnp.stack(ks_l)
    new_v_sample = jnp.stack(vs_l)
    new_conv_sample = jnp.stack(cs_l)
    new_delta_sample = jnp.stack(ss_l)
    return (yp, ys, new_k_prompt, new_v_prompt, new_conv_prompt, new_delta_prompt,
            new_k_sample, new_v_sample, new_conv_sample, new_delta_sample)


_drawn_inputs = setup_inputs


def setup_inputs(seed=0):
    import zlib

    import numpy as np

    out = dict(_drawn_inputs(seed))
    spreads = {}
    factors = {'g_pre_mix': 2.936,
     'g_post_mix': 3.274,
     'g_post_ffn': 8.0,
     'attn_sinks': 5.99,
     'delta_norm': 2.963}
    for name, (base, spread) in spreads.items():
        noise = np.random.default_rng([zlib.crc32(name.encode()), seed]).standard_normal(out[name].shape)
        drawn = base * np.exp(spread * noise) if base else spread * noise
        out[name] = __import__('jax').numpy.asarray(drawn.astype(out[name].dtype))
    for name, factor in factors.items():
        out[name] = (out[name] * factor).astype(out[name].dtype)
    return out
```

```python
from contextlib import ExitStack
from collections import namedtuple

import numpy as np
import concourse.bass as bass
from concourse import mybir

ALU = mybir.AluOpType
ACT = mybir.ActivationFunctionType
AX = mybir.AxisListType
F32 = mybir.dt.float32
U32 = mybir.dt.uint32

P = 128
D = 1024
KT = D // P
SEQ = 512
NT = SEQ // P
NB = 8
TOK = SEQ + NB
HALF = TOK // 2
HQ, HD = 8, 64
HG = 4
DH = 4
CT_N = 12
WIN = 128
NAT_W = 264
PH = 8
TOPK = 16
NKEY = 128
SLOTS = 8
EPS = 1e-6
NEG = -1e30
B_ADA1, B_CONV, B_Q, B_Z, B_GA, B_GB, B_ADA2, B_BR, B_QRY = 16, 12, 4, 4, 8, 8, 32, 8, 16
C_ID, C_LE, C_GT, C_ONE, C_LVL, C_IOTA, C_TK, C_KT = 0, 128, 256, 384, 512, 1408, 1424, 1432
C_W = 1560
K_BADA, K_GPM, K_GQM, K_GPF, K_GQF, K_CONV, K_DN, K_SINK, K_ALOG, K_DT, K_SINKS = 0, 48, 56, 64, 72, 80, 128, 129, 137, 141, 145
K_W = 146


class Steps:

    def __init__(self, eng, own):
        self.eng, self.own, self.n = eng, own, {}

    def __call__(self, ins, sem=None):
        sem = self.own if sem is None else sem
        ins.then_inc(sem, 1)
        self.n[sem.name] = self.n.get(sem.name, 0) + 1
        self.eng.wait_ge(sem, self.n[sem.name])


class Ring:

    def __init__(self, eng, banks, full, free):
        self.eng, self.banks, self.full, self.free, self.n = eng, banks, full, free, 0

    def to_fill(self):
        if self.n >= len(self.banks):
            self.eng.wait_ge(self.free, self.n - len(self.banks) + 1)
        self.n += 1
        return self.banks[(self.n - 1) % len(self.banks)]

    def to_read(self):
        self.eng.wait_ge(self.full, self.n + 1)
        self.n += 1
        return self.banks[(self.n - 1) % len(self.banks)]


def build(nc, I, O):
    with ExitStack() as ctx:
        def sb(name, shape, dt=F32):
            return ctx.enter_context(nc.sbuf_tensor(name, shape, dt))

        def sem(name):
            return ctx.enter_context(nc.semaphore(name))

        consts = sb("consts", [P, C_W])
        cols = sb("cols", [P, K_W])
        onehot = sb("onehot", [33, 384])
        relx = sb("relx", [33, HQ])
        rels = sb("rels", [33, NB * HQ])
        skt = sb("skt", [P, 2, NKEY])
        cT = sb("cT", [P, KT, 1 + NB])
        adaT = sb("adaT", [P, 6 * KT, 1 + NB])
        small = sb("small", [P, 360])
        zeros = sb("zeros", [P, P])
        bext = sb("bext", [HQ, 384])
        delta = sb("delta", [P, 512])
        cpo = sb("cpo", [P, CT_N, 3])
        arena = sb("arena", [P, 48480])
        ident, le, gt, ones = (consts[:, c:c + P] for c in (C_ID, C_LE, C_GT, C_ONE))

        def at(lo, *shape):
            n = int(np.prod(shape))
            v = arena[:, lo:lo + n]
            if len(shape) == 2:
                v = v.rearrange("p (a b) -> p a b", b=shape[1])
            if len(shape) == 3:
                v = v.rearrange("p (a b c) -> p a b c", b=shape[1], c=shape[2])
            return v

        def wide(v, shape):
            return v.to_broadcast(shape)

        X0, HT0, WB0, CT0, KV0, QT0, Z0, GA0, GB0, R0, E0 = (
            0, 5120, 9280, 13376, 19616, 23712, 25792, 27872, 32032, 36192, 44384)

        def at(lo, *shape):
            v = arena[:, lo:lo + int(np.prod(shape))]
            if len(shape) == 2:
                v = v.rearrange("p (a b) -> p a b", b=shape[1])
            if len(shape) == 3:
                v = v.rearrange("p (a b c) -> p a b c", b=shape[1], c=shape[2])
            return v

        x_t = at(X0, NT + 1, D)
        hT = at(HT0, KT, TOK)
        wb = at(WB0, 4, D)
        ct = at(CT0, CT_N, TOK)
        qT = at(QT0, 4, TOK)
        zT = at(Z0, DH, TOK)
        gaT, gbT = at(GA0, KT, TOK), at(GB0, KT, TOK)
        junk = at(GA0, D)
        rnb = at(R0, 2, TOK)
        bias = at(R0, HQ, 256)
        wnat = at(R0 + 2048, KT, NAT_W)
        prob = at(R0 + 2048, HQ, 256)
        sqb = at(R0 + 4160, 2, TOK)
        probT = at(R0 + 4096, 2 * HQ, P)
        ubuf = at(R0 + 6144, 2, 547)
        keyc, valc = at(R0 + 6144, NB, P), at(R0 + 7168, NB, P)
        cst, cso = (at(E0 + 1832 + i, CT_N * NB, 3).rearrange("p (m b) i -> p m b i", b=NB) for i in (0, 288))
        nat = at(E0, NT + 1, NAT_W)
        kT = at(E0 + 1320, SEQ)
        attT, odT = at(HT0, 4, TOK), at(HT0 + 2080, DH, TOK)
        kdec, vb = at(KV0, NT, 512), at(KV0 + 2048, NT, 512)
        sdel = at(X0, DH, NB, P)
        mgt = at(X0 + 4096, 2, 512)
        Lc, Wc, Tc = (at(R0 + 2048 * i, NT, 512) for i in range(3))
        Lm, A2 = at(R0 + 6144, NT, 512), at(E0 + 1832, NT, 512)
        ATc = at(CT0 + 8 * TOK, NT, 512)
        E1, E2 = at(QT0, 2, 512), at(QT0 + 1024, 2, 512)
        vdiag = at(R0, NB, P)
        wout = at(CT0, KT, D)
        v_g1, v_a2, v_s2 = (at(R0 + D * i, D) for i in (0, 1, 2))
        s_g1, s_a2, s_s2 = (at(R0 + D * i, D) for i in (3, 4, 5))
        v_g2, s_g2 = at(R0 + 6144, D), at(R0 + 7168, D)
        t1, t2 = at(E0, D), at(E0 + D, D)
        h2 = at(HT0, NT, D)
        h2s, h2sb = at(E0 + 2 * D, D), at(E0 + 3 * D, D)
        h2T = gbT
        qryT = at(CT0, 2 * PH, TOK)
        uring, vring = at(QT0, SLOTS, D), at(QT0 + SLOTS * D, SLOTS, D)
        sc = at(WB0, 2, 2 * PH * NKEY)
        cand = at(QT0 + 2 * SLOTS * D, 2048)
        B0 = QT0 + 2 * SLOTS * D
        s_in, s_out = at(B0, 2, NKEY), at(B0 + 1680, 2, NKEY)
        sv, si = at(B0 + 384, 2, TOPK), at(B0 + 416, 2, TOPK).bitcast(U32)
        cand, cand2 = at(B0 + 448, TOPK * TOPK), at(B0 + 704, TOPK * TOPK)
        hit = at(B0 + 960, 2, TOPK, TOPK)
        sif, pf, ee = at(B0 + 1472, 2, TOPK), at(B0 + 1504, 2, TOPK), at(B0 + 1536, 2, TOPK)
        pint = at(B0 + 1568, 2, TOPK).bitcast(U32)
        best, pos, gexp = at(B0 + 1600, TOPK), at(B0 + 1616, TOPK).bitcast(U32), at(B0 + 1632, TOPK)
        ef = at(B0 + 1648, TOPK)
        nbest, gsum = at(B0 + 1664, 1), at(B0 + 1665, 1)
        diag = at(CT0 + 2 * PH * TOK, SLOTS, P)
        B2 = E0 + 2 * D
        gate, eidx = at(B2, 2, PH * TOPK), at(B2 + 256, 2, PH * TOPK).bitcast(U32)
        sgate, sidx = at(B2 + 512, SLOTS), at(B2 + 520, SLOTS).bitcast(U32)

        def sm(lo, n):
            return small[:, lo:lo + n]
        ssx, rstd, eps, eps128 = sm(0, 8), sm(8, 8), sm(16, 1), sm(17, 1)
        mx8, nm8, sm8, es8 = sm(18, 8), sm(26, 8), sm(34, 8), sm(42, 8)
        gg = sm(50, 20).rearrange("p (t h) -> p t h", h=DH)
        beta = sm(70, 20).rearrange("p (t h) -> p t h", h=DH)
        gtmp, gtmp2 = (sm(a, 20).rearrange("p (t h) -> p t h", h=DH) for a in (90, 110))
        ealog = sm(130, 4)
        ex = sm(134, 48)
        nbeg = sm(182, 16)
        rms4, rms4r = sm(198, 4), sm(202, 4)
        lt64 = sm(206, 64)
        act8 = sm(270, 16).rearrange("p (a j) -> p a j", j=SLOTS)
        w8 = sm(286, 16).rearrange("p (a j) -> p a j", j=SLOTS)
        cur = sm(302, 16).bitcast(U32).rearrange("p (a j) -> p a j", j=SLOTS)
        svv = sm(318, 32)
        gcur = sm(350, 8)
        kn8, vn8 = at(R0 + 2048, 512)[0:NB], at(R0 + 2560, 512)[0:NB]
        sdv = [at(E0 + 1832 + 32 * i, 32) for i in range(13)]

        dbank = [ctx.enter_context(nc.psum_tensor(f"dbank{i}", [P, 512], F32)) for i in range(4)]
        abank = [ctx.enter_context(nc.psum_tensor(f"abank{i}", [P, 512], F32)) for i in range(2)]
        fsum = [ctx.enter_context(nc.psum_tensor(f"fsum{i}", [P, 512], F32)) for i in range(2)]

        names = """dring_full dring_free aring_full aring_free w_used consts_in cols_in cT_in x_in wnat_in bias_in
            cst_in keyc_in valc_in sdel_in wout_in xr_in skt_in silu_c ss_ready rms_ready rstd_ready xn_ready hT_ready
            conv_in conv_out silu_out sq_ready rn_ready l2_done nat_ready rels_ready qT_ready kT_ready ext_ready ext_out
            zg_ready gx_ready beta_ready g_ready nm_ready exp_done prob_ready probT_ready att_done lt_ready kTs_ready
            ex_ready vb_ready mg_ready E_ready L_ready lm_ready a2_ready wt_ready S_ready r_ready vn_ready qs_ready
            o_ready orms_ready on_ready od_done sg_ready sa_ready sp_ready sn_ready vd_ready sd_ready merged_ready dg_ready
            ms_ready mr_ready h2_ready h2T_ready qry_ready h2sb_ready sc_ready best_ready gexp_ready topk_done
            sel_out sel_in gelu_ready w_ready diag_ready gc_ready f_read y_ready
            out_small out_k out_delta out_y dve_turn pool_turn dve_step act_step pool_step""".split()
        s = namedtuple("Semaphores", names)(*(sem(n) for n in names))
        w_full = [sem(f"w_full{i}") for i in range(4)]
        u_in = [sem(f"u_in{i}") for i in range(SLOTS)]
        v_in = [sem(f"v_in{i}") for i in range(SLOTS)]
        u_used = [sem(f"u_used{i}") for i in range(SLOTS)]
        v_used = [sem(f"v_used{i}") for i in range(SLOTS)]

        ROWS = [P] * NT + [NB]
        COL = [t * P for t in range(NT)] + [SEQ]

        def tcols(t):
            return slice(COL[t], COL[t] + ROWS[t])

        N_STREAM = B_ADA1 + B_CONV + B_Q + B_Z + B_GA + B_GB + B_ADA2 + B_BR + B_QRY
        block = ctx.enter_context(nc.Block())

        @block.sync
        def _(sp):
            for n in range(N_STREAM):
                if n >= 4:
                    sp.wait_ge(s.w_used, n - 3)
                if n == N_STREAM - B_QRY:
                    sp.wait_ge(s.sd_ready, 1)
                    sp.dma_start(wout, I["wout"]).then_inc(s.wout_in, 16)
                sp.dma_start(wb[:, n % 4, :], I["wstream"][n]).then_inc(w_full[n % 4], 16)
            sp.wait_ge(s.y_ready, 1)
            sp.dma_start(O["ys"], x_t[0:NB, NT, :]).then_inc(s.out_y, 16)
            for t in range(NT):
                sp.wait_ge(s.y_ready, t + 2)
                sp.dma_start(O["yp"][t * P:(t + 1) * P, :], x_t[:, t, :]).then_inc(s.out_y, 16)
            sp.wait_ge(s.out_y, 16 * (NT + 1))

        @block.gpsimd
        def _(pool):
            step = Steps(pool, s.pool_step)
            pool.dma_start(cT[:, :, :], I["cT"]).then_inc(s.cT_in, 16)
            pool.dma_start(x_t[:, 0:NT, :], I["x"].rearrange("(t p) d -> p t d", p=P)).then_inc(s.x_in, 16)
            pool.dma_start(x_t[0:NB, NT, :], I["xs"]).then_inc(s.x_in, 16)
            pool.dma_start(consts[:, :], I["consts"]).then_inc(s.consts_in, 16)
            pool.dma_start(onehot[:, :], I["onehot"]).then_inc(s.consts_in, 16)
            pool.dma_start(cols[:, :], I["cols"]).then_inc(s.cols_in, 16)
            pool.dma_start(relx[0:32, :], I["rel"]).then_inc(s.cols_in, 16)
            pool.dma_start(wnat, I["wnat"]).then_inc(s.wnat_in, 16)
            pool.dma_start(cst, I["cst"]).then_inc(s.cst_in, 16)
            pool.dma_start(skt[:, :, :], I["skt"]).then_inc(s.skt_in, 16)
            pool.wait_ge(s.conv_out, CT_N)
            pool.dma_start(O["convp"], cpo[:, :, :]).then_inc(s.out_small, 16)
            pool.dma_start(O["convs"], cso).then_inc(s.out_small, 16)
            pool.wait_ge(s.nat_ready, NT + 1)
            for c0, cache, win, last in ((0, "kc", "ks", "kp"), (P, "vc", "vs", "vp")):
                pool.dma_start(O[win][:, 0:WIN - 1, :], I[cache][:, 1:WIN, :]).then_inc(s.out_k, 16)
                pool.dma_start(O[win][:, WIN - 1, :], nat[0:NB, NT, c0:c0 + P]).then_inc(s.out_k, 16)
                pool.dma_start(O[last], nat[:, NT - 1, c0:c0 + P]).then_inc(s.out_small, 16)
            pool.wait_ge(s.out_k, 64)
            pool.dma_start(keyc, O["ks"].rearrange("b w c -> w b c")).then_inc(s.keyc_in, 16)
            pool.dma_start(valc, O["vs"].rearrange("b w c -> w b c")).then_inc(s.valc_in, 16)
            pool.wait_ge(s.ext_ready, 1)
            pool.dma_start(I["skew"], bext[:, :].unsqueeze(1).to_broadcast([HQ, P, 384])).then_inc(s.ext_out, 16)
            pool.wait_ge(s.ext_out, 16)
            pool.wait_ge(s.l2_done, 2 * DH)
            pool.dma_start(bias, bass.AP(tensor=I["skew"].tensor, offset=P - 1,
                                         ap=[[383, P], [P * 384, HQ], [1, 256]])).then_inc(s.bias_in, 16)
            pool.wait_ge(s.hT_ready, KT + 1)
            pool.dma_start(sdel, I["sdel"]).then_inc(s.sdel_in, 16)
            pool.wait_ge(s.S_ready, NT + 1)
            pool.dma_start(O["deltap"], delta[:, :]).then_inc(s.out_delta, 16)
            pool.wait_ge(s.sd_ready, 1)
            pool.dma_start(O["deltas"], sdel).then_inc(s.out_delta, 16)
            pool.wait_ge(s.out_delta, 32)
            pool.dma_start(x_t[:, 0:NT, :], I["x"].rearrange("(t p) d -> p t d", p=P)).then_inc(s.xr_in, 16)
            pool.dma_start(x_t[0:NB, NT, :], I["xs"]).then_inc(s.xr_in, 16)
            pool.wait_ge(s.out_small, 64)

            def fetch(r, a, idx):
                if r is not None:
                    for j in range(SLOTS):
                        pool.wait_ge(u_used[j], r)
                pool.tensor_copy(cur[:, a, :], idx).then_inc(s.pool_step, 1)
                pool.wait_ge(s.pool_step, 1 if r is None else r + 1)
                pool.sem_inc(s.pool_turn, 1)
                for j in range(SLOTS):
                    pool.indirect_dma_start(uring[:, j, :], None, I["eu"],
                                            bass.IndirectOffsetOnAxis(cur[:, a, j:j + 1], 0)).then_inc(u_in[j], 16)
                for j in range(SLOTS):
                    if r is not None:
                        pool.wait_ge(v_used[j], r)
                        pool.sem_inc(s.pool_turn, 1)
                    pool.indirect_dma_start(vring[:, j, :], None, I["ev"],
                                            bass.IndirectOffsetOnAxis(cur[:, a, j:j + 1], 0)).then_inc(v_in[j], 16)

            pool.wait_ge(s.topk_done, PH)
            for src, tmp in ((eidx, "sidx"), (gate, "sgate")):
                pool.dma_start(I[tmp], src[0:NB, 0, :]).then_inc(s.sel_out, 16)
            pool.wait_ge(s.sel_out, 32)
            for dst, tmp in ((sidx, "sidx"), (sgate, "sgate")):
                for b in range(NB):
                    pool.dma_start(dst[b * TOPK:(b + 1) * TOPK, :],
                                   I[tmp][b, :].rearrange("(h k) -> k h", k=TOPK), allow_slow_non_contiguous=True).then_inc(s.sel_in, 16)
            pool.wait_ge(s.sel_in, 2 * 16 * NB)
            pool.wait_ge(s.qry_ready, 1)
            pool.wait_ge(s.h2_ready, NT + 1)
            fetch(None, 0, sidx)
            for t in range(NT):
                n = t + 1
                pool.wait_ge(s.topk_done, PH * (n + 1))
                with pool.Fori(0, PH) as h:
                    for a in range(2):
                        fetch(h * 2 + (1 + 2 * PH * t + a), (1 + a) % 2, eidx[:, n % 2, bass.ds(h * TOPK + a * SLOTS, SLOTS)])

        @block.scalar
        def _(act):
            step = Steps(act, s.act_step)
            ring = Ring(act, abank, s.aring_full, s.aring_free)
            A = act.activation

            def empty(dst, cols_from=slice(0, 512), rows=slice(0, P), func=ACT.Copy, **kw):
                b = ring.to_read()
                src = b[rows, cols_from]
                if len(dst.shape) == 3:
                    src = src.rearrange("p (a q) -> p a q", q=dst.shape[2])
                step(A(dst, src, func, **kw), s.aring_free)

            act.wait_ge(s.cT_in, 16)
            step(A(cT[:, :, :], cT[:, :, :], ACT.Silu), s.silu_c)
            for t in range(NT + 1):
                act.wait_ge(s.ss_ready, t + 1)
                step(A(rstd[0:ROWS[t], t:t + 1], ssx[0:ROWS[t], t:t + 1], ACT.Sqrt, bias=eps[0:ROWS[t], :], scale=1.0 / D), s.rms_ready)
            for t in range(NT + 1):
                act.wait_ge(s.rstd_ready, t + 1)
                step(A(x_t[0:ROWS[t], t, :], x_t[0:ROWS[t], t, :], ACT.Copy, scale=rstd[0:ROWS[t], t:t + 1]), s.xn_ready)
            rest = SEQ - HALF
            for m in range(CT_N + 1):
                if m < CT_N:
                    u = ubuf[:, m % 2, :]
                    if m >= 2:
                        act.wait_ge(s.conv_out, m - 1)
                    if m == 0:
                        act.wait_ge(s.dve_step, 1)
                    empty(u[:, 3:3 + HALF], slice(0, HALF))
                    b = ring.to_read()
                    step(A(u[:, 3 + HALF:3 + SEQ], b[:, 0:rest], ACT.Copy))
                    step(A(u[:, 515:547].rearrange("p (b i) -> p b i", i=4)[:, :, 3], b[:, rest:HALF], ACT.Copy), s.aring_free)
                    act.sem_inc(s.conv_in, 1)
                if m >= 1:
                    act.wait_ge(s.conv_out, m)
                    step(A(ct[:, m - 1, :], ct[:, m - 1, :], ACT.Silu), s.silu_out)
            for t in range(NT + 1):
                empty(nat[0:ROWS[t], t, :], slice(0, NAT_W), slice(0, ROWS[t]))
                act.sem_inc(s.nat_ready, 1)
            for m in range(B_Q):
                for c in range(2):
                    empty(qT[:, m, c * HALF:(c + 1) * HALF], slice(0, HALF))
            act.sem_inc(s.qT_ready, 1)
            empty(kT)
            act.sem_inc(s.kT_ready, 1)
            empty(bext[:, :], slice(0, 384), slice(0, HQ))
            act.sem_inc(s.ext_ready, 1)
            for m in range(2 * DH):
                if m >= 2:
                    act.wait_ge(s.l2_done, m - 1)
                for c in range(2):
                    empty(rnb[:, m % 2, c * HALF:(c + 1) * HALF], slice(0, HALF), func=ACT.Sqrt,
                          bias=eps128 if m < DH else eps, scale=float(P) if m < DH else 1.0)
                act.sem_inc(s.rn_ready, 1)
            for m in range(B_Z + B_GA + B_GB):
                dst = zT[:, m, :] if m < B_Z else (gaT[:, m - B_Z, :] if m < B_Z + B_GA else gbT[:, m - B_Z - B_GA, :])
                for c in range(2):
                    empty(dst[:, c * HALF:(c + 1) * HALF], slice(0, HALF), func=ACT.Silu if m < B_Z else ACT.Sigmoid)
            act.sem_inc(s.zg_ready, 1)
            act.wait_ge(s.cols_in, 32)
            step(A(ealog, cols[:, K_ALOG:K_ALOG + 4], ACT.Exp))
            act.wait_ge(s.gx_ready, 1)
            step(A(gtmp2, gtmp, ACT.Abs))
            step(A(gtmp2, gtmp2, ACT.Exp, scale=-1.0))
            step(A(gtmp2, gtmp2, ACT.Ln, bias=ones[:, 0:1]))
            step(A(beta, nat[:, :, 260:264], ACT.Sigmoid), s.beta_ready)
            for blk in range(NT):
                lo = 0 if blk else P
                act.wait_ge(s.nm_ready, blk + 1)
                for h in range(HQ):
                    step(A(prob[:, h, lo:256], prob[:, h, lo:256], ACT.Exp, bias=nm8[:, h:h + 1], accum_out=sm8[:, h:h + 1]))
                step(A(es8, es8, ACT.Exp), s.exp_done)
                for i in range(2 if blk == 0 else 4):
                    empty(probT[:, 4 * i:4 * i + 4, :])
                act.sem_inc(s.probT_ready, 1)
                empty(attT[:, :, blk * P:(blk + 1) * P])
            for i in range(2):
                empty(probT[:, 4 * i:4 * i + 4, :])
            act.sem_inc(s.kTs_ready, 1)
            act.wait_ge(s.nm_ready, NT + 1)
            step(A(prob[0:64, 0, 0:P], prob[0:64, 0, 0:P], ACT.Exp, bias=nm8[0:64, 0:1], accum_out=sm8[0:64, 0:1]))
            step(A(es8[0:64, 0:1], es8[0:64, 0:1], ACT.Exp), s.exp_done)
            b = ring.to_read()
            step(A(attT[:, :, SEQ:TOK], b[:, 0:32].rearrange("p (b g) -> p g b", g=HG), ACT.Copy), s.aring_free)
            act.sem_inc(s.att_done, 1)
            empty(ex, slice(0, 48), func=ACT.Exp)
            act.sem_inc(s.ex_ready, 1)
            for ch in range(NT):
                if ch >= 2:
                    act.wait_ge(s.L_ready, ch - 1)
                empty(E1[:, ch % 2, :], func=ACT.Exp)
                empty(E2[:, ch % 2, :], func=ACT.Exp)
                act.sem_inc(s.E_ready, 1)
            act.wait_ge(s.out_small, 64)
            for lv in range(7):
                for ch in range(NT):
                    empty(A2[:, ch, :])
                    act.sem_inc(s.a2_ready, 1)
            for ch in range(NT):
                empty(E1[:, 1, :])
                act.sem_inc(s.qs_ready, 1)
                empty(E2[:, 0, :])
                act.sem_inc(s.vn_ready, 1)
                act.wait_ge(s.o_ready, ch + 1)
                step(A(rms4, rms4, ACT.Sqrt, bias=eps, scale=1.0 / P), s.orms_ready)
            b = ring.to_read()
            step(A(sdv[0], b[:, 0:32], ACT.Exp))
            step(A(sdv[1], b[:, 32:64], ACT.Copy), s.aring_free)
            act.sem_inc(s.sa_ready, 1)
            empty(sdv[2], slice(0, 32), func=ACT.Sqrt, bias=eps, scale=1.0 / P)
            act.sem_inc(s.sa_ready, 1)
            for i in range(NT + 2):
                if i <= NT:
                    for _ in range(2):
                        act.wait_ge(s.ms_ready, 2 * i + _ + 1)
                        step(A(rstd[0:ROWS[i], 0:1], ssx[0:ROWS[i], 0:1], ACT.Sqrt, bias=eps[0:ROWS[i], :], scale=1.0 / D), s.mr_ready)
                if 1 <= i <= NT:
                    for g in range(2):
                        empty(h2T[:, 4 * g:4 * g + 4, (i - 1) * P:i * P])
            empty(h2T[:, :, SEQ:TOK], slice(0, KT * NB))
            act.sem_inc(s.h2T_ready, 1)
            for m in range(B_QRY):
                for c in range(2):
                    empty(qryT[:, m, c * HALF:(c + 1) * HALF], slice(0, HALF))
            act.sem_inc(s.qry_ready, 1)

            def scores(n):
                rows = ROWS[(n - 1) % (NT + 1)]
                if n >= 2:
                    act.wait_ge(s.topk_done, PH * (n - 1))
                for g in range(4):
                    empty(sc[0:rows, n % 2, g * 512:(g + 1) * 512], rows=slice(0, rows))
                act.sem_inc(s.sc_ready, 1)

            def best_exp(rows, k):
                act.wait_ge(s.best_ready, k)
                A(gexp[0:rows, :], best[0:rows, :], ACT.Exp, bias=nbest[0:rows, :],
                  accum_out=gsum[0:rows, :]).then_inc(s.gexp_ready, 1)

            def weigh(r, a, base):
                act.wait_ge(u_used[SLOTS - 1], r + 1)
                A(act8[:, a, :], act8[:, a, :], ACT.Gelu).then_inc(s.gelu_ready, 1)
                act.wait_ge(s.w_ready, r + 1)
                for j in range(SLOTS):
                    if not (isinstance(r, int) and r == 0):
                        act.wait_ge(v_used[j], r)
                    A(diag[:, j, 0:base.shape[1]], base, ACT.Copy, scale=w8[:, a, j:j + 1]).then_inc(s.diag_ready, 1)

            scores(0)
            with act.Fori(0, PH) as h:
                best_exp(NB, h + 1)
            scores(1)
            with act.Fori(0, PH) as h:
                best_exp(P, h + (PH + 1))
            weigh(0, 0, consts[:, C_TK:C_TK + NB])
            act.wait_ge(s.ms_ready, 2 * NT + 3)
            step(A(rstd[0:NB, 0:1], ssx[0:NB, 0:1], ACT.Sqrt, bias=eps[0:NB, :], scale=1.0 / D), s.mr_ready)
            for t in range(NT):
                if t + 1 < NT:
                    scores(t + 2)
                with act.Fori(0, PH) as h:
                    for a in range(2):
                        weigh(h * 2 + (1 + 2 * PH * t + a), (1 + a) % 2, ident)
                        if a == 1 and t + 1 < NT:
                            best_exp(P, h + (PH * (t + 2) + 1))
                act.wait_ge(s.ms_ready, 2 * NT + 4 + t)
                step(A(rstd[:, 0:1], ssx[:, 0:1], ACT.Sqrt, bias=eps, scale=1.0 / D), s.mr_ready)

        @block.tensor
        def _(pe):
            dring = Ring(pe, dbank, s.dring_full, s.dring_free)
            aring = Ring(pe, abank, s.aring_full, s.aring_free)
            stream = [0]

            def mm(out, lhsT, rhs, first=True, last=True):
                return pe.matmul(out, lhsT, rhs, start=first, stop=last)

            def weights():
                n = stream[0]
                pe.wait_ge(w_full[n % 4], 16 * (n // 4 + 1))
                stream[0] += 1
                return wb[:, n % 4, :].rearrange("p (k m) -> p k m", m=P)

            def block_before_used(ins):
                if stream[0] > 1:
                    ins.then_inc(s.w_used, 1)

            def project(x):
                w = weights()
                for c in range(2):
                    b = aring.to_fill()
                    for k in range(KT):
                        last = mm(b[:, 0:HALF], w[:, k, :], x[:, k, c * HALF:(c + 1) * HALF], k == 0, k == KT - 1)
                        if c == 0 and k == 0:
                            block_before_used(last)
                    last.then_inc(s.aring_full, 1)

            def modulation(tiles):
                for g in range(tiles // KT):
                    b = dring.to_fill()
                    for j in range(KT):
                        w = weights()
                        for k in range(KT):
                            last = mm(b[:, 9 * j:9 * j + 9], w[:, k, :], cT[:, k, :], k == 0, k == KT - 1)
                            if k == 0:
                                block_before_used(last)
                    last.then_inc(s.dring_full, 1)

            pe.wait_ge(s.silu_c, 1)
            modulation(B_ADA1)
            pe.wait_ge(s.consts_in, 32)
            pe.wait_ge(s.xn_ready, NT + 1)
            for k in range(KT):
                b = dring.to_fill()
                for t in range(NT):
                    last = pe.transpose(b[:, t * P:(t + 1) * P], x_t[:, t, k * P:(k + 1) * P], ident)
                last.then_inc(s.dring_full, 1)
            b = dring.to_fill()
            for k in range(KT):
                last = pe.transpose(b[:, k * NB:(k + 1) * NB], x_t[0:NB, NT, k * P:(k + 1) * P], consts[0:NB, 0:NB])
            last.then_inc(s.dring_full, 1)
            pe.wait_ge(s.hT_ready, KT + 1)
            for m in range(CT_N):
                project(hT)
            pe.wait_ge(s.wnat_in, 16)
            for t in range(NT + 1):
                b = aring.to_fill()
                for k in range(KT):
                    last = mm(b[0:ROWS[t], 0:NAT_W], hT[:, k, tcols(t)], wnat[:, k, :], k == 0, k == KT - 1)
                last.then_inc(s.aring_full, 1)
            for m in range(B_Q):
                project(hT)
            pe.wait_ge(s.nat_ready, NT)
            b = aring.to_fill()
            for t in range(NT):
                last = pe.transpose(b[:, t * P:(t + 1) * P], nat[:, t, 0:P], ident)
            last.then_inc(s.aring_full, 1)
            pe.wait_ge(s.rels_ready, 1)
            b = aring.to_fill()
            mm(b[0:HQ, 0:384], relx[:, :], onehot[:, :]).then_inc(s.aring_full, 1)
            for m in range(2 * DH):
                pe.wait_ge(s.sq_ready, m + 1)
                for c in range(2):
                    b = aring.to_fill()
                    mm(b[:, 0:HALF], ones, sqb[:, m % 2, c * HALF:(c + 1) * HALF]).then_inc(s.aring_full, 1)
            for m in range(B_Z + B_GA + B_GB):
                project(hT)
            modulation(B_ADA2)
            pe.wait_ge(s.qT_ready, 1)
            pe.wait_ge(s.kT_ready, 1)
            for blk in range(NT):
                lo = 0 if blk else P
                for i in range(HQ // 2):
                    b = dring.to_fill()
                    for e in range(2):
                        h = 2 * i + e
                        g, rows = h % HG, slice(64 * (h // HG), 64 * (h // HG) + 64)
                        last = mm(b[:, e * 256 + lo:e * 256 + 256], qT[rows, g, blk * P:(blk + 1) * P],
                                  kT[rows, (blk - 1) * P + lo:(blk + 1) * P])
                    last.then_inc(s.dring_full, 1)
                pe.wait_ge(s.prob_ready, blk + 1)
                parts = [(h, c) for h in range(HQ) for c in ((1,) if blk == 0 else (0, 1))]
                for i in range(len(parts) // 4):
                    b = aring.to_fill()
                    for e, (h, c) in enumerate(parts[4 * i:4 * i + 4]):
                        last = pe.transpose(b[:, e * P:(e + 1) * P], prob[:, h, c * P:(c + 1) * P], ident)
                    last.then_inc(s.aring_full, 1)
                pe.wait_ge(s.probT_ready, blk + 1)
                b = aring.to_fill()
                for i, (h, c) in enumerate(parts):
                    half = 64 * (h // HG)
                    last = mm(b[half:half + 64, (h % HG) * P:(h % HG + 1) * P],
                              nat[:, blk - 1 + c, P + half:P + half + 64], probT[:, i, :],
                              blk == 0 or c == 0, c == 1)
                last.then_inc(s.aring_full, 1)
            pe.wait_ge(s.keyc_in, 16)
            for i in range(2):
                b = aring.to_fill()
                for e in range(4):
                    last = pe.transpose(b[:, e * P:(e + 1) * P], keyc[:, 4 * i + e, :], ident)
                last.then_inc(s.aring_full, 1)
            pe.wait_ge(s.kTs_ready, 1)
            for kv in range(2):
                b = dring.to_fill()
                rows = slice(64 * kv, 64 * kv + 64)
                for q in range(NB):
                    last = mm(b[:, q * HG:(q + 1) * HG], probT[rows, q, :], qT[rows, :, SEQ + q])
                last.then_inc(s.dring_full, 1)
            b = dring.to_fill()
            mm(b[0:64, 0:P], rels[:, :], onehot[:, P:2 * P]).then_inc(s.dring_full, 1)
            pe.wait_ge(s.lt_ready, 1)
            b = dring.to_fill()
            pe.transpose(b[0:64, 0:P], lt64, ident).then_inc(s.dring_full, 1)
            pe.wait_ge(s.prob_ready, NT + 1)
            b = dring.to_fill()
            pe.transpose(b[:, 0:64], prob[0:64, 0, 0:P], consts[0:64, 0:64]).then_inc(s.dring_full, 1)
            pe.wait_ge(s.lt_ready, 2)
            pe.wait_ge(s.valc_in, 16)
            b = aring.to_fill()
            for q in range(NB):
                for kv in range(2):
                    last = mm(b[64 * kv:64 * kv + 64, q * HG:(q + 1) * HG], valc[:, q, 64 * kv:64 * kv + 64],
                              lt64[:, q * HQ + kv * HG:q * HQ + kv * HG + HG])
            last.then_inc(s.aring_full, 1)
            pe.wait_ge(s.g_ready, 1)
            b = aring.to_fill()
            for i, tri in enumerate((le, gt, ones)):
                last = mm(b[:, 16 * i:16 * i + 16], tri, gg[:, 0:NT, :])
            last.then_inc(s.aring_full, 1)
            pe.wait_ge(s.l2_done, 2 * DH)
            for ch in range(NT):
                for first in (DH, 2 * DH):
                    b = dring.to_fill()
                    for h in range(DH):
                        last = pe.transpose(b[:, h * P:(h + 1) * P], ct[:, first + h, ch * P:(ch + 1) * P], ident)
                    last.then_inc(s.dring_full, 1)
            for ch in range(NT):
                here = slice(ch * P, (ch + 1) * P)
                pe.wait_ge(s.mg_ready, ch + 1)
                b = aring.to_fill()
                mm(b[:, :], le, mgt[:, ch % 2, :]).then_inc(s.aring_full, 1)
                b = aring.to_fill()
                for h in range(DH):
                    last = mm(b[:, h * P:(h + 1) * P], mgt[:, ch % 2, h * P:(h + 1) * P], le)
                last.then_inc(s.aring_full, 1)
                for right in (DH, 0):
                    b = dring.to_fill()
                    for h in range(DH):
                        last = mm(b[:, h * P:(h + 1) * P], ct[:, DH + h, here], ct[:, right + h, here])
                    last.then_inc(s.dring_full, 1)
            for lv in range(7):
                for ch in range(NT):
                    pe.wait_ge(s.lm_ready, NT * lv + ch + 1)
                    pe.wait_ge(s.wt_ready, NT * lv + ch + 1)
                    b = aring.to_fill()
                    for h in range(DH):
                        hs = slice(h * P, (h + 1) * P)
                        last = mm(b[:, hs], Lm[:, ch, hs], Wc[:, ch, hs])
                    last.then_inc(s.aring_full, 1)
                for ch in range(NT):
                    pe.wait_ge(s.a2_ready, NT * lv + ch + 1)
                    for left, right in ((Tc, A2), (A2, Tc)):
                        b = dring.to_fill()
                        for h in range(DH):
                            hs = slice(h * P, (h + 1) * P)
                            last = mm(b[:, hs], left[:, ch, hs], right[:, ch, hs])
                        last.then_inc(s.dring_full, 1)
            pe.wait_ge(s.wt_ready, NT * 8)
            for ch in range(NT):
                def per_head(ring, full, left, right):
                    b = ring.to_fill()
                    for h in range(DH):
                        last = mm(b[:, h * P:(h + 1) * P], left(h), right[:, h * P:(h + 1) * P])
                    last.then_inc(full, 1)
                here = slice(ch * P, (ch + 1) * P)
                pe.wait_ge(s.S_ready, ch + 1)
                per_head(dring, s.dring_full, lambda h: ct[:, DH + h, here], delta)
                per_head(aring, s.aring_full, lambda h: ct[:, h, here], delta)
                pe.wait_ge(s.r_ready, ch + 1)
                per_head(aring, s.aring_full, lambda h: Wc[:, ch, h * P:(h + 1) * P], E1[:, 0, :])
                pe.wait_ge(s.vn_ready, ch + 1)
                per_head(dring, s.dring_full, lambda h: kdec[:, ch, h * P:(h + 1) * P], E2[:, 0, :])
                per_head(dring, s.dring_full, lambda h: ATc[:, ch, h * P:(h + 1) * P], E2[:, 0, :])
                pe.wait_ge(s.on_ready, ch + 1)
                b = dring.to_fill()
                for h in range(DH):
                    last = pe.transpose(b[:, h * P:(h + 1) * P], E2[:, 1, h * P:(h + 1) * P], ident)
                last.then_inc(s.dring_full, 1)
            pe.wait_ge(s.sg_ready, 1)
            b = aring.to_fill()
            mm(b[:, 0:64], consts[0:NB, C_ONE:C_ONE + P], at(E0 + 1832 + 32 * 3, 64)[0:NB, :]).then_inc(s.aring_full, 1)
            pe.wait_ge(s.sdel_in, 16)
            b = dring.to_fill()
            for h in range(DH):
                for q in range(NB):
                    c0 = 2 * (h * NB + q)
                    last = mm(b[:, c0:c0 + 2], sdel[:, h, q, :], ct[:, h:h + DH + 1:DH, SEQ + q])
            last.then_inc(s.dring_full, 1)
            pe.wait_ge(s.sp_ready, 1)
            b = dring.to_fill()
            mm(b[:, 0:32], ones, sdv[5]).then_inc(s.dring_full, 1)
            b = dring.to_fill()
            for h in range(DH):
                last = pe.transpose(b[0:NB, h * P:(h + 1) * P], sdv[12][:, h * NB:(h + 1) * NB], ident)
            last.then_inc(s.dring_full, 1)
            pe.wait_ge(s.sn_ready, 1)
            b = dring.to_fill()
            for h in range(DH):
                last = pe.transpose(b[0:NB, h * P:(h + 1) * P], sdv[8][:, h * NB:(h + 1) * NB], ident)
            last.then_inc(s.dring_full, 1)
            pe.wait_ge(s.sn_ready, 2)
            b = aring.to_fill()
            mm(b[:, 0:32], ones, sdv[10]).then_inc(s.aring_full, 1)
            for h in range(DH):
                pe.wait_ge(s.vd_ready, h + 1)
                for g in range(2):
                    b = dring.to_fill()
                    mm(b[:, :], kn8[:, h * P:(h + 1) * P], at(R0 + 1024 * (h % 2), 1024)[0:NB, g * 512:(g + 1) * 512]).then_inc(s.dring_full, 1)
            pe.wait_ge(s.att_done, 1)
            pe.wait_ge(s.od_done, NT + 1)
            for m in range(B_BR):
                w = weights()
                for c in range(2):
                    for k0, x in ((0, attT), (4, odT)):
                        b = dring.to_fill()
                        for k in range(4):
                            last = mm(b[:, 0:HALF], w[:, k0 + k, :], x[:, k, c * HALF:(c + 1) * HALF], k == 0, k == 3)
                            if c == 0 and k0 == 0 and k == 0:
                                block_before_used(last)
                        last.then_inc(s.dring_full, 1)
            for i, v in enumerate((2, 4, 3, 5)):
                pe.wait_ge(s.dg_ready, i + 1)
                for g in range(2):
                    b = dring.to_fill()
                    mm(b[:, :], ones, t1[:, g * 512:(g + 1) * 512]).then_inc(s.dring_full, 1)
                for g in range(2):
                    b = dring.to_fill()
                    for j in range(4):
                        last = pe.transpose(b[0:NB, j * P:(j + 1) * P], adaT[:, v * KT + 4 * g + j, 1:9], ident)
                    last.then_inc(s.dring_full, 1)
            pe.wait_ge(s.merged_ready, KT)
            pe.wait_ge(s.wout_in, 16)
            for i in range(NT + 2):
                if i <= NT:
                    for g in range(2):
                        b = dring.to_fill()
                        for k in range(KT):
                            last = mm(b[0:ROWS[i], :], gaT[:, k, tcols(i)], wout[:, k, g * 512:(g + 1) * 512], k == 0, k == KT - 1)
                        last.then_inc(s.dring_full, 1)
                if 1 <= i <= NT:
                    pe.wait_ge(s.h2_ready, i)
                    for g in range(2):
                        b = aring.to_fill()
                        for j in range(4):
                            last = pe.transpose(b[:, j * P:(j + 1) * P], h2[:, i - 1, (4 * g + j) * P:(4 * g + j + 1) * P], ident)
                        last.then_inc(s.aring_full, 1)
            pe.wait_ge(s.h2_ready, NT + 1)
            b = aring.to_fill()
            for k in range(KT):
                last = pe.transpose(b[:, k * NB:(k + 1) * NB], h2s[0:NB, k * P:(k + 1) * P], consts[0:NB, 0:NB])
            last.then_inc(s.aring_full, 1)
            for g in range(2):
                b = dring.to_fill()
                mm(b[:, :], consts[0:NB, C_KT:C_KT + P], h2s[0:NB, g * 512:(g + 1) * 512]).then_inc(s.dring_full, 1)
            pe.wait_ge(s.h2T_ready, 1)
            for m in range(B_QRY):
                project(h2T)

            def scores(n):
                t = (n - 1) % (NT + 1)
                for g in range(4):
                    b = aring.to_fill()
                    for e in range(4):
                        m = 4 * g + e
                        last = mm(b[0:ROWS[t], e * P:(e + 1) * P], qryT[:, m, tcols(t)], skt[:, m % 2, :])
                    last.then_inc(s.aring_full, 1)

            def clear(n):
                if n:
                    pe.wait_ge(s.f_read, n)
                for g in range(2):
                    pe.matmul(fsum[g][:, :], zeros[:, :], consts[:, 0:512], start=True, stop=False, skip_group_check=True)

            def add_round(r, cols_):
                for j in range(SLOTS):
                    pe.wait_ge(s.diag_ready, r * SLOTS + (j + 1))
                    pe.wait_ge(v_in[j], r * 16 + 16)
                    for g in range(2):
                        last = pe.matmul(fsum[g][0:cols_, :], diag[:, j, 0:cols_], vring[:, j, g * 512:(g + 1) * 512],
                                         start=False, stop=False, skip_group_check=True)
                    last.then_inc(v_used[j], 1)

            pe.wait_ge(s.skt_in, 16)
            pe.wait_ge(s.qry_ready, 1)
            scores(0)
            scores(1)
            clear(0)
            add_round(0, NB)
            for t in range(NT):
                if t + 1 < NT:
                    scores(t + 2)
                clear(t + 1)
                with pe.Fori(0, PH) as h:
                    for a in range(2):
                        add_round(h * 2 + (1 + 2 * PH * t + a), P)

        @block.vector
        def _(dve):
            step = Steps(dve, s.dve_step)
            ring = Ring(dve, dbank, s.dring_full, s.dring_free)
            TT, TS, STT, TTR = dve.tensor_tensor, dve.tensor_scalar, dve.scalar_tensor_tensor, dve.tensor_tensor_reduce
            copy, recip = dve.tensor_copy, dve.reciprocal

            def bc(v, axis, n):
                shape = list(v.shape)
                shape.insert(axis, n)
                return v.unsqueeze(axis).to_broadcast(shape)

            def three(v, q=P):
                return v.rearrange("p (a q) -> p a q", q=q)

            step(dve.memset(ubuf, 0.0))
            step(dve.memset(eps, EPS))
            step(dve.memset(eps128, EPS * P))
            step(dve.memset(nat[:, NT, :], 0.0))
            step(dve.memset(zeros[:, :], 0.0))
            step(dve.memset(relx[32:33, :], NEG))
            dve.wait_ge(s.x_in, 32)
            for t in range(NT + 1):
                r = slice(0, ROWS[t])
                step(TTR(junk[r, :], x_t[r, t, :], x_t[r, t, :], 1.0, 0.0, ALU.mult, ALU.add, ssx[r, t:t + 1]), s.ss_ready)
            for t in range(NT + 1):
                dve.wait_ge(s.rms_ready, t + 1)
                step(recip(rstd[0:ROWS[t], t:t + 1], rstd[0:ROWS[t], t:t + 1]), s.rstd_ready)

            def modulation(v):
                a = adaT[:, v * KT:(v + 1) * KT, :]
                b = ring.to_read()
                step(TT(a, b[:, 0:72].rearrange("p (k c) -> p k c", c=9),
                        bc(cols[:, K_BADA + v * KT:K_BADA + (v + 1) * KT], 2, 9), ALU.add), s.dring_free)
                gain = {1: K_GPM, 2: K_GQM, 4: K_GPF, 5: K_GQF}.get(v)
                if gain is not None:
                    step(STT(a, a, 1.0 if v in (1, 4) else 0.0, bc(cols[:, gain:gain + KT], 2, 9), ALU.add, ALU.mult))

            dve.wait_ge(s.cols_in, 32)
            modulation(0)
            modulation(1)
            for k in range(KT):
                b = ring.to_read()
                step(TS(hT[:, k, 0:SEQ], b[:, :], adaT[:, KT + k, 0:1], adaT[:, k, 0:1], ALU.mult, ALU.add), s.dring_free)
                dve.sem_inc(s.hT_ready, 1)
            b = ring.to_read()
            step(TT(hT[:, :, SEQ:TOK], three(b[:, 0:KT * NB], NB), adaT[:, KT:2 * KT, 1:9], ALU.mult), s.dring_free)
            step(TT(hT[:, :, SEQ:TOK], hT[:, :, SEQ:TOK], adaT[:, 0:KT, 1:9], ALU.add), s.hT_ready)
            step(copy(rels[:, :].rearrange("p (b h) -> p b h", h=HQ), bc(relx[:, :], 1, NB)), s.rels_ready)
            dve.wait_ge(s.cst_in, 16)
            for m in range(CT_N):
                dve.wait_ge(s.conv_in, m + 1)
                u = ubuf[:, m % 2, :]
                us = u[:, 515:547].rearrange("p (b i) -> p b i", i=4)
                step(copy(us[:, :, 0:3], cst[:, m, :, :]))
                step(copy(cpo[:, m, :], u[:, SEQ:SEQ + 3]))
                step(copy(cso[:, m, :, :], us[:, :, 1:4]))
                for i in range(4):
                    w = cols[:, K_CONV + 4 * m + i:K_CONV + 4 * m + i + 1]
                    for out, src in ((ct[:, m, 0:SEQ], u[:, i:i + SEQ]), (ct[:, m, SEQ:TOK], us[:, :, i])):
                        if i == 0:
                            step(TS(out, src, w, None, ALU.mult))
                        elif i < 3 or out.shape[1] == SEQ:
                            step(STT(out, src, w, out, ALU.mult, ALU.add))
                        else:
                            step(STT(out, src, w, out, ALU.mult, ALU.add), s.conv_out)
            for m in range(2 * DH + 1):
                if m < 2 * DH:
                    dve.wait_ge(s.silu_out, m + 1)
                    step(TT(sqb[:, m % 2, :], ct[:, m, :], ct[:, m, :], ALU.mult), s.sq_ready)
                if m >= 1:
                    dve.wait_ge(s.rn_ready, m)
                    r = rnb[:, (m - 1) % 2, :]
                    step(recip(r, r))
                    step(TT(ct[:, m - 1, :], ct[:, m - 1, :], r, ALU.mult), s.l2_done)
            dve.wait_ge(s.nat_ready, NT + 1)
            step(TT(gtmp, nat[:, :, 256:260], bc(cols[:, K_DT:K_DT + 4], 1, NT + 1), ALU.add), s.gx_ready)
            for v in (2, 3, 4, 5):
                modulation(v)
            dve.wait_ge(s.beta_ready, 1)
            step(STT(gg, gtmp, 0.0, gtmp2, ALU.max, ALU.add))
            step(STT(gg, gg, -1.0, bc(ealog, 1, NT + 1), ALU.mult, ALU.mult), s.g_ready)
            dve.wait_ge(s.bias_in, 16)
            for blk in range(NT):
                lo = 0 if blk else P
                if blk:
                    dve.wait_ge(s.probT_ready, blk)
                for i in range(HQ // 2):
                    b = ring.to_read()
                    step(STT(prob[:, 2 * i:2 * i + 2, lo:256], three(b[:, :], 256)[:, :, lo:256], HD ** -0.5,
                             bias[:, 2 * i:2 * i + 2, lo:256], ALU.mult, ALU.add), s.dring_free)
                step(dve.tensor_reduce(mx8, prob[:, :, lo:256], AX.X, ALU.max))
                step(TT(mx8, mx8, cols[:, K_SINK:K_SINK + 8], ALU.max))
                step(TT(es8, cols[:, K_SINK:K_SINK + 8], mx8, ALU.subtract))
                step(TS(nm8, mx8, -1.0, None, ALU.mult), s.nm_ready)
                dve.wait_ge(s.exp_done, blk + 1)
                step(TT(sm8, sm8, es8, ALU.add))
                step(recip(sm8, sm8))
                step(TT(prob[:, :, lo:256], prob[:, :, lo:256], bc(sm8, 2, 256 - lo), ALU.mult), s.prob_ready)
            dve.wait_ge(s.probT_ready, NT)
            for kv in range(2):
                b = ring.to_read()
                step(TS(lt64.rearrange("p (q v g) -> p q v g", v=2, g=HG)[:, :, kv, :], three(b[:, 0:NB * HG], HG), HD ** -0.5, None, ALU.mult), s.dring_free)
            dve.sem_inc(s.lt_ready, 1)
            q0 = prob[0:64, 0, 0:P]
            b = ring.to_read()
            step(copy(q0, b[0:64, 0:P]), s.dring_free)
            b = ring.to_read()
            step(TT(q0, b[0:64, 0:P], q0, ALU.add), s.dring_free)
            mx, nm, sm_, es, sink = mx8[0:64, 0:1], nm8[0:64, 0:1], sm8[0:64, 0:1], es8[0:64, 0:1], cols[0:64, K_SINKS:K_SINKS + 1]
            step(dve.tensor_reduce(mx, q0, AX.X, ALU.max))
            step(TT(mx, mx, sink, ALU.max))
            step(TT(es, sink, mx, ALU.subtract))
            step(TS(nm, mx, -1.0, None, ALU.mult), s.nm_ready)
            dve.wait_ge(s.exp_done, NT + 1)
            step(TT(sm_, sm_, es, ALU.add))
            step(recip(sm_, sm_))
            step(TS(q0, q0, sm_, None, ALU.mult), s.prob_ready)
            b = ring.to_read()
            step(copy(lt64, b[:, 0:64]), s.dring_free)
            dve.sem_inc(s.lt_ready, 1)
            step(copy(three(svv, NB), ct[:, 2 * DH:3 * DH, SEQ:TOK]))
            dve.wait_ge(s.ex_ready, 1)
            for ch in range(NT):
                b = ring.to_read()
                step(TT(three(kdec[:, ch, :]), three(b[:, :]), bc(ex[:, 16 + 4 * ch:20 + 4 * ch], 2, P), ALU.mult), s.dring_free)
                b = ring.to_read()
                step(TT(three(vb[:, ch, :]), three(b[:, :]), bc(beta[:, ch, :], 2, P), ALU.mult), s.dring_free)
            step(STT(three(nbeg, DH), three(ex[:, 0:16], DH), -1.0, beta[:, 0:NT, :], ALU.mult, ALU.mult))

            def spread(ch):
                step(TT(three(mgt[:, ch % 2, :]), bc(gt, 1, DH), bc(gg[:, ch, :], 2, P), ALU.mult), s.mg_ready)

            spread(0)
            for ch in range(NT):
                if ch + 1 < NT:
                    spread(ch + 1)
                dve.wait_ge(s.E_ready, ch + 1)
                e1, e2 = three(E1[:, ch % 2, :]), three(E2[:, ch % 2, :])
                step(TT(e1, e1, bc(gt, 1, DH), ALU.mult))
                step(TT(e1, e1, bc(beta[:, ch, :], 2, P), ALU.mult))
                b = ring.to_read()
                step(TT(Lc[:, ch, :], b[:, :], E1[:, ch % 2, :], ALU.mult), s.dring_free)
                step(TT(e2, e2, bc(le, 1, DH), ALU.mult))
                b = ring.to_read()
                step(TT(ATc[:, ch, :], b[:, :], E2[:, ch % 2, :], ALU.mult), s.dring_free)
                dve.sem_inc(s.L_ready, 1)
                step(copy(three(Tc[:, ch, :]), bc(ident, 1, DH)))
                step(copy(three(Wc[:, ch, :]), bc(ident, 1, DH)), s.wt_ready)
            for lv in range(7):
                mask = consts[:, C_LVL + lv * P:C_LVL + (lv + 1) * P]
                for ch in range(NT):
                    step(TT(three(Lm[:, ch, :]), three(Lc[:, ch, :]), bc(mask, 1, DH), ALU.mult), s.lm_ready)
                for ch in range(NT):
                    b = ring.to_read()
                    step(TT(Wc[:, ch, :], Wc[:, ch, :], b[:, :], ALU.subtract), s.dring_free)
                    b = ring.to_read()
                    step(TT(Tc[:, ch, :], Tc[:, ch, :], b[:, :], ALU.subtract), s.dring_free)
                    dve.sem_inc(s.wt_ready, 1)
            R, qs, o = E1[:, 0, :], E1[:, 1, :], E2[:, 1, :]
            step(dve.memset(delta[:, :], 0.0), s.S_ready)
            for ch in range(NT):
                cs = slice(4 * ch, 4 * ch + 4)
                b = ring.to_read()
                step(TT(three(R), three(b[:, :]), bc(nbeg[:, cs], 2, P), ALU.mult), s.dring_free)
                step(TT(R, R, vb[:, ch, :], ALU.add), s.r_ready)
                dve.wait_ge(s.qs_ready, ch + 1)
                step(TT(three(o), three(qs), bc(ex[:, cs], 2, P), ALU.mult))
                step(TT(three(delta[:, :]), three(delta[:, :]), bc(ex[:, 32 + 4 * ch:36 + 4 * ch], 2, P), ALU.mult))
                b = ring.to_read()
                step(TT(delta[:, :], delta[:, :], b[:, :], ALU.add), s.dring_free)
                dve.sem_inc(s.S_ready, 1)
                b = ring.to_read()
                step(TT(o, o, b[:, :], ALU.add), s.dring_free)
                step(TT(R, o, o, ALU.mult))
                step(dve.tensor_reduce(rms4, three(R), AX.X, ALU.add), s.o_ready)
                dve.wait_ge(s.orms_ready, ch + 1)
                step(recip(rms4, rms4))
                step(TT(three(o), three(o), bc(rms4, 2, P), ALU.mult), s.on_ready)
                b = ring.to_read()
                here = slice(ch * P, (ch + 1) * P)
                step(STT(odT[:, :, here], three(b[:, :]), cols[:, K_DN:K_DN + 1], zT[:, :, here], ALU.mult, ALU.mult), s.dring_free)
                dve.sem_inc(s.od_done, 1)
            eg, be, rr, sgx, prod, ks_, qs_, vn, oo, oo2 = sdv[0], sdv[1], sdv[2], at(E0 + 1832 + 96, 64), sdv[5], sdv[6], sdv[7], sdv[8], sdv[9], sdv[10]
            i8 = consts[0:NB, 0:NB]
            for i, v in enumerate((gg, beta)):
                step(TT(three(sgx[0:NB, 32 * i:32 * i + 32], NB), bc(v[0:NB, NT, :], 2, NB), bc(i8, 1, DH), ALU.mult), s.dve_step if i == 0 else s.sg_ready)
            step(copy(three(sdv[12], NB), ct[:, DH:2 * DH, SEQ:TOK]))
            step(TT(three(prod, NB), ct[:, 0:DH, SEQ:TOK], three(sdv[12], NB), ALU.mult), s.sp_ready)
            dve.wait_ge(s.sa_ready, 1)
            b = ring.to_read()
            kq = b[:, 0:64].rearrange("p (c z) -> p c z", z=2)
            step(TT(ks_, kq[:, :, 1], eg, ALU.mult))
            step(TT(qs_, kq[:, :, 0], eg, ALU.mult), s.dring_free)
            step(TT(vn, svv, ks_, ALU.subtract))
            step(TT(vn, vn, be, ALU.mult), s.sn_ready)
            b = ring.to_read()
            step(TT(oo, b[:, 0:32], vn, ALU.mult), s.dring_free)
            step(TT(oo, oo, qs_, ALU.add))
            step(TT(oo2, oo, oo, ALU.mult), s.sn_ready)
            b = ring.to_read()
            step(copy(kn8, b[0:NB, :]), s.dring_free)
            b = ring.to_read()
            step(copy(vn8, b[0:NB, :]), s.dring_free)
            for h in range(DH):
                vd = at(R0 + 1024 * (h % 2), NB, P)[0:NB]
                step(TT(vd, bc(vn8[:, h * P:(h + 1) * P], 1, NB), bc(i8, 2, P), ALU.mult), s.vd_ready)
                for g in range(2):
                    st = sdel[:, h, 4 * g:4 * g + 4, :]
                    b = ring.to_read()
                    step(TT(st, st, bc(eg[:, h * NB + 4 * g:h * NB + 4 * g + 4], 2, P), ALU.mult))
                    step(TT(st, st, three(b[:, :]), ALU.add), s.dring_free)
            dve.sem_inc(s.sd_ready, 1)
            dve.wait_ge(s.sa_ready, 2)
            step(recip(rr, rr))
            step(TT(oo, oo, rr, ALU.mult))
            step(STT(odT[:, :, SEQ:TOK], three(oo, NB), cols[:, K_DN:K_DN + 1], zT[:, :, SEQ:TOK], ALU.mult, ALU.mult), s.od_done)
            for m in range(KT):
                for c in range(2):
                    for g in (gaT, gbT):
                        v = g[:, m, c * HALF:(c + 1) * HALF]
                        b = ring.to_read()
                        step(TT(v, v, b[:, 0:HALF], ALU.mult), s.dring_free)
                step(TT(gaT[:, m, :], gaT[:, m, :], gbT[:, m, :], ALU.add), s.merged_ready)
            dve.wait_ge(s.out_small, 64)
            for v, vp_, vs_ in ((2, v_g1, s_g1), (4, v_a2, s_a2), (3, v_s2, s_s2), (5, v_g2, s_g2)):
                step(TT(three(t1), bc(ident, 1, KT), bc(adaT[:, v * KT:(v + 1) * KT, 0], 2, P), ALU.mult), s.dg_ready)
                for dst, r in ((vp_, P), (vs_, NB)):
                    for g in range(2):
                        b = ring.to_read()
                        step(copy(dst[0:r, g * 512:(g + 1) * 512], b[0:r, :]), s.dring_free)

            def mean_square(src, r, k):
                step(TTR(t2[r, :], src, src, 1.0, 0.0, ALU.mult, ALU.add, ssx[r, 0:1]), s.ms_ready)
                dve.wait_ge(s.mr_ready, k)
                step(recip(rstd[r, 0:1], rstd[r, 0:1]))

            dve.wait_ge(s.xr_in, 32)
            for t in range(NT + 1):
                r = slice(0, ROWS[t])
                g1, a2, s2 = (v_g1, v_a2, v_s2) if t < NT else (s_g1, s_a2, s_s2)
                h = h2[r, t, :] if t < NT else h2s[r, :]
                for g in range(2):
                    b = ring.to_read()
                    step(copy(t1[r, g * 512:(g + 1) * 512], b[r, :]), s.dring_free)
                mean_square(t1[r, :], r, 2 * t + 1)
                step(STT(t1[r, :], t1[r, :], rstd[r, 0:1], g1[r, :], ALU.mult, ALU.mult))
                step(TT(x_t[r, t, :], x_t[r, t, :], t1[r, :], ALU.add))
                mean_square(x_t[r, t, :], r, 2 * t + 2)
                step(STT(h, x_t[r, t, :], rstd[r, 0:1], a2[r, :], ALU.mult, ALU.mult))
                step(TT(h, h, s2[r, :], ALU.add), s.h2_ready)
            for g in range(2):
                b = ring.to_read()
                step(copy(h2sb[:, g * 512:(g + 1) * 512], b[:, :]), s.dring_free)

            def search(rows, n, h, k, base):
                r = slice(0, rows)
                at_ = [base]

                def then(ins):
                    ins.then_inc(s.dve_step, 1)
                    at_[0] = at_[0] + 1
                    dve.wait_ge(s.dve_step, at_[0])
                def alone(ins):
                    then(ins)
                    dve.sem_inc(s.dve_turn, 1)

                def sixteen(val, idx, src, spare):
                    alone(dve.max(val[:, 0:8], src))
                    alone(dve.max_index(idx[:, 0:8], val[:, 0:8], src))
                    alone(dve.match_replace(spare, val[:, 0:8], src, -3e38))
                    alone(dve.max(val[:, 8:16], spare))
                    then(dve.max_index(idx[:, 8:16], val[:, 8:16], spare))

                alone(copy(s_in[r].rearrange("p a q -> p (a q)"), sc[r, n % 2, bass.ds(h * (2 * NKEY), 2 * NKEY)]))

                for p in range(2):
                    sixteen(sv[r, p, :], si[r, p, :], s_in[r, p, :], s_out[r, p, :])
                    if p == 0:
                        dve.sem_inc(s.dve_turn, 1)
                alone(TT(three(cand[r, :], TOPK), bc(sv[r, 0, :], 2, TOPK), bc(sv[r, 1, :], 1, TOPK), ALU.add))
                sixteen(best[r, :], pos[r, :], cand[r, :], cand2[r, :])
                TS(nbest[r, :], best[r, 0:1], -1.0, None, ALU.mult).then_inc(s.best_ready, 1)
                then(copy(sif[r], si[r]))
                then(TS(pint[r, 0, :], pos[r, :], 4, None, ALU.logical_shift_right))
                then(TS(pint[r, 1, :], pos[r, :], 15, None, ALU.bitwise_and))
                then(copy(pf[r], pint[r]))
                then(TT(hit[r].rearrange("p a k i -> p (a k) i"), bc(pf[r].rearrange("p a k -> p (a k)"), 2, TOPK),
                        bc(consts[r, C_IOTA:C_IOTA + TOPK], 1, 2 * TOPK), ALU.is_equal))
                then(TT(hit[r], hit[r], bc(sif[r], 2, TOPK), ALU.mult))
                then(dve.tensor_reduce(ee[r], hit[r], AX.X, ALU.add))
                then(STT(ef[r, :], ee[r, 0, :], float(NKEY), ee[r, 1, :], ALU.mult, ALU.add))
                then(copy(eidx[r, n % 2, bass.ds(h * TOPK, TOPK)], ef[r, :]))
                dve.wait_ge(s.gexp_ready, k)
                then(recip(gsum[r, :], gsum[r, :]))
                then(TS(gexp[r, :], gexp[r, :], gsum[r, 0:1], None, ALU.mult))
                copy(gate[r, n % 2, bass.ds(h * TOPK, TOPK)], gexp[r, :]).then_inc(s.topk_done, 1)
                dve.wait_ge(s.topk_done, k)

            N_SEARCH = 28

            def dots(r, a, x, g):
                for j in range(SLOTS):
                    dve.wait_ge(u_in[j], r * 16 + 16)
                    TTR(uring[:, j, :], uring[:, j, :], x, 1.0, 0.0, ALU.mult, ALU.add, act8[:, a, j:j + 1]).then_inc(u_used[j], 1)
                dve.wait_ge(s.gelu_ready, r + 1)
                TT(w8[:, a, :], act8[:, a, :], g, ALU.mult).then_inc(s.w_ready, 1)

            def finish(t, n, g2):
                r = slice(0, ROWS[t])
                for j in range(SLOTS):
                    dve.wait_ge(v_used[j], 1 if n == 0 else 1 + 2 * PH * n)
                for g in range(2):
                    ins = copy(t1[r, g * 512:(g + 1) * 512], fsum[g][r, :])
                    fstep(ins, s.f_read if g else None)
                fstep(TTR(t2[r, :], t1[r, :], t1[r, :], 1.0, 0.0, ALU.mult, ALU.add, ssx[r, 0:1]), s.ms_ready)
                dve.wait_ge(s.mr_ready, 2 * (NT + 1) + n + 1)
                fstep(recip(rstd[r, 0:1], rstd[r, 0:1]))
                fstep(STT(t1[r, :], t1[r, :], rstd[r, 0:1], g2[r, :], ALU.mult, ALU.mult))
                fstep(TT(x_t[r, t, :], x_t[r, t, :], t1[r, :], ALU.add), s.y_ready)

            def fstep(ins, sem_=None):
                if sem_ is None:
                    steps[0] += 1
                    ins.then_inc(s.dve_step, 1)
                    dve.wait_ge(s.dve_step, steps[0])
                else:
                    step(ins, sem_)

            steps = [step.n[s.dve_step.name]]

            def searches(rows, n, k0):
                base = steps[0]
                with dve.Fori(0, PH) as h:
                    search(rows, n, h, h + (k0 + 1), h * N_SEARCH + base)
                steps[0] += PH * N_SEARCH

            dve.wait_ge(s.qry_ready, 1)
            dve.wait_ge(s.sc_ready, 1)
            searches(NB, 0, 0)
            dve.wait_ge(s.sc_ready, 2)
            searches(P, 1, PH)
            dve.wait_ge(s.sel_in, 2 * 16 * NB)
            dots(0, 0, h2sb, sgate)
            finish(NT, 0, s_g2)
            for t in range(NT):
                n = t + 1
                base = steps[0]
                if t + 1 < NT:
                    dve.wait_ge(s.sc_ready, n + 2)
                with dve.Fori(0, PH) as h:
                    for a in range(2):
                        r = h * 2 + (1 + 2 * PH * t + a)
                        dve.wait_ge(s.w_ready, r)
                        copy(gcur[:, :], gate[:, n % 2, bass.ds(h * TOPK + a * SLOTS, SLOTS)]).then_inc(s.gc_ready, 1)
                        dve.wait_ge(s.gc_ready, r)
                        dots(r, (1 + a) % 2, h2[:, t, :], gcur[:, :])
                    if t + 1 < NT:
                        search(P, n + 1, h, h + (PH * (n + 1) + 1), h * N_SEARCH + base)
                if t + 1 < NT:
                    steps[0] += PH * N_SEARCH
                finish(t, n, v_g2)


def layout(a):
    f = lambda v: np.ascontiguousarray(v, dtype=np.float32)
    blocks = lambda w: w.reshape(KT, P, -1, P).transpose(2, 1, 0, 3)
    w_in, w_ada = a["w_in"][0], a["w_ada"][0]
    aq, ak, av, conv, dec, bb, z, g_a, g_b = np.split(w_in, np.cumsum([512, 128, 128, 1536, 4, 4, 512, 1024]), axis=1)
    pair = [h * HD + i for g in range(HG) for h in (g, g + HG) for i in range(HD)]
    ada = blocks(w_ada)
    branch = np.concatenate([a["w_att_out"][0][pair], a["w_delta_out"][0]], axis=0)
    wstream = np.concatenate([ada[0:16], blocks(conv), blocks(aq[:, pair]), blocks(z), blocks(g_a), blocks(g_b), ada[16:48],
                              blocks(branch), blocks(a["w_query"][0])], axis=0)
    tile = lambda v: v.reshape(-1, P).T
    cols = np.concatenate(
        [tile(a["b_ada"][0]), tile(a["g_pre_mix"][0]), tile(a["g_post_mix"][0]), tile(a["g_pre_ffn"][0]), tile(a["g_post_ffn"][0]),
         a["w_conv"][0].reshape(4, CT_N, P).transpose(2, 1, 0).reshape(P, -1), tile(a["delta_norm"][0]),
         np.broadcast_to(a["attn_sinks"][0], (P, 8)), np.broadcast_to(a["a_log"][0], (P, 4)), np.broadcast_to(a["dt_bias"][0], (P, 4)),
         np.tile(a["attn_sinks"][0], 16)[:, None]], axis=1)
    c = np.concatenate([a["c_prompt"], a["c_sample"]], axis=0)
    return {
        "cT": f(c.T.reshape(KT, P, 1 + NB).transpose(1, 0, 2)),
        "x": f(a["x_prompt"][0]), "xs": f(a["x_sample"][:, 0]),
        "wstream": f(wstream), "wnat": f(np.concatenate([ak, av, dec, bb], axis=1).reshape(KT, P, NAT_W).transpose(1, 0, 2)),
        "wout": f(a["w_out"][0].reshape(KT, P, D).transpose(1, 0, 2)),
        "cols": f(cols), "rel": f(a["rel_bias"]),
        "cst": f(a["state_conv"][0].reshape(NB, 3, CT_N, P).transpose(3, 2, 0, 1)),
        "kc": f(a["cache_swa_k"][0].reshape(NB, WIN, P)), "vc": f(a["cache_swa_v"][0].reshape(NB, WIN, P)),
        "sdel": f(a["state_delta"][0].transpose(2, 1, 0, 3)),
        "skt": f(a["sub_keys"][0].transpose(2, 0, 1)),
        "eu": f(a["expert_u"][0]), "ev": f(a["expert_v"][0]),
    }


def constants():
    r, c = np.arange(P)[:, None], np.arange(P)[None, :]
    out = [r == c, r <= c, r > c, np.ones((P, P))]
    for lv in range(7):
        m = 1 << lv
        out.append((r // (2 * m) == c // (2 * m)) & (r % (2 * m) >= m) & (c % (2 * m) < m))
    out.append(np.broadcast_to(np.arange(TOPK), (P, TOPK)))
    out.append(r // TOPK == c[:, 0:NB])
    out.append((c // TOPK == r) & (r < NB))
    onehot = np.zeros((33, 384), np.float32)
    for i in range(384):
        d = 255 - i
        if 0 <= d < WIN:
            big = 16 + int(np.log(np.float32(max(d, 1)) / np.float32(16)) / np.float32(np.log(8.0)) * np.float32(16))
            onehot[d if d < 16 else min(big, 31), i] = 1.0
        else:
            onehot[32, i] = 1.0
    return {"consts": np.concatenate([np.asarray(o, np.float32) for o in out], axis=1), "onehot": onehot}


OUTS = {"yp": (SEQ, D), "ys": (NB, D), "kp": (WIN, P), "vp": (WIN, P), "convp": (P, CT_N, 3), "deltap": (P, 512),
        "ks": (NB, WIN, P), "vs": (NB, WIN, P), "convs": (P, CT_N, NB, 3), "deltas": (P, DH, NB, P)}


def kernel(**inputs):
    import concourse.bacc as bacc
    from concourse.bass_utils import run_bass_kernel_spmd

    nc = bacc.Bacc("TRN2", target_bir_lowering=False, num_devices=1)
    arrays = layout({k: np.asarray(v) for k, v in inputs.items()})
    arrays.update(constants())
    ins = {k: nc.dram_tensor("in_" + k, v.shape, F32, kind="ExternalInput").ap() for k, v in arrays.items()}
    ins["skew"] = nc.dram_tensor("skew", (HQ, P, 384), F32, kind="Internal").ap()
    ins["sidx"] = nc.dram_tensor("sidx", (NB, P), U32, kind="Internal").ap()
    ins["sgate"] = nc.dram_tensor("sgate", (NB, P), F32, kind="Internal").ap()
    outs = {k: nc.dram_tensor("out_" + k, v, F32, kind="ExternalOutput").ap() for k, v in OUTS.items()}
    build(nc, ins, outs)
    got = run_bass_kernel_spmd(nc, [{"in_" + k: v for k, v in arrays.items()}], core_ids=[0]).results[0]
    o = {k: got["out_" + k] for k in OUTS}
    win = lambda v: v.reshape(1, -1, WIN, 2, HD)
    return (o["yp"].reshape(1, SEQ, D), o["ys"].reshape(NB, 1, D), win(o["kp"]), win(o["vp"]),
            np.ascontiguousarray(o["convp"].transpose(2, 1, 0)).reshape(1, 1, 3, CT_N * P),
            np.ascontiguousarray(o["deltap"].reshape(P, DH, P).transpose(1, 0, 2)).reshape(1, 1, DH, P, P),
            win(o["ks"]), win(o["vs"]),
            np.ascontiguousarray(o["convs"].transpose(2, 3, 1, 0)).reshape(1, NB, 3, CT_N * P),
            np.ascontiguousarray(o["deltas"].transpose(2, 1, 0, 3)).reshape(1, NB, DH, P, P))
```

```python
from contextlib import ExitStack
from collections import namedtuple

import numpy as np
import concourse.bass as bass
from concourse import mybir

ALU = mybir.AluOpType
ACT = mybir.ActivationFunctionType
AX = mybir.AxisListType
F32 = mybir.dt.float32
U32 = mybir.dt.uint32

P = 128
D = 1024
KT = D // P
SEQ = 512
NT = SEQ // P
NB = 8
TOK = SEQ + NB
CUT = SEQ // 2
PARTS = ((0, CUT), (CUT, TOK))
HQ, HD = 8, 64
HG = 4
DH = 4
CT_N = 12
WIN = 128
NAT_W = 264
PH = 8
TOPK = 16
N_SEARCH = 27
NKEY = 128
SLOTS = 8
EPS = 1e-6
NEG = -1e30
B_ADA1, B_CONV, B_Q, B_Z, B_GA, B_GB, B_ADA2, B_BR, B_QRY = 16, 12, 4, 4, 8, 8, 32, 8, 16
C_ID, C_LE, C_GT, C_ONE, C_LVL, C_IOTA, C_TK, C_KT = 0, 128, 256, 384, 512, 1408, 1424, 1432
C_W = 1560
K_BADA, K_GPM, K_GQM, K_GPF, K_GQF, K_CONV, K_DN, K_SINK, K_ALOG, K_DT, K_SINKS = 0, 48, 56, 64, 72, 80, 128, 129, 137, 141, 145
K_W = 146


class Steps:

    def __init__(self, eng, own):
        self.eng, self.own, self.n = eng, own, {}

    def __call__(self, ins, sem=None):
        sem = self.own if sem is None else sem
        ins.then_inc(sem, 1)
        self.n[sem.name] = self.n.get(sem.name, 0) + 1
        self.eng.wait_ge(sem, self.n[sem.name])


class Ring:

    def __init__(self, eng, banks, full, free):
        self.eng, self.banks, self.full, self.free, self.n = eng, banks, full, free, 0

    def to_fill(self):
        if self.n >= len(self.banks):
            self.eng.wait_ge(self.free, self.n - len(self.banks) + 1)
        self.n += 1
        return self.banks[(self.n - 1) % len(self.banks)]

    def to_read(self):
        self.eng.wait_ge(self.full, self.n + 1)
        self.n += 1
        return self.banks[(self.n - 1) % len(self.banks)]


def build(nc, I, O):
    with ExitStack() as ctx:
        def sb(name, shape, dt=F32):
            return ctx.enter_context(nc.sbuf_tensor(name, shape, dt))

        def sem(name):
            return ctx.enter_context(nc.semaphore(name))

        consts = sb("consts", [P, C_W])
        cols = sb("cols", [P, K_W])
        onehot = sb("onehot", [33, 384])
        relx = sb("relx", [33, HQ])
        rels = sb("rels", [33, NB * HQ])
        skt = sb("skt", [P, 2, NKEY])
        cT = sb("cT", [P, KT, 1 + NB])
        adaT = sb("adaT", [P, 6 * KT, 1 + NB])
        small = sb("small", [P, 360])
        zeros = sb("zeros", [P, P])
        bext = sb("bext", [HQ, 384])
        delta = sb("delta", [P, 512])
        cpo = sb("cpo", [P, CT_N, 3])
        arena = sb("arena", [P, 48480])
        ident, le, gt, ones = (consts[:, c:c + P] for c in (C_ID, C_LE, C_GT, C_ONE))

        X0, HT0, WB0, CT0, KV0, QT0, Z0, GA0, GB0, R0, E0 = (
            0, 5120, 9280, 13376, 19616, 23712, 25792, 27872, 32032, 36192, 44384)

        def at(lo, *shape):
            v = arena[:, lo:lo + int(np.prod(shape))]
            if len(shape) == 2:
                v = v.rearrange("p (a b) -> p a b", b=shape[1])
            if len(shape) == 3:
                v = v.rearrange("p (a b c) -> p a b c", b=shape[1], c=shape[2])
            return v

        x_t = at(X0, NT + 1, D)
        hT = at(HT0, KT, TOK)
        wb = at(WB0, 4, D)
        ct = at(CT0, CT_N, TOK)
        qT = at(QT0, 4, TOK)
        zT = at(Z0, DH, TOK)
        gaT, gbT = at(GA0, KT, TOK), at(GB0, KT, TOK)
        junk = at(GA0, D)
        rnb = at(R0, 2, TOK)
        bias = at(R0, HQ, 256)
        wnat = at(R0 + 2048, KT, NAT_W)
        prob = at(R0 + 2048, HQ, 256)
        sqb = at(R0 + 4160, 2, TOK)
        probT = at(R0 + 4096, 2 * HQ, P)
        ubuf = at(R0 + 6144, 2, 547)
        keyc, valc = at(R0 + 6144, NB, P), at(R0 + 7168, NB, P)
        cst, cso = (at(E0 + 1832 + i, CT_N * NB, 3).rearrange("p (m b) i -> p m b i", b=NB) for i in (0, 288))
        nat = at(E0, NT + 1, NAT_W)
        kT = at(E0 + 1320, SEQ)
        attT = qT
        odT = at(HT0 + 4 * TOK, DH, TOK)
        kdec, vb = at(KV0, NT, 512), at(KV0 + 2048, NT, 512)
        sdel = at(X0, DH, NB, P)
        mgt = at(X0 + 4096, 2, 512)
        Lc, Wc, Tc = (at(R0 + 2048 * i, NT, 512) for i in range(3))
        Lm, A2 = at(R0 + 6144, NT, 512), at(E0 + 1832, NT, 512)
        ATc = at(CT0 + 8 * TOK, NT, 512)
        E1, E2 = at(HT0, 2, 512), at(HT0 + 1024, 2, 512)
        vdiag = at(R0, NB, P)
        wout = at(CT0, KT, D)
        v_g1, v_a2, v_s2 = (at(R0 + D * i, D) for i in (0, 1, 2))
        s_g1, s_a2, s_s2 = (at(R0 + D * i, D) for i in (3, 4, 5))
        v_g2, s_g2 = at(R0 + 6144, D), at(R0 + 7168, D)
        t1, t2 = at(E0, D), at(E0 + D, D)
        h2 = at(HT0, NT, D)
        h2s = at(E0 + 2 * D, D)
        h2T = [at(GB0, KT, CUT), at(GB0 + KT * CUT, KT, TOK - CUT)]
        Q0 = QT0 - 64
        qryT = [at(Q0, 2 * PH, CUT), at(Q0, 2 * PH, TOK - CUT)]
        uring = [at(CT0 + D * j, D) for j in range(SLOTS)]
        vring = [at(GA0 + D * j, D) for j in range(4)] + [at(R0 + D * j, D) for j in range(4)]
        sc = [at(R0 + 4 * D, 2 * PH * NKEY), at(GB0, 2 * PH * NKEY)]
        diag, h2sb = at(WB0, SLOTS, P), at(WB0 + D, D)

        class Lane:

            def __init__(self, lo, lo2, lo3):
                self.s_in, self.s_out = at(lo, 2, NKEY), at(lo + 256, 2, NKEY)
                self.sv, self.si = at(lo + 512, 2, TOPK), at(lo + 544, 2, TOPK).bitcast(U32)
                self.sif, self.pf, self.ee = at(lo + 576, 2, TOPK), at(lo + 608, 2, TOPK), at(lo + 640, 2, TOPK)
                self.pint = at(lo + 672, 2, TOPK).bitcast(U32)
                self.best, self.pos = at(lo + 704, TOPK), at(lo + 720, TOPK).bitcast(U32)
                self.gexp, self.ef = at(lo + 736, TOPK), at(lo + 752, TOPK)
                self.cand, self.cand2 = at(lo2, TOPK * TOPK), at(lo2 + 256, TOPK * TOPK)
                self.hit = at(lo2 + 512, 2, TOPK, TOPK)
                self.nbest, self.gsum = at(lo3, 1), at(lo3 + 1, 1)

        F1, F2, F3 = CT0 + 8 * D, E0 + 3 * D, HT0 + 4 * D
        lanes = [Lane(F1, F1 + 768, F3), Lane(WB0 + 2 * D, WB0 + 3 * D, F3 + 2)]
        gate, eidx = at(F2, 2, PH * TOPK), at(F2 + 256, 2, PH * TOPK).bitcast(U32)
        sgate, sidx = at(F3 + 4, SLOTS), at(F3 + 12, SLOTS).bitcast(U32)

        def sm(lo, n):
            return small[:, lo:lo + n]
        ssx, rstd, eps, eps128 = sm(0, 8), sm(8, 8), sm(16, 1), sm(17, 1)
        mx8, nm8, sm8, es8 = sm(18, 8), sm(26, 8), sm(34, 8), sm(42, 8)
        gg = sm(50, 20).rearrange("p (t h) -> p t h", h=DH)
        beta = sm(70, 20).rearrange("p (t h) -> p t h", h=DH)
        gtmp, gtmp2 = (sm(a, 20).rearrange("p (t h) -> p t h", h=DH) for a in (90, 110))
        ealog = sm(130, 4)
        ex = sm(134, 48)
        nbeg = sm(182, 16)
        rms4, rms4r = sm(198, 4), sm(202, 4)
        lt64 = sm(206, 64)
        act8 = sm(270, 16).rearrange("p (a j) -> p a j", j=SLOTS)
        w8 = sm(286, 16).rearrange("p (a j) -> p a j", j=SLOTS)
        cur = sm(302, 16).bitcast(U32).rearrange("p (a j) -> p a j", j=SLOTS)
        svv = sm(318, 32)
        gcur = sm(350, 8)
        kn8, vn8 = at(R0 + 2048, 512)[0:NB], at(R0 + 2560, 512)[0:NB]
        sdv = [at(E0 + 1832 + 32 * i, 32) for i in range(13)]

        dbank = [ctx.enter_context(nc.psum_tensor(f"dbank{i}", [P, 512], F32)) for i in range(4)]
        abank = [ctx.enter_context(nc.psum_tensor(f"abank{i}", [P, 512], F32)) for i in range(2)]
        fsum = [[ctx.enter_context(nc.psum_tensor(f"fsum{i}", [P, 512], F32)) for i in range(2)], dbank[0:2]]

        names = """dring_full dring_free aring_full aring_free w_used consts_in cols_in cT_in x_in wnat_in bias_in
            cst_in keyc_in valc_in sdel_in wout_in xr_in skt_in silu_c ss_ready rms_ready rstd_ready xn_ready hT_ready
            conv_in conv_out silu_out sq_ready rn_ready l2_done nat_ready rels_ready qT_ready kT_ready ext_ready ext_out
            gx_ready beta_ready g_ready nm_ready exp_done prob_ready probT_ready att_done lt_ready kTs_ready
            ex_ready vb_ready mg_ready E_ready L_ready lm_ready a2_ready wt_ready S_ready r_ready vn_ready qs_ready
            o_ready orms_ready on_ready od_done sg_ready sa_ready sp_ready sn_ready vd_ready sd_ready merged_ready dg_ready
            ms_ready mr_ready h2_ready h2T_ready qry_ready h2sb_ready sc_ready best_ready gexp_ready topk_done
            sel_out sel_in gelu_ready w_ready diag_ready gc_ready f_read y_ready
            out_small out_k out_delta out_y dve_turn pool_turn dve_step act_step pool_step""".split()
        s = namedtuple("Semaphores", names)(*(sem(n) for n in names))
        w_full = [sem(f"w_full{i}") for i in range(4)]
        u_in = [sem(f"u_in{i}") for i in range(SLOTS)]
        v_in = [sem(f"v_in{i}") for i in range(SLOTS)]
        u_used = [sem(f"u_used{i}") for i in range(SLOTS)]
        v_used = [sem(f"v_used{i}") for i in range(SLOTS)]

        ROWS = [P] * NT + [NB]
        COL = [t * P for t in range(NT)] + [SEQ]

        def tcols(t):
            return slice(COL[t], COL[t] + ROWS[t])

        def searched(t, h):
            return h * (1 if t < NT - 1 else 2) + PH * t

        def next_heads(t, h):
            if isinstance(h, int) and h == PH - 1:
                return ([], [(t + 1, 0), (NT, 0)], [(t + 1, 0)])[(t < NT - 1) + (t < NT - 2)]
            return [(t, h + 1)] + [(NT, h + 1)] * (t == NT - 1)

        N_FIRST = B_ADA1 + B_CONV + B_Q + B_Z + B_GA + B_GB + B_ADA2 + B_BR + B_QRY
        block = ctx.enter_context(nc.Block())

        @block.sync
        def _(sp):
            for n in range(N_FIRST):
                if n >= 4:
                    sp.wait_ge(s.w_used, n - 3)
                if n == N_FIRST - B_QRY:
                    sp.wait_ge(s.sd_ready, 1)
                    sp.dma_start(wout, I["wout"]).then_inc(s.wout_in, 16)
                sp.dma_start(wb[:, n % 4, :], I["wstream"][n]).then_inc(w_full[n % 4], 16)
            for m in range(B_QRY):
                sp.wait_ge(s.w_used, N_FIRST - 1 + m)
                sp.dma_start(wb[:, 2 + m % 2, :], I["wstream"][N_FIRST - B_QRY + m]).then_inc(w_full[2 + m % 2], 16)
            for t in range(NT + 1):
                if t == NT - 1:
                    sp.wait_ge(s.topk_done, PH * (NT + 1))
                    for src, tmp in ((eidx, "sidx"), (gate, "sgate")):
                        sp.dma_start(I[tmp], src[0:NB, NT % 2, :]).then_inc(s.sel_out, 16)
                    sp.wait_ge(s.sel_out, 32)
                    for dst, tmp in ((sidx, "sidx"), (sgate, "sgate")):
                        for b in range(NB):
                            sp.dma_start(dst[b * TOPK:(b + 1) * TOPK, :],
                                           I[tmp][b, :].rearrange("(h k) -> k h", k=TOPK), allow_slow_non_contiguous=True).then_inc(s.sel_in, 16)
                sp.wait_ge(s.y_ready, t + 1)
                out = O["yp"][t * P:(t + 1) * P, :] if t < NT else O["ys"]
                sp.dma_start(out, x_t[0:ROWS[t], t, :]).then_inc(s.out_y, 16)
            sp.wait_ge(s.out_y, 16 * (NT + 1))

        @block.gpsimd
        def _(pool):
            step = Steps(pool, s.pool_step)
            pool.dma_start(cT[:, :, :], I["cT"]).then_inc(s.cT_in, 16)
            pool.dma_start(x_t[:, 0:NT, :], I["x"].rearrange("(t p) d -> p t d", p=P)).then_inc(s.x_in, 16)
            pool.dma_start(x_t[0:NB, NT, :], I["xs"]).then_inc(s.x_in, 16)
            pool.dma_start(consts[:, :], I["consts"]).then_inc(s.consts_in, 16)
            pool.dma_start(onehot[:, :], I["onehot"]).then_inc(s.consts_in, 16)
            pool.dma_start(cols[:, :], I["cols"]).then_inc(s.cols_in, 16)
            pool.dma_start(relx[0:32, :], I["rel"]).then_inc(s.cols_in, 16)
            pool.dma_start(wnat, I["wnat"]).then_inc(s.wnat_in, 16)
            pool.dma_start(cst, I["cst"]).then_inc(s.cst_in, 16)
            pool.dma_start(skt[:, :, :], I["skt"]).then_inc(s.skt_in, 16)
            pool.wait_ge(s.conv_out, CT_N)
            pool.dma_start(O["convp"], cpo[:, :, :]).then_inc(s.out_small, 16)
            pool.dma_start(O["convs"], cso).then_inc(s.out_small, 16)
            pool.wait_ge(s.nat_ready, NT + 1)
            for c0, cache, win, last in ((0, "kc", "ks", "kp"), (P, "vc", "vs", "vp")):
                pool.dma_start(O[win][:, 0:WIN - 1, :], I[cache][:, 1:WIN, :]).then_inc(s.out_k, 16)
                pool.dma_start(O[win][:, WIN - 1, :], nat[0:NB, NT, c0:c0 + P]).then_inc(s.out_k, 16)
                pool.dma_start(O[last], nat[:, NT - 1, c0:c0 + P]).then_inc(s.out_small, 16)
            pool.wait_ge(s.out_k, 64)
            pool.dma_start(keyc, O["ks"].rearrange("b w c -> w b c")).then_inc(s.keyc_in, 16)
            pool.dma_start(valc, O["vs"].rearrange("b w c -> w b c")).then_inc(s.valc_in, 16)
            pool.wait_ge(s.ext_ready, 1)
            pool.dma_start(I["skew"], bext[:, :].unsqueeze(1).to_broadcast([HQ, P, 384])).then_inc(s.ext_out, 16)
            pool.wait_ge(s.ext_out, 16)
            pool.wait_ge(s.l2_done, 2 * DH)
            pool.dma_start(bias, bass.AP(tensor=I["skew"].tensor, offset=P - 1,
                                         ap=[[383, P], [P * 384, HQ], [1, 256]])).then_inc(s.bias_in, 16)
            pool.wait_ge(s.hT_ready, KT + 1)
            pool.dma_start(sdel, I["sdel"]).then_inc(s.sdel_in, 16)
            pool.wait_ge(s.S_ready, NT + 1)
            pool.dma_start(O["deltap"], delta[:, :]).then_inc(s.out_delta, 16)
            pool.wait_ge(s.sd_ready, 1)
            pool.dma_start(O["deltas"], sdel).then_inc(s.out_delta, 16)
            pool.wait_ge(s.out_delta, 32)
            pool.dma_start(x_t[:, 0:NT, :], I["x"].rearrange("(t p) d -> p t d", p=P)).then_inc(s.xr_in, 16)
            pool.dma_start(x_t[0:NB, NT, :], I["xs"]).then_inc(s.xr_in, 16)
            pool.wait_ge(s.out_small, 64)

            def fetch(r, a, idx):
                later = not (isinstance(r, int) and r == 0)
                if later:
                    for j in range(SLOTS):
                        pool.wait_ge(u_used[j], r)
                pool.tensor_copy(cur[:, a, :], idx).then_inc(s.pool_step, 1)
                pool.wait_ge(s.pool_step, r + 1)
                pool.sem_inc(s.pool_turn, 1)
                for j in range(SLOTS):
                    pool.indirect_dma_start(uring[j], None, I["eu"],
                                            bass.IndirectOffsetOnAxis(cur[:, a, j:j + 1], 0)).then_inc(u_in[j], 16)
                for j in range(SLOTS):
                    if later:
                        pool.wait_ge(v_used[j], r)
                        pool.sem_inc(s.pool_turn, 1)
                    pool.indirect_dma_start(vring[j], None, I["ev"],
                                            bass.IndirectOffsetOnAxis(cur[:, a, j:j + 1], 0)).then_inc(v_in[j], 16)

            pool.wait_ge(s.h2_ready, NT + 1)
            for t in range(NT):
                def head(h):
                    pool.wait_ge(s.topk_done, searched(t, h) + 1)
                    for a in range(2):
                        fetch(h * 2 + (2 * PH * t + a), a, eidx[:, t % 2, bass.ds(h * TOPK + a * SLOTS, SLOTS)])
                if t == 0:
                    head(0)
                with pool.Fori(1 if t == 0 else 0, PH) as h:
                    head(h)
            pool.wait_ge(s.sel_in, 2 * 16 * NB)
            fetch(2 * PH * NT, 0, sidx)

        @block.scalar
        def _(act):
            step = Steps(act, s.act_step)
            ring = Ring(act, abank, s.aring_full, s.aring_free)
            A = act.activation

            def empty(dst, cols_from=slice(0, 512), rows=slice(0, P), func=ACT.Copy, **kw):
                b = ring.to_read()
                src = b[rows, cols_from]
                if len(dst.shape) == 3:
                    src = src.rearrange("p (a q) -> p a q", q=dst.shape[2])
                step(A(dst, src, func, **kw), s.aring_free)

            act.wait_ge(s.cT_in, 16)
            step(A(cT[:, :, :], cT[:, :, :], ACT.Silu), s.silu_c)
            for t in range(NT + 1):
                act.wait_ge(s.ss_ready, t + 1)
                step(A(rstd[0:ROWS[t], t:t + 1], ssx[0:ROWS[t], t:t + 1], ACT.Sqrt, bias=eps[0:ROWS[t], :], scale=1.0 / D), s.rms_ready)
            for t in range(NT + 1):
                act.wait_ge(s.rstd_ready, t + 1)
                step(A(x_t[0:ROWS[t], t, :], x_t[0:ROWS[t], t, :], ACT.Copy, scale=rstd[0:ROWS[t], t:t + 1]), s.xn_ready)
            for m in range(CT_N + 1):
                if m < CT_N:
                    u = ubuf[:, m % 2, :]
                    if m >= 2:
                        act.wait_ge(s.conv_out, m - 1)
                    if m == 0:
                        act.wait_ge(s.dve_step, 1)
                    empty(u[:, 3:3 + CUT], slice(0, CUT))
                    b = ring.to_read()
                    step(A(u[:, 3 + CUT:3 + SEQ], b[:, 0:SEQ - CUT], ACT.Copy))
                    step(A(u[:, 515:547].rearrange("p (b i) -> p b i", i=4)[:, :, 3], b[:, SEQ - CUT:TOK - CUT], ACT.Copy), s.aring_free)
                    act.sem_inc(s.conv_in, 1)
                if m >= 1:
                    act.wait_ge(s.conv_out, m)
                    step(A(ct[:, m - 1, :], ct[:, m - 1, :], ACT.Silu), s.silu_out)
            for t in range(NT + 1):
                empty(nat[0:ROWS[t], t, :], slice(0, NAT_W), slice(0, ROWS[t]))
                act.sem_inc(s.nat_ready, 1)
            for m in range(B_Q):
                for lo, hi in PARTS:
                    empty(qT[:, m, lo:hi], slice(0, hi - lo))
            act.sem_inc(s.qT_ready, 1)
            empty(kT)
            act.sem_inc(s.kT_ready, 1)
            empty(bext[:, :], slice(0, 384), slice(0, HQ))
            act.sem_inc(s.ext_ready, 1)
            gate_at = [0]

            def gates(n):
                for m in range(gate_at[0], gate_at[0] + n):
                    dst = zT[:, m, :] if m < B_Z else (gaT[:, m - B_Z, :] if m < B_Z + B_GA else gbT[:, m - B_Z - B_GA, :])
                    for lo, hi in PARTS:
                        empty(dst[:, lo:hi], slice(0, hi - lo), func=ACT.Silu if m < B_Z else ACT.Sigmoid)
                gate_at[0] += n

            for m in range(2 * DH):
                if m >= 2:
                    act.wait_ge(s.l2_done, m - 1)
                for lo, hi in PARTS:
                    empty(rnb[:, m % 2, lo:hi], slice(0, hi - lo), func=ACT.Sqrt,
                          bias=eps128 if m < DH else eps, scale=float(P) if m < DH else 1.0)
                act.sem_inc(s.rn_ready, 1)
                gates(1)
            act.wait_ge(s.cols_in, 32)
            step(A(ealog, cols[:, K_ALOG:K_ALOG + 4], ACT.Exp))
            act.wait_ge(s.gx_ready, 1)
            step(A(gtmp2, gtmp, ACT.Abs))
            step(A(gtmp2, gtmp2, ACT.Exp, scale=-1.0))
            step(A(gtmp2, gtmp2, ACT.Ln, bias=ones[:, 0:1]))
            step(A(beta, nat[:, :, 260:264], ACT.Sigmoid), s.beta_ready)
            for blk in range(NT):
                lo = 0 if blk else P
                gates(2)
                act.wait_ge(s.nm_ready, blk + 1)
                for h in range(HQ):
                    step(A(prob[:, h, lo:256], prob[:, h, lo:256], ACT.Exp, bias=nm8[:, h:h + 1], accum_out=sm8[:, h:h + 1]))
                step(A(es8, es8, ACT.Exp), s.exp_done)
                for i in range(2 if blk == 0 else 4):
                    empty(probT[:, 4 * i:4 * i + 4, :])
                act.sem_inc(s.probT_ready, 1)
                gates(1)
                empty(attT[:, :, blk * P:(blk + 1) * P])
            for i in range(2):
                empty(probT[:, 4 * i:4 * i + 4, :])
            act.sem_inc(s.kTs_ready, 1)
            act.wait_ge(s.nm_ready, NT + 1)
            step(A(prob[0:64, 0, 0:P], prob[0:64, 0, 0:P], ACT.Exp, bias=nm8[0:64, 0:1], accum_out=sm8[0:64, 0:1]))
            step(A(es8[0:64, 0:1], es8[0:64, 0:1], ACT.Exp), s.exp_done)
            b = ring.to_read()
            step(A(attT[:, :, SEQ:TOK], b[:, 0:32].rearrange("p (b g) -> p g b", g=HG), ACT.Copy), s.aring_free)
            act.sem_inc(s.att_done, 1)
            empty(ex, slice(0, 48), func=ACT.Exp)
            act.sem_inc(s.ex_ready, 1)
            for ch in range(NT):
                if ch >= 2:
                    act.wait_ge(s.L_ready, ch - 1)
                empty(E1[:, ch % 2, :], func=ACT.Exp)
                empty(E2[:, ch % 2, :], func=ACT.Exp)
                act.sem_inc(s.E_ready, 1)
            act.wait_ge(s.out_small, 64)
            for lv in range(1, 7):
                for ch in range(NT):
                    empty(A2[:, ch, :])
                    act.sem_inc(s.a2_ready, 1)
            for ch in range(NT):
                empty(E1[:, 1, :])
                act.sem_inc(s.qs_ready, 1)
                empty(E2[:, 0, :])
                act.sem_inc(s.vn_ready, 1)
                act.wait_ge(s.o_ready, ch + 1)
                step(A(rms4, rms4, ACT.Sqrt, bias=eps, scale=1.0 / P), s.orms_ready)
            b = ring.to_read()
            step(A(sdv[0], b[:, 0:32], ACT.Exp))
            step(A(sdv[1], b[:, 32:64], ACT.Copy), s.aring_free)
            act.sem_inc(s.sa_ready, 1)
            empty(sdv[2], slice(0, 32), func=ACT.Sqrt, bias=eps, scale=1.0 / P)
            act.sem_inc(s.sa_ready, 1)

            def norm(i):
                t = i // 2 if i < 2 * (NT + 1) else i - 2 * (NT + 1)
                r = slice(0, ROWS[t])
                act.wait_ge(s.ms_ready, i + 1)
                step(A(rstd[r, 0:1], ssx[r, 0:1], ACT.Sqrt, bias=eps[r, :], scale=1.0 / D), s.mr_ready)

            def transposed(t):
                for g in range(2):
                    empty(h2T[t // 2][:, 4 * g:4 * g + 4, (t % 2) * P:(t % 2 + 1) * P])

            def scores(n):
                rows = ROWS[n]
                if n >= 2:
                    act.wait_ge(s.topk_done, PH * (n - 1))
                for g in range(4):
                    empty(sc[n % 2][0:rows, g * 512:(g + 1) * 512], rows=slice(0, rows))
                act.sem_inc(s.sc_ready, 1)

            def best_exp(count, jobs):
                for i, (n, h) in enumerate(jobs):
                    r, lane = slice(0, ROWS[n]), lanes[i]
                    act.wait_ge(s.best_ready, count + (i + 1))
                    A(lane.gexp[r, :], lane.best[r, :], ACT.Exp, bias=lane.nbest[r, :],
                      accum_out=lane.gsum[r, :]).then_inc(s.gexp_ready, 1)

            for i in range(4):
                norm(i)
            transposed(0)
            transposed(1)
            act.sem_inc(s.h2T_ready, 1)
            for m in range(B_QRY):
                if m % 3 == 0:
                    norm(4 + m // 3)
                empty(qryT[0][:, m, :], slice(0, CUT))
            act.sem_inc(s.qry_ready, 1)
            act.wait_ge(s.h2_ready, NT + 1)
            scores(0)
            scores(1)
            best_exp(0, [(0, 0)])
            transposed(2)
            transposed(3)
            empty(h2T[1][:, :, SEQ - CUT:], slice(0, KT * NB))
            act.sem_inc(s.h2T_ready, 1)
            late, late_banks = ring.n, [ring.banks[(ring.n + i) % 2] for i in range(2)]

            def query(h, a):
                act.wait_ge(s.aring_full, h * 2 + (late + a + 1))
                A(qryT[1][:, bass.ds(h * 2 + a, 1), :], late_banks[a][:, 0:TOK - CUT].unsqueeze(1), ACT.Copy).then_inc(s.aring_free, 1)

            def weigh(r, a, base):
                act.wait_ge(u_used[SLOTS - 1], r + 1)
                A(act8[:, a, :], act8[:, a, :], ACT.Gelu).then_inc(s.gelu_ready, 1)
                act.wait_ge(s.w_ready, r + 1)
                for j in range(SLOTS):
                    if not (isinstance(r, int) and r == 0):
                        act.wait_ge(v_used[j], r)
                    A(diag[:, j, 0:base.shape[1]], base, ACT.Copy, scale=w8[:, a, j:j + 1]).then_inc(s.diag_ready, 1)

            for t in range(NT):
                if 0 < t < NT - 1:
                    scores(t + 1)

                def head(h):
                    weigh(h * 2 + 2 * PH * t, 0, ident)
                    if t == 0:
                        query(h, 0)
                    if next_heads(t, h):
                        best_exp(searched(t, h) + (1 if t < NT - 1 else 2), next_heads(t, h))
                    if t and isinstance(h, int) and h == 0:
                        norm(2 * (NT + 1) + t - 1)
                    weigh(h * 2 + (2 * PH * t + 1), 1, ident)
                    if t == 0:
                        query(h, 1)
                head(0)
                with act.Fori(1, PH - 1) as h:
                    head(h)
                if t == NT - 2:
                    scores(NT)
                head(PH - 1)
                if t == 0:
                    ring.n += B_QRY
                    step.n[s.aring_free.name] += B_QRY
                    act.wait_ge(s.aring_free, step.n[s.aring_free.name])
                    act.sem_inc(s.qry_ready, 1)
            weigh(2 * PH * NT, 0, consts[:, C_TK:C_TK + NB])
            norm(3 * (NT + 1) - 2)
            norm(3 * (NT + 1) - 1)

        @block.tensor
        def _(pe):
            dring = Ring(pe, dbank, s.dring_full, s.dring_free)
            aring = Ring(pe, abank, s.aring_full, s.aring_free)
            stream = [0]

            def mm(out, lhsT, rhs, first=True, last=True):
                return pe.matmul(out, lhsT, rhs, start=first, stop=last)

            def weights():
                n = stream[0]
                pe.wait_ge(w_full[n % 4], 16 * (n // 4 + 1))
                stream[0] += 1
                return wb[:, n % 4, :].rearrange("p (k m) -> p k m", m=P)

            def block_before_used(ins):
                if stream[0] > 1:
                    ins.then_inc(s.w_used, 1)

            def project(x, parts=PARTS):
                w = weights()
                for i, (lo, hi) in enumerate(parts):
                    b = aring.to_fill()
                    for k in range(KT):
                        last = mm(b[:, 0:hi - lo], w[:, k, :], x[:, k, lo:hi], k == 0, k == KT - 1)
                        if i == 0 and k == 0:
                            block_before_used(last)
                    last.then_inc(s.aring_full, 1)

            def modulation(tiles):
                for g in range(tiles // KT):
                    b = dring.to_fill()
                    for j in range(KT):
                        w = weights()
                        for k in range(KT):
                            last = mm(b[:, 9 * j:9 * j + 9], w[:, k, :], cT[:, k, :], k == 0, k == KT - 1)
                            if k == 0:
                                block_before_used(last)
                    last.then_inc(s.dring_full, 1)

            pe.wait_ge(s.silu_c, 1)
            modulation(B_ADA1)
            pe.wait_ge(s.consts_in, 32)
            pe.wait_ge(s.xn_ready, NT + 1)
            for k in range(KT):
                b = dring.to_fill()
                for t in range(NT):
                    last = pe.transpose(b[:, t * P:(t + 1) * P], x_t[:, t, k * P:(k + 1) * P], ident)
                last.then_inc(s.dring_full, 1)
            b = dring.to_fill()
            for k in range(KT):
                last = pe.transpose(b[:, k * NB:(k + 1) * NB], x_t[0:NB, NT, k * P:(k + 1) * P], consts[0:NB, 0:NB])
            last.then_inc(s.dring_full, 1)
            pe.wait_ge(s.hT_ready, KT + 1)
            for m in range(CT_N):
                project(hT)
            pe.wait_ge(s.wnat_in, 16)
            for t in range(NT + 1):
                b = aring.to_fill()
                for k in range(KT):
                    last = mm(b[0:ROWS[t], 0:NAT_W], hT[:, k, tcols(t)], wnat[:, k, :], k == 0, k == KT - 1)
                last.then_inc(s.aring_full, 1)
            for m in range(B_Q):
                project(hT)
            pe.wait_ge(s.nat_ready, NT)
            b = aring.to_fill()
            for t in range(NT):
                last = pe.transpose(b[:, t * P:(t + 1) * P], nat[:, t, 0:P], ident)
            last.then_inc(s.aring_full, 1)
            pe.wait_ge(s.rels_ready, 1)
            b = aring.to_fill()
            mm(b[0:HQ, 0:384], relx[:, :], onehot[:, :]).then_inc(s.aring_full, 1)
            for m in range(2 * DH):
                pe.wait_ge(s.sq_ready, m + 1)
                for lo, hi in PARTS:
                    b = aring.to_fill()
                    mm(b[:, 0:hi - lo], ones, sqb[:, m % 2, lo:hi]).then_inc(s.aring_full, 1)
                project(hT)
            pe.wait_ge(s.qT_ready, 1)
            pe.wait_ge(s.kT_ready, 1)
            for blk in range(NT):
                lo = 0 if blk else P
                for i in range(HQ // 2):
                    b = dring.to_fill()
                    for e in range(2):
                        h = 2 * i + e
                        g, rows = h % HG, slice(64 * (h // HG), 64 * (h // HG) + 64)
                        last = mm(b[:, e * 256 + lo:e * 256 + 256], qT[rows, g, blk * P:(blk + 1) * P],
                                  kT[rows, (blk - 1) * P + lo:(blk + 1) * P])
                    last.then_inc(s.dring_full, 1)
                project(hT)
                project(hT)
                pe.wait_ge(s.prob_ready, blk + 1)
                parts = [(h, c) for h in range(HQ) for c in ((1,) if blk == 0 else (0, 1))]
                for i in range(len(parts) // 4):
                    b = aring.to_fill()
                    for e, (h, c) in enumerate(parts[4 * i:4 * i + 4]):
                        last = pe.transpose(b[:, e * P:(e + 1) * P], prob[:, h, c * P:(c + 1) * P], ident)
                    last.then_inc(s.aring_full, 1)
                project(hT)
                pe.wait_ge(s.probT_ready, blk + 1)
                b = aring.to_fill()
                for i, (h, c) in enumerate(parts):
                    half = 64 * (h // HG)
                    last = mm(b[half:half + 64, (h % HG) * P:(h % HG + 1) * P],
                              nat[:, blk - 1 + c, P + half:P + half + 64], probT[:, i, :],
                              blk == 0 or c == 0, c == 1)
                last.then_inc(s.aring_full, 1)
            modulation(KT)
            pe.wait_ge(s.keyc_in, 16)
            for i in range(2):
                b = aring.to_fill()
                for e in range(4):
                    last = pe.transpose(b[:, e * P:(e + 1) * P], keyc[:, 4 * i + e, :], ident)
                last.then_inc(s.aring_full, 1)
            pe.wait_ge(s.kTs_ready, 1)
            for kv in range(2):
                b = dring.to_fill()
                rows = slice(64 * kv, 64 * kv + 64)
                for q in range(NB):
                    last = mm(b[:, q * HG:(q + 1) * HG], probT[rows, q, :], qT[rows, :, SEQ + q])
                last.then_inc(s.dring_full, 1)
            b = dring.to_fill()
            mm(b[0:64, 0:P], rels[:, :], onehot[:, P:2 * P]).then_inc(s.dring_full, 1)
            pe.wait_ge(s.lt_ready, 1)
            b = dring.to_fill()
            pe.transpose(b[0:64, 0:P], lt64, ident).then_inc(s.dring_full, 1)
            pe.wait_ge(s.prob_ready, NT + 1)
            b = dring.to_fill()
            pe.transpose(b[:, 0:64], prob[0:64, 0, 0:P], consts[0:64, 0:64]).then_inc(s.dring_full, 1)
            pe.wait_ge(s.lt_ready, 2)
            pe.wait_ge(s.valc_in, 16)
            b = aring.to_fill()
            for q in range(NB):
                for kv in range(2):
                    last = mm(b[64 * kv:64 * kv + 64, q * HG:(q + 1) * HG], valc[:, q, 64 * kv:64 * kv + 64],
                              lt64[:, q * HQ + kv * HG:q * HQ + kv * HG + HG])
            last.then_inc(s.aring_full, 1)
            pe.wait_ge(s.g_ready, 1)
            b = aring.to_fill()
            for i, tri in enumerate((le, gt, ones)):
                last = mm(b[:, 16 * i:16 * i + 16], tri, gg[:, 0:NT, :])
            last.then_inc(s.aring_full, 1)
            pe.wait_ge(s.l2_done, 2 * DH)
            for ch in range(NT):
                for first in (DH, 2 * DH):
                    b = dring.to_fill()
                    for h in range(DH):
                        last = pe.transpose(b[:, h * P:(h + 1) * P], ct[:, first + h, ch * P:(ch + 1) * P], ident)
                    last.then_inc(s.dring_full, 1)
            for ch in range(NT):
                here = slice(ch * P, (ch + 1) * P)
                pe.wait_ge(s.mg_ready, ch + 1)
                b = aring.to_fill()
                mm(b[:, :], le, mgt[:, ch % 2, :]).then_inc(s.aring_full, 1)
                b = aring.to_fill()
                for h in range(DH):
                    last = mm(b[:, h * P:(h + 1) * P], mgt[:, ch % 2, h * P:(h + 1) * P], le)
                last.then_inc(s.aring_full, 1)
                for right in (DH, 0):
                    b = dring.to_fill()
                    for h in range(DH):
                        last = mm(b[:, h * P:(h + 1) * P], ct[:, DH + h, here], ct[:, right + h, here])
                    last.then_inc(s.dring_full, 1)
            for ch in range(NT):
                pe.wait_ge(s.lm_ready, ch + 1)
                b = dring.to_fill()
                for h in range(DH):
                    last = pe.transpose(b[:, h * P:(h + 1) * P], Lm[:, ch, h * P:(h + 1) * P], ident)
                last.then_inc(s.dring_full, 1)
            for lv in range(1, 7):
                for ch in range(NT):
                    pe.wait_ge(s.lm_ready, NT * lv + ch + 1)
                    pe.wait_ge(s.wt_ready, NT * (lv - 1) + ch + 1)
                    b = aring.to_fill()
                    for h in range(DH):
                        hs = slice(h * P, (h + 1) * P)
                        last = mm(b[:, hs], Lm[:, ch, hs], Wc[:, ch, hs])
                    last.then_inc(s.aring_full, 1)
                for ch in range(NT):
                    pe.wait_ge(s.a2_ready, NT * (lv - 1) + ch + 1)
                    for left, right in ((Tc, A2), (A2, Tc)) if lv < 6 else ((Tc, A2),):
                        b = dring.to_fill()
                        for h in range(DH):
                            hs = slice(h * P, (h + 1) * P)
                            last = mm(b[:, hs], left[:, ch, hs], right[:, ch, hs])
                        last.then_inc(s.dring_full, 1)
            pe.wait_ge(s.wt_ready, NT * 7)
            for ch in range(NT):
                def per_head(ring, full, left, right):
                    b = ring.to_fill()
                    for h in range(DH):
                        last = mm(b[:, h * P:(h + 1) * P], left(h), right[:, h * P:(h + 1) * P])
                    last.then_inc(full, 1)
                here = slice(ch * P, (ch + 1) * P)
                pe.wait_ge(s.S_ready, ch + 1)
                per_head(dring, s.dring_full, lambda h: ct[:, DH + h, here], delta)
                per_head(aring, s.aring_full, lambda h: ct[:, h, here], delta)
                if ch < NT - 1:
                    modulation(KT)
                pe.wait_ge(s.r_ready, ch + 1)
                per_head(aring, s.aring_full, lambda h: Wc[:, ch, h * P:(h + 1) * P], E1[:, 0, :])
                pe.wait_ge(s.vn_ready, ch + 1)
                per_head(dring, s.dring_full, lambda h: kdec[:, ch, h * P:(h + 1) * P], E2[:, 0, :])
                per_head(dring, s.dring_full, lambda h: ATc[:, ch, h * P:(h + 1) * P], E2[:, 0, :])
                pe.wait_ge(s.on_ready, ch + 1)
                b = dring.to_fill()
                for h in range(DH):
                    last = pe.transpose(b[:, h * P:(h + 1) * P], E2[:, 1, h * P:(h + 1) * P], ident)
                last.then_inc(s.dring_full, 1)
            pe.wait_ge(s.sg_ready, 1)
            b = aring.to_fill()
            mm(b[:, 0:64], consts[0:NB, C_ONE:C_ONE + P], at(E0 + 1832 + 32 * 3, 64)[0:NB, :]).then_inc(s.aring_full, 1)
            pe.wait_ge(s.sdel_in, 16)
            b = dring.to_fill()
            for h in range(DH):
                for q in range(NB):
                    c0 = 2 * (h * NB + q)
                    last = mm(b[:, c0:c0 + 2], sdel[:, h, q, :], ct[:, h:h + DH + 1:DH, SEQ + q])
            last.then_inc(s.dring_full, 1)
            pe.wait_ge(s.sp_ready, 1)
            b = dring.to_fill()
            mm(b[:, 0:32], ones, sdv[5]).then_inc(s.dring_full, 1)
            b = dring.to_fill()
            for h in range(DH):
                last = pe.transpose(b[0:NB, h * P:(h + 1) * P], sdv[12][:, h * NB:(h + 1) * NB], ident)
            last.then_inc(s.dring_full, 1)
            pe.wait_ge(s.sn_ready, 1)
            b = dring.to_fill()
            for h in range(DH):
                last = pe.transpose(b[0:NB, h * P:(h + 1) * P], sdv[8][:, h * NB:(h + 1) * NB], ident)
            last.then_inc(s.dring_full, 1)
            pe.wait_ge(s.sn_ready, 2)
            b = aring.to_fill()
            mm(b[:, 0:32], ones, sdv[10]).then_inc(s.aring_full, 1)
            for h in range(DH):
                pe.wait_ge(s.vd_ready, h + 1)
                for g in range(2):
                    b = dring.to_fill()
                    mm(b[:, :], kn8[:, h * P:(h + 1) * P], at(R0 + 1024 * (h % 2), 1024)[0:NB, g * 512:(g + 1) * 512]).then_inc(s.dring_full, 1)
            pe.wait_ge(s.att_done, 1)
            pe.wait_ge(s.od_done, NT + 1)
            for m in range(B_BR):
                w = weights()
                for lo, hi in PARTS:
                    for k0, x in ((0, attT), (4, odT)):
                        b = dring.to_fill()
                        for k in range(4):
                            last = mm(b[:, 0:hi - lo], w[:, k0 + k, :], x[:, k, lo:hi], k == 0, k == 3)
                            if lo == 0 and k0 == 0 and k == 0:
                                block_before_used(last)
                        last.then_inc(s.dring_full, 1)
            for i, v in enumerate((2, 4, 3, 5)):
                pe.wait_ge(s.dg_ready, i + 1)
                for g in range(2):
                    b = dring.to_fill()
                    mm(b[:, :], ones, t1[:, g * 512:(g + 1) * 512]).then_inc(s.dring_full, 1)
                for g in range(2):
                    b = dring.to_fill()
                    for j in range(4):
                        last = pe.transpose(b[0:NB, j * P:(j + 1) * P], adaT[:, v * KT + 4 * g + j, 1:9], ident)
                    last.then_inc(s.dring_full, 1)
            def mix(t):
                for g in range(2):
                    b = dring.to_fill()
                    for k in range(KT):
                        last = mm(b[0:ROWS[t], :], gaT[:, k, tcols(t)], wout[:, k, g * 512:(g + 1) * 512], k == 0, k == KT - 1)
                    last.then_inc(s.dring_full, 1)

            def transposed(t):
                pe.wait_ge(s.h2_ready, t + 1)
                for g in range(2):
                    b = aring.to_fill()
                    for j in range(4):
                        last = pe.transpose(b[:, j * P:(j + 1) * P], h2[:, t, (4 * g + j) * P:(4 * g + j + 1) * P], ident)
                    last.then_inc(s.aring_full, 1)

            def scores(n):
                part, lo = (n // 2, (n % 2) * P) if n < NT else (1, SEQ - CUT)
                for g in range(4):
                    b = aring.to_fill()
                    for e in range(4):
                        m = 4 * g + e
                        last = mm(b[0:ROWS[n], e * P:(e + 1) * P], qryT[part][:, m, lo:lo + ROWS[n]], skt[:, m % 2, :])
                    last.then_inc(s.aring_full, 1)

            pe.wait_ge(s.merged_ready, KT)
            pe.wait_ge(s.wout_in, 16)
            for t in range(NT + 1):
                mix(t)
            transposed(0)
            transposed(1)
            pe.wait_ge(s.h2T_ready, 1)
            for m in range(B_QRY):
                project(h2T[0], ((0, CUT),))
            pe.wait_ge(s.skt_in, 16)
            pe.wait_ge(s.qry_ready, 1)
            scores(0)
            scores(1)
            transposed(2)
            transposed(3)
            pe.wait_ge(s.h2_ready, NT + 1)
            b = aring.to_fill()
            for k in range(KT):
                last = pe.transpose(b[:, k * NB:(k + 1) * NB], h2s[0:NB, k * P:(k + 1) * P], consts[0:NB, 0:NB])
            last.then_inc(s.aring_full, 1)
            for g in range(2):
                b = dring.to_fill()
                mm(b[:, :], consts[0:NB, C_KT:C_KT + P], h2s[0:NB, g * 512:(g + 1) * 512]).then_inc(s.dring_full, 1)
            pe.wait_ge(s.h2T_ready, 2)

            late, late_banks = aring.n, [aring.banks[(aring.n + i) % 2] for i in range(2)]

            def query(h, a):
                w = wb[:, 2 + a, :].rearrange("p (k m) -> p k m", m=P)
                pe.wait_ge(w_full[2 + a], h * 16 + 16 * (N_FIRST // 4 + 1))
                pe.wait_ge(s.aring_free, h * 2 + (late + a - 1))
                for k in range(KT):
                    last = mm(late_banks[a][:, 0:TOK - CUT], w[:, k, :], h2T[1][:, k, :], k == 0, k == KT - 1)
                    if k == 0:
                        block_before_used(last)
                last.then_inc(s.aring_full, 1)

            def clear(n):
                if n == 1:
                    pe.wait_ge(s.dring_free, dring.n)
                if n >= 2:
                    pe.wait_ge(s.f_read, n - 1)
                for g in range(2):
                    pe.matmul(fsum[n % 2][g][:, :], zeros[:, :], consts[:, 0:512], start=True, stop=False, skip_group_check=True)

            def add_round(n, r, cols_):
                for j in range(SLOTS):
                    pe.wait_ge(s.diag_ready, r * SLOTS + (j + 1))
                    pe.wait_ge(v_in[j], r * 16 + 16)
                    for g in range(2):
                        last = pe.matmul(fsum[n % 2][g][0:cols_, :], diag[:, j, 0:cols_], vring[j][:, g * 512:(g + 1) * 512],
                                         start=False, stop=False, skip_group_check=True)
                    last.then_inc(v_used[j], 1)

            for t in range(NT):
                if t == 1:
                    pe.wait_ge(s.qry_ready, 2)
                if 0 < t < NT - 1:
                    scores(t + 1)
                clear(t)

                def head(h):
                    for a in range(2):
                        if t == 0:
                            query(h, a)
                        add_round(t, h * 2 + (2 * PH * t + a), P)
                with pe.Fori(0, PH - 1) as h:
                    head(h)
                if t == NT - 2:
                    scores(NT)
                head(PH - 1)
                if t == 0:
                    aring.n += B_QRY
            clear(NT)
            add_round(NT, 2 * PH * NT, NB)

        @block.vector
        def _(dve):
            step = Steps(dve, s.dve_step)
            ring = Ring(dve, dbank, s.dring_full, s.dring_free)
            TT, TS, STT, TTR = dve.tensor_tensor, dve.tensor_scalar, dve.scalar_tensor_tensor, dve.tensor_tensor_reduce
            copy, recip = dve.tensor_copy, dve.reciprocal

            def bc(v, axis, n):
                shape = list(v.shape)
                shape.insert(axis, n)
                return v.unsqueeze(axis).to_broadcast(shape)

            def three(v, q=P):
                return v.rearrange("p (a q) -> p a q", q=q)

            step(dve.memset(ubuf, 0.0))
            step(dve.memset(eps, EPS))
            step(dve.memset(eps128, EPS * P))
            step(dve.memset(nat[:, NT, :], 0.0))
            step(dve.memset(zeros[:, :], 0.0))
            step(dve.memset(relx[32:33, :], NEG))
            dve.wait_ge(s.x_in, 32)
            for t in range(NT + 1):
                r = slice(0, ROWS[t])
                step(TTR(junk[r, :], x_t[r, t, :], x_t[r, t, :], 1.0, 0.0, ALU.mult, ALU.add, ssx[r, t:t + 1]), s.ss_ready)
            for t in range(NT + 1):
                dve.wait_ge(s.rms_ready, t + 1)
                step(recip(rstd[0:ROWS[t], t:t + 1], rstd[0:ROWS[t], t:t + 1]), s.rstd_ready)

            def modulation(v):
                a = adaT[:, v * KT:(v + 1) * KT, :]
                b = ring.to_read()
                step(TT(a, b[:, 0:72].rearrange("p (k c) -> p k c", c=9),
                        bc(cols[:, K_BADA + v * KT:K_BADA + (v + 1) * KT], 2, 9), ALU.add), s.dring_free)
                gain = {1: K_GPM, 2: K_GQM, 4: K_GPF, 5: K_GQF}.get(v)
                if gain is not None:
                    step(STT(a, a, 1.0 if v in (1, 4) else 0.0, bc(cols[:, gain:gain + KT], 2, 9), ALU.add, ALU.mult))

            dve.wait_ge(s.cols_in, 32)
            modulation(0)
            modulation(1)
            for k in range(KT):
                b = ring.to_read()
                step(TS(hT[:, k, 0:SEQ], b[:, :], adaT[:, KT + k, 0:1], adaT[:, k, 0:1], ALU.mult, ALU.add), s.dring_free)
                dve.sem_inc(s.hT_ready, 1)
            b = ring.to_read()
            step(TT(hT[:, :, SEQ:TOK], three(b[:, 0:KT * NB], NB), adaT[:, KT:2 * KT, 1:9], ALU.mult), s.dring_free)
            step(TT(hT[:, :, SEQ:TOK], hT[:, :, SEQ:TOK], adaT[:, 0:KT, 1:9], ALU.add), s.hT_ready)
            step(copy(rels[:, :].rearrange("p (b h) -> p b h", h=HQ), bc(relx[:, :], 1, NB)), s.rels_ready)
            dve.wait_ge(s.cst_in, 16)
            for m in range(CT_N):
                dve.wait_ge(s.conv_in, m + 1)
                u = ubuf[:, m % 2, :]
                us = u[:, 515:547].rearrange("p (b i) -> p b i", i=4)
                step(copy(us[:, :, 0:3], cst[:, m, :, :]))
                step(copy(cpo[:, m, :], u[:, SEQ:SEQ + 3]))
                step(copy(cso[:, m, :, :], us[:, :, 1:4]))
                for i in range(4):
                    w = cols[:, K_CONV + 4 * m + i:K_CONV + 4 * m + i + 1]
                    for out, src in ((ct[:, m, 0:SEQ], u[:, i:i + SEQ]), (ct[:, m, SEQ:TOK], us[:, :, i])):
                        if i == 0:
                            step(TS(out, src, w, None, ALU.mult))
                        elif i < 3 or out.shape[1] == SEQ:
                            step(STT(out, src, w, out, ALU.mult, ALU.add))
                        else:
                            step(STT(out, src, w, out, ALU.mult, ALU.add), s.conv_out)
            for m in range(2 * DH + 1):
                if m < 2 * DH:
                    dve.wait_ge(s.silu_out, m + 1)
                    step(TT(sqb[:, m % 2, :], ct[:, m, :], ct[:, m, :], ALU.mult), s.sq_ready)
                if m >= 1:
                    dve.wait_ge(s.rn_ready, m)
                    r = rnb[:, (m - 1) % 2, :]
                    step(recip(r, r))
                    step(TT(ct[:, m - 1, :], ct[:, m - 1, :], r, ALU.mult), s.l2_done)
            dve.wait_ge(s.nat_ready, NT + 1)
            step(TT(gtmp, nat[:, :, 256:260], bc(cols[:, K_DT:K_DT + 4], 1, NT + 1), ALU.add), s.gx_ready)
            dve.wait_ge(s.beta_ready, 1)
            step(STT(gg, gtmp, 0.0, gtmp2, ALU.max, ALU.add))
            step(STT(gg, gg, -1.0, bc(ealog, 1, NT + 1), ALU.mult, ALU.mult), s.g_ready)
            dve.wait_ge(s.bias_in, 16)
            for blk in range(NT):
                lo = 0 if blk else P
                if blk:
                    dve.wait_ge(s.probT_ready, blk)
                for i in range(HQ // 2):
                    b = ring.to_read()
                    step(STT(prob[:, 2 * i:2 * i + 2, lo:256], three(b[:, :], 256)[:, :, lo:256], HD ** -0.5,
                             bias[:, 2 * i:2 * i + 2, lo:256], ALU.mult, ALU.add), s.dring_free)
                step(dve.tensor_reduce(mx8, prob[:, :, lo:256], AX.X, ALU.max))
                step(TT(mx8, mx8, cols[:, K_SINK:K_SINK + 8], ALU.max))
                step(TT(es8, cols[:, K_SINK:K_SINK + 8], mx8, ALU.subtract))
                step(TS(nm8, mx8, -1.0, None, ALU.mult), s.nm_ready)
                dve.wait_ge(s.exp_done, blk + 1)
                step(TT(sm8, sm8, es8, ALU.add))
                step(recip(sm8, sm8))
                step(TT(prob[:, :, lo:256], prob[:, :, lo:256], bc(sm8, 2, 256 - lo), ALU.mult), s.prob_ready)
            modulation(2)
            dve.wait_ge(s.probT_ready, NT)
            for kv in range(2):
                b = ring.to_read()
                step(TS(lt64.rearrange("p (q v g) -> p q v g", v=2, g=HG)[:, :, kv, :], three(b[:, 0:NB * HG], HG), HD ** -0.5, None, ALU.mult), s.dring_free)
            dve.sem_inc(s.lt_ready, 1)
            q0 = prob[0:64, 0, 0:P]
            b = ring.to_read()
            step(copy(q0, b[0:64, 0:P]), s.dring_free)
            b = ring.to_read()
            step(TT(q0, b[0:64, 0:P], q0, ALU.add), s.dring_free)
            mx, nm, sm_, es, sink = mx8[0:64, 0:1], nm8[0:64, 0:1], sm8[0:64, 0:1], es8[0:64, 0:1], cols[0:64, K_SINKS:K_SINKS + 1]
            step(dve.tensor_reduce(mx, q0, AX.X, ALU.max))
            step(TT(mx, mx, sink, ALU.max))
            step(TT(es, sink, mx, ALU.subtract))
            step(TS(nm, mx, -1.0, None, ALU.mult), s.nm_ready)
            dve.wait_ge(s.exp_done, NT + 1)
            step(TT(sm_, sm_, es, ALU.add))
            step(recip(sm_, sm_))
            step(TS(q0, q0, sm_, None, ALU.mult), s.prob_ready)
            b = ring.to_read()
            step(copy(lt64, b[:, 0:64]), s.dring_free)
            dve.sem_inc(s.lt_ready, 1)
            step(copy(three(svv, NB), ct[:, 2 * DH:3 * DH, SEQ:TOK]))
            dve.wait_ge(s.ex_ready, 1)
            for ch in range(NT):
                b = ring.to_read()
                step(TT(three(kdec[:, ch, :]), three(b[:, :]), bc(ex[:, 16 + 4 * ch:20 + 4 * ch], 2, P), ALU.mult), s.dring_free)
                b = ring.to_read()
                step(TT(three(vb[:, ch, :]), three(b[:, :]), bc(beta[:, ch, :], 2, P), ALU.mult), s.dring_free)
            step(STT(three(nbeg, DH), three(ex[:, 0:16], DH), -1.0, beta[:, 0:NT, :], ALU.mult, ALU.mult))

            def spread(ch):
                step(TT(three(mgt[:, ch % 2, :]), bc(gt, 1, DH), bc(gg[:, ch, :], 2, P), ALU.mult), s.mg_ready)

            spread(0)
            for ch in range(NT):
                if ch + 1 < NT:
                    spread(ch + 1)
                dve.wait_ge(s.E_ready, ch + 1)
                e1, e2 = three(E1[:, ch % 2, :]), three(E2[:, ch % 2, :])
                step(TT(e1, e1, bc(gt, 1, DH), ALU.mult))
                step(TT(e1, e1, bc(beta[:, ch, :], 2, P), ALU.mult))
                b = ring.to_read()
                step(TT(Lc[:, ch, :], b[:, :], E1[:, ch % 2, :], ALU.mult), s.dring_free)
                step(TT(e2, e2, bc(le, 1, DH), ALU.mult))
                b = ring.to_read()
                step(TT(ATc[:, ch, :], b[:, :], E2[:, ch % 2, :], ALU.mult), s.dring_free)
                dve.sem_inc(s.L_ready, 1)
            for lv in range(7):
                mask = consts[:, C_LVL + lv * P:C_LVL + (lv + 1) * P]
                for ch in range(NT):
                    step(TT(three(Lm[:, ch, :]), three(Lc[:, ch, :]), bc(mask, 1, DH), ALU.mult), s.lm_ready)
                for ch in range(NT):
                    if lv == 0:
                        step(TT(three(Tc[:, ch, :]), bc(ident, 1, DH), three(Lm[:, ch, :]), ALU.subtract))
                        b = ring.to_read()
                        step(TT(three(Wc[:, ch, :]), bc(ident, 1, DH), three(b[:, :]), ALU.subtract), s.dring_free)
                        dve.sem_inc(s.wt_ready, 1)
                        continue
                    b = ring.to_read()
                    step(TT(Wc[:, ch, :], Wc[:, ch, :], b[:, :], ALU.subtract), s.dring_free)
                    if lv < 6:
                        b = ring.to_read()
                        step(TT(Tc[:, ch, :], Tc[:, ch, :], b[:, :], ALU.subtract), s.dring_free)
                    dve.sem_inc(s.wt_ready, 1)
            R, qs, o = E1[:, 0, :], E1[:, 1, :], E2[:, 1, :]
            step(dve.memset(delta[:, :], 0.0), s.S_ready)
            for ch in range(NT):
                cs = slice(4 * ch, 4 * ch + 4)
                b = ring.to_read()
                step(TT(three(R), three(b[:, :]), bc(nbeg[:, cs], 2, P), ALU.mult), s.dring_free)
                step(TT(R, R, vb[:, ch, :], ALU.add), s.r_ready)
                if ch < NT - 1:
                    modulation(3 + ch)
                dve.wait_ge(s.qs_ready, ch + 1)
                step(TT(three(o), three(qs), bc(ex[:, cs], 2, P), ALU.mult))
                step(TT(three(delta[:, :]), three(delta[:, :]), bc(ex[:, 32 + 4 * ch:36 + 4 * ch], 2, P), ALU.mult))
                b = ring.to_read()
                step(TT(delta[:, :], delta[:, :], b[:, :], ALU.add), s.dring_free)
                dve.sem_inc(s.S_ready, 1)
                b = ring.to_read()
                step(TT(o, o, b[:, :], ALU.add), s.dring_free)
                step(TT(R, o, o, ALU.mult))
                step(dve.tensor_reduce(rms4, three(R), AX.X, ALU.add), s.o_ready)
                dve.wait_ge(s.orms_ready, ch + 1)
                step(recip(rms4, rms4))
                step(TT(three(o), three(o), bc(rms4, 2, P), ALU.mult), s.on_ready)
                b = ring.to_read()
                here = slice(ch * P, (ch + 1) * P)
                step(STT(odT[:, :, here], three(b[:, :]), cols[:, K_DN:K_DN + 1], zT[:, :, here], ALU.mult, ALU.mult), s.dring_free)
                dve.sem_inc(s.od_done, 1)
            eg, be, rr, sgx, prod, ks_, qs_, vn, oo, oo2 = sdv[0], sdv[1], sdv[2], at(E0 + 1832 + 96, 64), sdv[5], sdv[6], sdv[7], sdv[8], sdv[9], sdv[10]
            i8 = consts[0:NB, 0:NB]
            for i, v in enumerate((gg, beta)):
                step(TT(three(sgx[0:NB, 32 * i:32 * i + 32], NB), bc(v[0:NB, NT, :], 2, NB), bc(i8, 1, DH), ALU.mult), s.dve_step if i == 0 else s.sg_ready)
            step(copy(three(sdv[12], NB), ct[:, DH:2 * DH, SEQ:TOK]))
            step(TT(three(prod, NB), ct[:, 0:DH, SEQ:TOK], three(sdv[12], NB), ALU.mult), s.sp_ready)
            dve.wait_ge(s.sa_ready, 1)
            b = ring.to_read()
            kq = b[:, 0:64].rearrange("p (c z) -> p c z", z=2)
            step(TT(ks_, kq[:, :, 1], eg, ALU.mult))
            step(TT(qs_, kq[:, :, 0], eg, ALU.mult), s.dring_free)
            step(TT(vn, svv, ks_, ALU.subtract))
            step(TT(vn, vn, be, ALU.mult), s.sn_ready)
            b = ring.to_read()
            step(TT(oo, b[:, 0:32], vn, ALU.mult), s.dring_free)
            step(TT(oo, oo, qs_, ALU.add))
            step(TT(oo2, oo, oo, ALU.mult), s.sn_ready)
            b = ring.to_read()
            step(copy(kn8, b[0:NB, :]), s.dring_free)
            b = ring.to_read()
            step(copy(vn8, b[0:NB, :]), s.dring_free)
            for h in range(DH):
                vd = at(R0 + 1024 * (h % 2), NB, P)[0:NB]
                step(TT(vd, bc(vn8[:, h * P:(h + 1) * P], 1, NB), bc(i8, 2, P), ALU.mult), s.vd_ready)
                for g in range(2):
                    st = sdel[:, h, 4 * g:4 * g + 4, :]
                    b = ring.to_read()
                    step(TT(st, st, bc(eg[:, h * NB + 4 * g:h * NB + 4 * g + 4], 2, P), ALU.mult))
                    step(TT(st, st, three(b[:, :]), ALU.add), s.dring_free)
            dve.sem_inc(s.sd_ready, 1)
            dve.wait_ge(s.sa_ready, 2)
            step(recip(rr, rr))
            step(TT(oo, oo, rr, ALU.mult))
            step(STT(odT[:, :, SEQ:TOK], three(oo, NB), cols[:, K_DN:K_DN + 1], zT[:, :, SEQ:TOK], ALU.mult, ALU.mult), s.od_done)
            for m in range(KT):
                for lo, hi in PARTS:
                    for g in (gaT, gbT):
                        v = g[:, m, lo:hi]
                        b = ring.to_read()
                        step(TT(v, v, b[:, 0:hi - lo], ALU.mult), s.dring_free)
                step(TT(gaT[:, m, :], gaT[:, m, :], gbT[:, m, :], ALU.add), s.merged_ready)
            dve.wait_ge(s.out_small, 64)
            for v, vp_, vs_ in ((2, v_g1, s_g1), (4, v_a2, s_a2), (3, v_s2, s_s2), (5, v_g2, s_g2)):
                step(TT(three(t1), bc(ident, 1, KT), bc(adaT[:, v * KT:(v + 1) * KT, 0], 2, P), ALU.mult), s.dg_ready)
                for dst, r in ((vp_, P), (vs_, NB)):
                    for g in range(2):
                        b = ring.to_read()
                        step(copy(dst[0:r, g * 512:(g + 1) * 512], b[0:r, :]), s.dring_free)

            def mean_square(src, r, k):
                step(TTR(t2[r, :], src, src, 1.0, 0.0, ALU.mult, ALU.add, ssx[r, 0:1]), s.ms_ready)
                dve.wait_ge(s.mr_ready, k)
                step(recip(rstd[r, 0:1], rstd[r, 0:1]))

            dve.wait_ge(s.xr_in, 32)

            def residual(t):
                r = slice(0, ROWS[t])
                g1, a2, s2 = (v_g1, v_a2, v_s2) if t < NT else (s_g1, s_a2, s_s2)
                h = h2[r, t, :] if t < NT else h2s[r, :]
                for g in range(2):
                    b = ring.to_read()
                    step(copy(t1[r, g * 512:(g + 1) * 512], b[r, :]), s.dring_free)
                mean_square(t1[r, :], r, 2 * t + 1)
                step(STT(t1[r, :], t1[r, :], rstd[r, 0:1], g1[r, :], ALU.mult, ALU.mult))
                step(TT(x_t[r, t, :], x_t[r, t, :], t1[r, :], ALU.add))
                mean_square(x_t[r, t, :], r, 2 * t + 2)
                step(STT(h, x_t[r, t, :], rstd[r, 0:1], a2[r, :], ALU.mult, ALU.mult))
                step(TT(h, h, s2[r, :], ALU.add), s.h2_ready)

            def search(jobs, count, base):
                looped = not isinstance(base, int)
                steps_done = [0]
                last = {}

                def after(*keys, bare=False):
                    dve.wait_ge(s.dve_step, base + max(last.get(k, 0) for k in keys))
                    if bare and looped:
                        dve.sem_inc(s.dve_turn, 1)

                def did(key, ins):
                    ins.then_inc(s.dve_step, 1)
                    steps_done[0] += 1
                    last[key] = steps_done[0]

                def sixteen(chains):
                    for key, val, idx, src, spare in chains:
                        after(key, bare=True)
                        did(key, dve.max(val[:, 0:8], src))
                    for key, val, idx, src, spare in chains:
                        after(key, bare=True)
                        did(key, dve.max_index(idx[:, 0:8], val[:, 0:8], src))
                    for key, val, idx, src, spare in chains:
                        after(key, bare=True)
                        did(key, dve.match_replace(spare, val[:, 0:8], src, -3e38))
                    for key, val, idx, src, spare in chains:
                        after(key, bare=True)
                        did(key, dve.max(val[:, 8:16], spare))
                    for key, val, idx, src, spare in chains:
                        after(key, bare=True)
                        did(key, dve.max_index(idx[:, 8:16], val[:, 8:16], spare))

                H = [(i, n, slice(0, ROWS[n]), h, lanes[i]) for i, (n, h) in enumerate(jobs)]
                for i, n, r, h, q in H:
                    after(i)
                    did(i, copy(q.s_in[r].rearrange("p a q -> p (a q)"), sc[n % 2][r, bass.ds(h * (2 * NKEY), 2 * NKEY)]))
                    last[i, 0] = last[i, 1] = last[i]
                sixteen([((i, p), q.sv[r, p, :], q.si[r, p, :], q.s_in[r, p, :], q.s_out[r, p, :]) for i, n, r, h, q in H for p in range(2)])
                for i, n, r, h, q in H:
                    after((i, 0), (i, 1))
                    did(i, TT(three(q.cand[r, :], TOPK), bc(q.sv[r, 0, :], 2, TOPK), bc(q.sv[r, 1, :], 1, TOPK), ALU.add))
                sixteen([(i, q.best[r, :], q.pos[r, :], q.cand[r, :], q.cand2[r, :]) for i, n, r, h, q in H])
                for i, n, r, h, q in H:
                    after(i)
                    TS(q.nbest[r, :], q.best[r, 0:1], -1.0, None, ALU.mult).then_inc(s.best_ready, 1)
                for i, n, r, h, q in H:
                    did(i, copy(q.sif[r], q.si[r]))
                    did((i, 0), TS(q.pint[r, 0, :], q.pos[r, :], 4, None, ALU.logical_shift_right))
                    did((i, 1), TS(q.pint[r, 1, :], q.pos[r, :], 15, None, ALU.bitwise_and))
                for i, n, r, h, q in H:
                    after((i, 0), (i, 1))
                    did((i, 0), copy(q.pf[r], q.pint[r]))
                for i, n, r, h, q in H:
                    after((i, 0))
                    did((i, 0), TT(q.hit[r].rearrange("p a k i -> p (a k) i"), bc(q.pf[r].rearrange("p a k -> p (a k)"), 2, TOPK),
                                   bc(consts[r, C_IOTA:C_IOTA + TOPK], 1, 2 * TOPK), ALU.is_equal))
                for i, n, r, h, q in H:
                    after((i, 0))
                    did((i, 0), TT(q.hit[r], q.hit[r], bc(q.sif[r], 2, TOPK), ALU.mult))
                for i, n, r, h, q in H:
                    after((i, 0))
                    did((i, 0), dve.tensor_reduce(q.ee[r], q.hit[r], AX.X, ALU.add))
                for i, n, r, h, q in H:
                    after((i, 0))
                    did((i, 0), STT(q.ef[r, :], q.ee[r, 0, :], float(NKEY), q.ee[r, 1, :], ALU.mult, ALU.add))
                for i, n, r, h, q in H:
                    dve.wait_ge(s.gexp_ready, count + (i + 1))
                    did(i, recip(q.gsum[r, :], q.gsum[r, :]))
                for i, n, r, h, q in H:
                    after((i, 0))
                    did((i, 0), copy(eidx[r, n % 2, bass.ds(h * TOPK, TOPK)], q.ef[r, :]))
                for i, n, r, h, q in H:
                    after(i, (i, 0))
                    TS(gate[r, n % 2, bass.ds(h * TOPK, TOPK)], q.gexp[r, :], q.gsum[r, 0:1], None, ALU.mult).then_inc(s.topk_done, 1)
                dve.wait_ge(s.topk_done, count + len(jobs))
                return steps_done[0]

            def dots(r, a, x, g):
                for j in range(SLOTS):
                    dve.wait_ge(u_in[j], r * 16 + 16)
                    TTR(uring[j], uring[j], x, 1.0, 0.0, ALU.mult, ALU.add, act8[:, a, j:j + 1]).then_inc(u_used[j], 1)
                dve.wait_ge(s.gelu_ready, r + 1)
                TT(w8[:, a, :], act8[:, a, :], g, ALU.mult).then_inc(s.w_ready, 1)

            steps = [0]

            def next_step(ins):
                ins.then_inc(s.dve_step, 1)
                steps[0] += 1
                dve.wait_ge(s.dve_step, steps[0])

            def finish(t, g2):
                r = slice(0, ROWS[t])
                dve.wait_ge(v_used[SLOTS - 1], 2 * PH * (t + 1) if t < NT else 2 * PH * NT + 1)
                next_step(copy(t1[r, 0:512], fsum[t % 2][0][r, :]))
                step(copy(t1[r, 512:1024], fsum[t % 2][1][r, :]), s.f_read)
                step(TTR(t2[r, :], t1[r, :], t1[r, :], 1.0, 0.0, ALU.mult, ALU.add, ssx[r, 0:1]), s.ms_ready)
                dve.wait_ge(s.mr_ready, 2 * (NT + 1) + t + 1)
                next_step(recip(rstd[r, 0:1], rstd[r, 0:1]))
                next_step(STT(t1[r, :], t1[r, :], rstd[r, 0:1], g2[r, :], ALU.mult, ALU.mult))
                step(TT(x_t[r, t, :], x_t[r, t, :], t1[r, :], ALU.add), s.y_ready)

            for t in range(NT + 1):
                residual(t)
            dve.wait_ge(s.sc_ready, 1)
            steps[0] = step.n[s.dve_step.name]
            steps[0] += search([(0, 0)], 0, steps[0])

            for g in range(2):
                b = ring.to_read()
                step(copy(h2sb[:, g * 512:(g + 1) * 512], b[:, :]), s.dring_free)

            for t in range(NT):
                lanes_in_use = 1 + (t == NT - 1)

                def head(h, base):
                    for a in range(2):
                        r = h * 2 + (2 * PH * t + a)
                        if not (isinstance(r, int) and r == 0):
                            dve.wait_ge(s.w_ready, r)
                        copy(gcur[:, :], gate[:, t % 2, bass.ds(h * TOPK + a * SLOTS, SLOTS)]).then_inc(s.gc_ready, 1)
                        dve.wait_ge(s.gc_ready, r + 1)
                        dots(r, a, h2[:, t, :], gcur[:, :])
                        if a == 0 and next_heads(t, h):
                            done = search(next_heads(t, h), searched(t, h) + lanes_in_use, base)
                            assert done == N_SEARCH * len(next_heads(t, h))
                            if isinstance(h, int):
                                steps[0] += done
                            if t and isinstance(h, int) and h == 0:
                                finish(t - 1, v_g2)
                head(0, steps[0])
                per_head = N_SEARCH * lanes_in_use
                with dve.Fori(1, PH - 1) as h:
                    head(h, h * per_head + (steps[0] - per_head))
                steps[0] += (PH - 2) * per_head
                if t < NT - 1:
                    dve.wait_ge(s.sc_ready, (2, 3, NT + 1)[t])
                head(PH - 1, steps[0])
            dve.wait_ge(s.sel_in, 2 * 16 * NB)
            dots(2 * PH * NT, 0, h2sb, sgate)
            finish(NT - 1, v_g2)
            finish(NT, s_g2)


def layout(a):
    f = lambda v: np.ascontiguousarray(v, dtype=np.float32)
    blocks = lambda w: w.reshape(KT, P, -1, P).transpose(2, 1, 0, 3)
    w_in, w_ada = a["w_in"][0], a["w_ada"][0]
    aq, ak, av, conv, dec, bb, z, g_a, g_b = np.split(w_in, np.cumsum([512, 128, 128, 1536, 4, 4, 512, 1024]), axis=1)
    pair = [h * HD + i for g in range(HG) for h in (g, g + HG) for i in range(HD)]
    ada = blocks(w_ada)
    branch = np.concatenate([a["w_att_out"][0][pair], a["w_delta_out"][0]], axis=0)
    wstream = np.concatenate([ada[0:16], blocks(conv), blocks(aq[:, pair]), blocks(z), blocks(g_a), blocks(g_b), ada[16:48],
                              blocks(branch), blocks(a["w_query"][0])], axis=0)
    tile = lambda v: v.reshape(-1, P).T
    cols = np.concatenate(
        [tile(a["b_ada"][0]), tile(a["g_pre_mix"][0]), tile(a["g_post_mix"][0]), tile(a["g_pre_ffn"][0]), tile(a["g_post_ffn"][0]),
         a["w_conv"][0].reshape(4, CT_N, P).transpose(2, 1, 0).reshape(P, -1), tile(a["delta_norm"][0]),
         np.broadcast_to(a["attn_sinks"][0], (P, 8)), np.broadcast_to(a["a_log"][0], (P, 4)), np.broadcast_to(a["dt_bias"][0], (P, 4)),
         np.tile(a["attn_sinks"][0], 16)[:, None]], axis=1)
    c = np.concatenate([a["c_prompt"], a["c_sample"]], axis=0)
    return {
        "cT": f(c.T.reshape(KT, P, 1 + NB).transpose(1, 0, 2)),
        "x": f(a["x_prompt"][0]), "xs": f(a["x_sample"][:, 0]),
        "wstream": f(wstream), "wnat": f(np.concatenate([ak, av, dec, bb], axis=1).reshape(KT, P, NAT_W).transpose(1, 0, 2)),
        "wout": f(a["w_out"][0].reshape(KT, P, D).transpose(1, 0, 2)),
        "cols": f(cols), "rel": f(a["rel_bias"]),
        "cst": f(a["state_conv"][0].reshape(NB, 3, CT_N, P).transpose(3, 2, 0, 1)),
        "kc": f(a["cache_swa_k"][0].reshape(NB, WIN, P)), "vc": f(a["cache_swa_v"][0].reshape(NB, WIN, P)),
        "sdel": f(a["state_delta"][0].transpose(2, 1, 0, 3)),
        "skt": f(a["sub_keys"][0].transpose(2, 0, 1)),
        "eu": f(a["expert_u"][0]), "ev": f(a["expert_v"][0]),
    }


def constants():
    r, c = np.arange(P)[:, None], np.arange(P)[None, :]
    out = [r == c, r <= c, r > c, np.ones((P, P))]
    for lv in range(7):
        m = 1 << lv
        out.append((r // (2 * m) == c // (2 * m)) & (r % (2 * m) >= m) & (c % (2 * m) < m))
    out.append(np.broadcast_to(np.arange(TOPK), (P, TOPK)))
    out.append(r // TOPK == c[:, 0:NB])
    out.append((c // TOPK == r) & (r < NB))
    onehot = np.zeros((33, 384), np.float32)
    for i in range(384):
        d = 255 - i
        if 0 <= d < WIN:
            big = 16 + int(np.log(np.float32(max(d, 1)) / np.float32(16)) / np.float32(np.log(8.0)) * np.float32(16))
            onehot[d if d < 16 else min(big, 31), i] = 1.0
        else:
            onehot[32, i] = 1.0
    return {"consts": np.concatenate([np.asarray(o, np.float32) for o in out], axis=1), "onehot": onehot}


OUTS = {"yp": (SEQ, D), "ys": (NB, D), "kp": (WIN, P), "vp": (WIN, P), "convp": (P, CT_N, 3), "deltap": (P, 512),
        "ks": (NB, WIN, P), "vs": (NB, WIN, P), "convs": (P, CT_N, NB, 3), "deltas": (P, DH, NB, P)}


def kernel(**inputs):
    import concourse.bacc as bacc
    from concourse.bass_utils import run_bass_kernel_spmd

    nc = bacc.Bacc("TRN2", target_bir_lowering=False, num_devices=1)
    arrays = layout({k: np.asarray(v) for k, v in inputs.items()})
    arrays.update(constants())
    ins = {k: nc.dram_tensor("in_" + k, v.shape, F32, kind="ExternalInput").ap() for k, v in arrays.items()}
    ins["skew"] = nc.dram_tensor("skew", (HQ, P, 384), F32, kind="Internal").ap()
    ins["sidx"] = nc.dram_tensor("sidx", (NB, P), U32, kind="Internal").ap()
    ins["sgate"] = nc.dram_tensor("sgate", (NB, P), F32, kind="Internal").ap()
    outs = {k: nc.dram_tensor("out_" + k, v, F32, kind="ExternalOutput").ap() for k, v in OUTS.items()}
    build(nc, ins, outs)
    got = run_bass_kernel_spmd(nc, [{"in_" + k: v for k, v in arrays.items()}], core_ids=[0]).results[0]
    o = {k: got["out_" + k] for k in OUTS}
    win = lambda v: v.reshape(1, -1, WIN, 2, HD)
    return (o["yp"].reshape(1, SEQ, D), o["ys"].reshape(NB, 1, D), win(o["kp"]), win(o["vp"]),
            np.ascontiguousarray(o["convp"].transpose(2, 1, 0)).reshape(1, 1, 3, CT_N * P),
            np.ascontiguousarray(o["deltap"].reshape(P, DH, P).transpose(1, 0, 2)).reshape(1, 1, DH, P, P),
            win(o["ks"]), win(o["vs"]),
            np.ascontiguousarray(o["convs"].transpose(2, 3, 1, 0)).reshape(1, NB, 3, CT_N * P),
            np.ascontiguousarray(o["deltas"].transpose(2, 1, 0, 3)).reshape(1, NB, DH, P, P))
```

```python
from contextlib import ExitStack
from collections import namedtuple

import numpy as np
import concourse.bass as bass
from concourse import mybir

ALU = mybir.AluOpType
ACT = mybir.ActivationFunctionType
AX = mybir.AxisListType
F32 = mybir.dt.float32
U32 = mybir.dt.uint32

P = 128
D = 1024
KT = D // P
SEQ = 512
NT = SEQ // P
NB = 8
TOK = SEQ + NB
CUT = SEQ // 2
PARTS = ((0, CUT), (CUT, TOK))
HQ, HD = 8, 64
HG = 4
DH = 4
CT_N = 12
WIN = 128
NAT_W = 264
PH = 8
TOPK = 16
N_SEARCH = 27
NKEY = 128
SLOTS = 8
EPS = 1e-6
NEG = -1e30
B_ADA1, B_CONV, B_Q, B_Z, B_GA, B_GB, B_ADA2, B_BR, B_QRY = 16, 12, 4, 4, 8, 8, 32, 8, 16
BEHIND, AHEAD = [1] * B_CONV + [2] * B_Q, [1, 2] * DH
C_ID, C_LE, C_GT, C_ONE, C_LVL, C_IOTA, C_TK, C_KT = 0, 128, 256, 384, 512, 1408, 1424, 1432
C_W = 1560
K_CONV, K_DN, K_SINK, K_ALOG, K_DT, K_SINKS = 0, 48, 49, 57, 61, 65
K_W = 66
NCOND = 1 + NB
CHUNK = 4


class Steps:

    def __init__(self, eng, own):
        self.eng, self.own, self.n = eng, own, {}

    def __call__(self, ins, sem=None):
        sem = self.own if sem is None else sem
        ins.then_inc(sem, 1)
        self.n[sem.name] = self.n.get(sem.name, 0) + 1
        self.eng.wait_ge(sem, self.n[sem.name])


class Ring:

    def __init__(self, eng, banks, full, free):
        self.eng, self.banks, self.full, self.free, self.n = eng, banks, full, free, 0

    def to_fill(self):
        if self.n >= len(self.banks):
            self.eng.wait_ge(self.free, self.n - len(self.banks) + 1)
        self.n += 1
        return self.banks[(self.n - 1) % len(self.banks)]

    def to_read(self):
        self.eng.wait_ge(self.full, self.n + 1)
        self.n += 1
        return self.banks[(self.n - 1) % len(self.banks)]


def build(nc, I, O):
    with ExitStack() as ctx:
        def sb(name, shape, dt=F32):
            return ctx.enter_context(nc.sbuf_tensor(name, shape, dt))

        def sem(name):
            return ctx.enter_context(nc.semaphore(name))

        consts = sb("consts", [P, C_W])
        cols = sb("cols", [P, K_W])
        onehot = sb("onehot", [33, 384])
        relx = sb("relx", [33, HQ])
        rels = sb("rels", [33, NB * HQ])
        skt = sb("skt", [P, 2, NKEY])
        cT = sb("cT", [P, KT, NCOND])
        adaT = sb("adaT", [P, 2 * KT, NCOND])
        small = sb("small", [P, 360])
        zeros = sb("zeros", [P, P])
        bext = sb("bext", [HQ, 384])
        delta = sb("delta", [P, 512])
        cpo = sb("cpo", [P, CT_N, 3])
        arena = sb("arena", [P, 48480])
        ident, le, gt, ones = (consts[:, c:c + P] for c in (C_ID, C_LE, C_GT, C_ONE))

        X0, HT0, WB0, CT0, KV0, QT0, Z0, GA0, GB0, R0, E0 = (
            0, 5120, 9280, 13376, 19616, 23712, 25792, 27872, 32032, 36192, 44384)

        def at(lo, *shape):
            v = arena[:, lo:lo + int(np.prod(shape))]
            if len(shape) == 2:
                v = v.rearrange("p (a b) -> p a b", b=shape[1])
            if len(shape) == 3:
                v = v.rearrange("p (a b c) -> p a b c", b=shape[1], c=shape[2])
            return v

        x_t = at(X0, NT + 1, D)
        hT = at(HT0, KT, TOK)
        wplace = [at(WB0 + D * i, D) for i in range(4)] + [at(E0 + 2408, D)]
        brow1, brow2 = at(GA0 + 2 * D, 2 * D)[0:NCOND], at(GB0, 4 * D)[0:NCOND]
        grow, mrow1, mrow2 = at(KV0, 4 * D)[0:NCOND], at(Z0, 2 * D)[0:NCOND], at(X0, 4 * D)[0:NCOND]
        ct = at(CT0, CT_N, TOK)
        qT = at(QT0, 4, TOK)
        zT = at(Z0, DH, TOK)
        gaT, gbT = at(GA0, KT, TOK), at(GB0, KT, TOK)
        junk = at(GA0, D)
        rnb = at(R0, 2, TOK)
        bias = at(R0, HQ, 256)
        wnat = at(R0 + 2048, KT, NAT_W)
        prob = at(R0 + 2048, HQ, 256)
        sqb = at(R0 + 4160, 2, TOK)
        probT = at(R0 + 4096, 2 * HQ, P)
        ubuf = at(R0 + 6144, 2, 547)
        keyc, valc = at(R0 + 6144, NB, P), at(R0 + 7168, NB, P)
        cst, cso = (at(E0 + 1832 + i, CT_N * NB, 3).rearrange("p (m b) i -> p m b i", b=NB) for i in (0, 288))
        nat = at(E0, NT + 1, NAT_W)
        kT = at(E0 + 1320, SEQ)
        attT = qT
        odT = at(HT0 + 4 * TOK, DH, TOK)
        kdec, vb = at(KV0, NT, 512), at(KV0 + 2048, NT, 512)
        sdel = at(X0, DH, NB, P)
        mgt = at(X0 + 4096, 2, 512)
        Lc, Wc, Tc = (at(R0 + 2048 * i, NT, 512) for i in range(3))
        Lm, A2 = at(R0 + 6144, NT, 512), at(E0 + 1832, NT, 512)
        ATc = at(CT0 + 8 * TOK, NT, 512)
        E1, E2 = at(HT0, 2, 512), at(HT0 + 1024, 2, 512)
        wout = at(CT0, KT, D)
        v_g1, v_a2, v_s2 = (at(R0 + D * i, D) for i in (0, 1, 2))
        s_g1, s_a2, s_s2 = (at(R0 + D * i, D) for i in (3, 4, 5))
        v_g2, s_g2 = at(R0 + 6144, D), at(R0 + 7168, D)
        t1, t2 = at(E0, D), at(E0 + 2 * D, D)
        h2 = at(HT0, NT, D)
        h2s = at(E0 + 2 * D, D)
        h2T = [at(GB0, KT, P), at(GB0 + D, KT, TOK - P)]
        Q0 = QT0 - 64
        qryT = [at(Q0, 2 * PH, P), at(WB0, 2 * PH, P), at(Q0, 2 * PH, TOK - CUT)]
        uring = [at(CT0 + D * j, D) for j in range(SLOTS)]
        vring = [at(GA0 + D * j, D) for j in range(4)] + [at(R0 + D * j, D) for j in range(4)]
        sc = [at(R0 + 4 * D, 2 * PH * NKEY), at(GB0, 2 * PH * NKEY)]
        diag, h2sb = at(E0 + D, SLOTS, P), at(WB0, D)

        class Lane:

            def __init__(self, lo, lo2, lo3):
                self.s_in, self.s_out = at(lo, 2, NKEY), at(lo + 256, 2, NKEY)
                self.sv, self.si = at(lo + 512, 2, TOPK), at(lo + 544, 2, TOPK).bitcast(U32)
                self.sif, self.pf, self.ee = at(lo + 576, 2, TOPK), at(lo + 608, 2, TOPK), at(lo + 640, 2, TOPK)
                self.pint = at(lo + 672, 2, TOPK).bitcast(U32)
                self.best, self.pos = at(lo + 704, TOPK), at(lo + 720, TOPK).bitcast(U32)
                self.gexp, self.ef = at(lo + 736, TOPK), at(lo + 752, TOPK)
                self.cand, self.cand2 = at(lo2, TOPK * TOPK), at(lo2 + 256, TOPK * TOPK)
                self.hit = at(lo2 + 512, 2, TOPK, TOPK)
                self.nbest, self.gsum = at(lo3, 1), at(lo3 + 1, 1)

        F1, F2, F3 = CT0 + 8 * D, E0 + 3 * D, HT0 + 4 * D
        lanes = [Lane(F1, F1 + 768, F3), Lane(WB0 + 2 * D, WB0 + 3 * D, F3 + 2)]
        gate, eidx = at(F2, 2, PH * TOPK), at(F2 + 256, 2, PH * TOPK).bitcast(U32)
        sgate, sidx = at(F3 + 4, SLOTS), at(F3 + 12, SLOTS).bitcast(U32)

        def sm(lo, n):
            return small[:, lo:lo + n]
        ssx, rstd, eps, eps128 = sm(0, 8), sm(8, 8), sm(16, 1), sm(17, 1)
        mx8, nm8, sm8, es8 = sm(18, 8), sm(26, 8), sm(34, 8), sm(42, 8)
        gg = sm(50, 20).rearrange("p (t h) -> p t h", h=DH)
        beta = sm(70, 20).rearrange("p (t h) -> p t h", h=DH)
        gtmp, gtmp2 = (sm(a, 20).rearrange("p (t h) -> p t h", h=DH) for a in (90, 110))
        ealog = sm(130, 4)
        ex = sm(134, 48)
        nbeg = sm(182, 16)
        rms4 = sm(198, 4)
        lt64 = sm(206, 64)
        act8 = sm(270, 16).rearrange("p (a j) -> p a j", j=SLOTS)
        w8 = sm(286, 16).rearrange("p (a j) -> p a j", j=SLOTS)
        cur = sm(302, 16).bitcast(U32).rearrange("p (a j) -> p a j", j=SLOTS)
        svv = sm(318, 32)
        gcur = sm(350, 8)
        kn8, vn8 = at(R0 + 2048, 512)[0:NB], at(R0 + 2560, 512)[0:NB]
        sdv = [at(E0 + 1832 + 32 * i, 32) for i in range(13)]

        dbank = [ctx.enter_context(nc.psum_tensor(f"dbank{i}", [P, 512], F32)) for i in range(4)]
        abank = [ctx.enter_context(nc.psum_tensor(f"abank{i}", [P, 512], F32)) for i in range(2)]
        fsum = [[ctx.enter_context(nc.psum_tensor(f"fsum{i}", [P, 512], F32)) for i in range(2)], dbank[0:2]]

        names = """dring_full dring_free aring_full aring_free w_used consts_in cols_in cT_in x_in wnat_in bias_in
            cst_in keyc_in valc_in sdel_in wout_in xr_in skt_in silu_c ss_ready rms_ready rstd_ready xn_ready hT_ready
            conv_in conv_out silu_out sq_ready rn_ready l2_done nat_ready rels_ready qT_ready kT_ready ext_ready ext_out
            gx_ready beta_ready g_ready nm_ready exp_done prob_ready probT_ready att_done lt_ready kTs_ready
            ex_ready  mg_ready E_ready L_ready lm_ready a2_ready wt_ready S_ready r_ready vn_ready qs_ready
            o_ready orms_ready on_ready od_done sg_ready sa_ready sp_ready sn_ready vd_ready sd_ready merged_ready rows_in brow_in mrow_ready mrows_ready mod_out mod_in
            ms_ready mr_ready h2_ready h2T_ready qry_ready  sc_ready best_ready gexp_ready topk_done
            sel_out sel_in gelu_ready w_ready diag_ready gc_ready f_read y_ready
            out_small out_k out_delta out_y dve_turn pool_turn dve_step act_step pool_step""".split()
        s = namedtuple("Semaphores", names)(*(sem(n) for n in names))
        w_full = [sem(f"w_full{i}") for i in range(5)]
        u_in = [sem(f"u_in{i}") for i in range(SLOTS)]
        v_in = [sem(f"v_in{i}") for i in range(SLOTS)]
        u_used = [sem(f"u_used{i}") for i in range(SLOTS)]
        v_used = [sem(f"v_used{i}") for i in range(SLOTS)]

        ROWS = [P] * NT + [NB]
        COL = [t * P for t in range(NT)] + [SEQ]

        def tcols(t):
            return slice(COL[t], COL[t] + ROWS[t])

        def searched(t, h):
            return h * (1 if t < NT - 1 else 2) + PH * t

        def next_heads(t, h):
            if isinstance(h, int) and h == PH - 1:
                return ([], [(t + 1, 0), (NT, 0)], [(t + 1, 0)])[(t < NT - 1) + (t < NT - 2)]
            return [(t, h + 1)] + [(NT, h + 1)] * (t == NT - 1)

        N_AHEAD = B_ADA1 + B_CONV + B_Q + B_Z + B_GA + B_GB + B_ADA2 - 4
        N_FIRST = N_AHEAD + 4 + B_BR + B_QRY
        PLACE = [n % 5 if n < N_AHEAD else n % 4 for n in range(N_FIRST)] + [2 + m % 2 for m in range(B_QRY)]

        def loads(n):
            return PLACE[:n + 1].count(PLACE[n])

        block = ctx.enter_context(nc.Block())

        @block.gpsimd
        def _(pool):
            step = Steps(pool, s.pool_step)
            def row(lo, n):
                return bass.AP(tensor=I["rows"].tensor, offset=lo, ap=[[0, NCOND], [1, n]])

            pool.dma_start(cT[:, :, :], I["cT"]).then_inc(s.cT_in, 16)
            pool.dma_start(x_t[:, 0:NT, :], I["x"].rearrange("(t p) d -> p t d", p=P)).then_inc(s.x_in, 16)
            pool.dma_start(x_t[0:NB, NT, :], I["xs"]).then_inc(s.x_in, 16)
            pool.dma_start(consts[:, :], I["consts"]).then_inc(s.consts_in, 16)
            pool.dma_start(brow1, row(0, 2 * D)).then_inc(s.rows_in, 16)
            pool.dma_start(grow, row(6 * D, 4 * D)).then_inc(s.rows_in, 16)
            pool.dma_start(onehot[:, :], I["onehot"]).then_inc(s.consts_in, 16)
            pool.dma_start(cols[:, :], I["cols"]).then_inc(s.cols_in, 16)
            pool.dma_start(relx[0:32, :], I["rel"]).then_inc(s.cols_in, 16)
            pool.dma_start(cst, I["cst"]).then_inc(s.cst_in, 16)
            pool.wait_ge(s.hT_ready, 1)
            pool.dma_start(brow2, row(2 * D, 4 * D)).then_inc(s.brow_in, 16)
            pool.dma_start(wnat, I["wnat"]).then_inc(s.wnat_in, 16)
            pool.dma_start(skt[:, :, :], I["skt"]).then_inc(s.skt_in, 16)
            pool.wait_ge(s.conv_out, CT_N)
            pool.dma_start(O["convp"], cpo[:, :, :]).then_inc(s.out_small, 16)
            pool.dma_start(O["convs"], cso).then_inc(s.out_small, 16)
            pool.wait_ge(s.nat_ready, NT + 1)
            for c0, cache, win, last in ((0, "kc", "ks", "kp"), (P, "vc", "vs", "vp")):
                pool.dma_start(O[win][:, 0:WIN - 1, :], I[cache][:, 1:WIN, :]).then_inc(s.out_k, 16)
                pool.dma_start(O[win][:, WIN - 1, :], nat[0:NB, NT, c0:c0 + P]).then_inc(s.out_k, 16)
                pool.dma_start(O[last], nat[:, NT - 1, c0:c0 + P]).then_inc(s.out_small, 16)
            pool.wait_ge(s.out_k, 64)
            pool.dma_start(keyc, O["ks"].rearrange("b w c -> w b c")).then_inc(s.keyc_in, 16)
            pool.dma_start(valc, O["vs"].rearrange("b w c -> w b c")).then_inc(s.valc_in, 16)
            pool.wait_ge(s.ext_ready, 1)
            pool.dma_start(I["skew"], bext[:, :].unsqueeze(1).to_broadcast([HQ, P, 384])).then_inc(s.ext_out, 16)
            pool.wait_ge(s.ext_out, 16)
            pool.wait_ge(s.l2_done, 2 * DH)
            pool.dma_start(bias, bass.AP(tensor=I["skew"].tensor, offset=P - 1,
                                         ap=[[383, P], [P * 384, HQ], [1, 256]])).then_inc(s.bias_in, 16)
            pool.wait_ge(s.mrows_ready, 8)
            pool.dma_start(I["mod"], mrow2).then_inc(s.mod_out, 16)
            pool.wait_ge(s.mod_out, 16)
            pool.dma_start(sdel, I["sdel"]).then_inc(s.sdel_in, 16)
            pool.wait_ge(s.S_ready, NT + 1)
            pool.dma_start(O["deltap"], delta[:, :]).then_inc(s.out_delta, 16)
            pool.wait_ge(s.sd_ready, 1)
            pool.dma_start(O["deltas"], sdel).then_inc(s.out_delta, 16)
            for i, (v, vs_) in enumerate(((v_g1, s_g1), (v_s2, s_s2), (v_a2, s_a2), (v_g2, s_g2))):
                pool.dma_start(v, bass.AP(tensor=I["mod"].tensor, offset=i * D, ap=[[0, P], [1, D]])).then_inc(s.mod_in, 16)
                pool.dma_start(vs_[0:NB, :], I["mod"][1:NCOND, i * D:(i + 1) * D]).then_inc(s.mod_in, 16)
            pool.wait_ge(s.out_delta, 32)
            pool.dma_start(x_t[:, 0:NT, :], I["x"].rearrange("(t p) d -> p t d", p=P)).then_inc(s.xr_in, 16)
            pool.dma_start(x_t[0:NB, NT, :], I["xs"]).then_inc(s.xr_in, 16)
            pool.wait_ge(s.out_small, 64)

            def fetch(r, a, idx):
                later = not (isinstance(r, int) and r == 0)
                if later:
                    for j in range(SLOTS):
                        pool.wait_ge(u_used[j], r)
                pool.tensor_copy(cur[:, a, :], idx).then_inc(s.pool_step, 1)
                pool.wait_ge(s.pool_step, r + 1)
                pool.sem_inc(s.pool_turn, 1)
                for j in range(SLOTS):
                    pool.indirect_dma_start(uring[j], None, I["eu"],
                                            bass.IndirectOffsetOnAxis(cur[:, a, j:j + 1], 0)).then_inc(u_in[j], 16)
                for j in range(SLOTS):
                    if later:
                        pool.wait_ge(v_used[j], r)
                        pool.sem_inc(s.pool_turn, 1)
                    pool.indirect_dma_start(vring[j], None, I["ev"],
                                            bass.IndirectOffsetOnAxis(cur[:, a, j:j + 1], 0)).then_inc(v_in[j], 16)

            pool.wait_ge(s.h2_ready, NT + 1)
            for t in range(NT):
                def head(h):
                    pool.wait_ge(s.topk_done, searched(t, h) + 1)
                    for a in range(2):
                        fetch(h * 2 + (2 * PH * t + a), a, eidx[:, t % 2, bass.ds(h * TOPK + a * SLOTS, SLOTS)])
                if t == 0:
                    head(0)
                with pool.Fori(1 if t == 0 else 0, PH) as h:
                    head(h)
            pool.wait_ge(s.sel_in, 2 * 16 * NB)
            fetch(2 * PH * NT, 0, sidx)

        @block.scalar
        def _(act):
            step = Steps(act, s.act_step)
            ring = Ring(act, abank, s.aring_full, s.aring_free)
            A = act.activation

            def empty(dst, cols_from=slice(0, 512), rows=slice(0, P), func=ACT.Copy, **kw):
                b = ring.to_read()
                src = b[rows, cols_from]
                if len(dst.shape) == 3:
                    src = src.rearrange("p (a q) -> p a q", q=dst.shape[2])
                step(A(dst, src, func, **kw), s.aring_free)

            act.wait_ge(s.cT_in, 16)
            step(A(cT[:, :, :], cT[:, :, :], ACT.Silu), s.silu_c)
            for t in range(NT + 1):
                act.wait_ge(s.ss_ready, t + 1)
                step(A(rstd[0:ROWS[t], t:t + 1], ssx[0:ROWS[t], t:t + 1], ACT.Sqrt, bias=eps[0:ROWS[t], :], scale=1.0 / D), s.rms_ready)
            for t in range(NT + 1):
                act.wait_ge(s.rstd_ready, t + 1)
                step(A(x_t[0:ROWS[t], t, :], x_t[0:ROWS[t], t, :], ACT.Copy, scale=rstd[0:ROWS[t], t:t + 1]), s.xn_ready)
            for m in range(CT_N + 1):
                if m < CT_N:
                    u = ubuf[:, m % 2, :]
                    if m >= 2:
                        act.wait_ge(s.conv_out, m - 1)
                    if m == 0:
                        act.wait_ge(s.dve_step, 1)
                    empty(u[:, 3:3 + CUT], slice(0, CUT))
                    b = ring.to_read()
                    step(A(u[:, 3 + CUT:3 + SEQ], b[:, 0:SEQ - CUT], ACT.Copy))
                    step(A(u[:, 515:547].rearrange("p (b i) -> p b i", i=4)[:, :, 3], b[:, SEQ - CUT:TOK - CUT], ACT.Copy), s.aring_free)
                    act.sem_inc(s.conv_in, 1)
                if m >= 1:
                    act.wait_ge(s.conv_out, m)
                    step(A(ct[:, m - 1, :], ct[:, m - 1, :], ACT.Silu), s.silu_out)
            for t in range(NT + 1):
                empty(nat[0:ROWS[t], t, :], slice(0, NAT_W), slice(0, ROWS[t]))
                act.sem_inc(s.nat_ready, 1)
            for m in range(B_Q):
                for lo, hi in PARTS:
                    empty(qT[:, m, lo:hi], slice(0, hi - lo))
            act.sem_inc(s.qT_ready, 1)
            empty(kT)
            act.sem_inc(s.kT_ready, 1)
            empty(bext[:, :], slice(0, 384), slice(0, HQ))
            act.sem_inc(s.ext_ready, 1)
            gate_at = [0]

            def gates(n):
                for m in range(gate_at[0], gate_at[0] + n):
                    dst = zT[:, m, :] if m < B_Z else (gaT[:, m - B_Z, :] if m < B_Z + B_GA else gbT[:, m - B_Z - B_GA, :])
                    for lo, hi in PARTS:
                        empty(dst[:, lo:hi], slice(0, hi - lo), func=ACT.Silu if m < B_Z else ACT.Sigmoid)
                gate_at[0] += n

            for m in range(2 * DH):
                if m >= 2:
                    act.wait_ge(s.l2_done, m - 1)
                for lo, hi in PARTS:
                    empty(rnb[:, m % 2, lo:hi], slice(0, hi - lo), func=ACT.Sqrt,
                          bias=eps128 if m < DH else eps, scale=float(P) if m < DH else 1.0)
                act.sem_inc(s.rn_ready, 1)
                gates(1)
            act.wait_ge(s.cols_in, 32)
            step(A(ealog, cols[:, K_ALOG:K_ALOG + 4], ACT.Exp))
            act.wait_ge(s.gx_ready, 1)
            step(A(gtmp2, gtmp, ACT.Abs))
            step(A(gtmp2, gtmp2, ACT.Exp, scale=-1.0))
            step(A(gtmp2, gtmp2, ACT.Ln, bias=ones[:, 0:1]))
            step(A(beta, nat[:, :, 260:264], ACT.Sigmoid), s.beta_ready)
            for blk in range(NT):
                lo = 0 if blk else P
                gates(1)
                act.wait_ge(s.nm_ready, blk + 1)
                for h in range(HQ):
                    step(A(prob[:, h, lo:256], prob[:, h, lo:256], ACT.Exp, bias=nm8[:, h:h + 1], accum_out=sm8[:, h:h + 1]))
                step(A(es8, es8, ACT.Exp), s.exp_done)
                gates(1)
                for i in range(2 if blk == 0 else 4):
                    empty(probT[:, 4 * i:4 * i + 4, :])
                act.sem_inc(s.probT_ready, 1)
                gates(1)
                empty(attT[:, :, blk * P:(blk + 1) * P])
            for i in range(2):
                empty(probT[:, 4 * i:4 * i + 4, :])
            act.sem_inc(s.kTs_ready, 1)
            act.wait_ge(s.nm_ready, NT + 1)
            step(A(prob[0:64, 0, 0:P], prob[0:64, 0, 0:P], ACT.Exp, bias=nm8[0:64, 0:1], accum_out=sm8[0:64, 0:1]))
            step(A(es8[0:64, 0:1], es8[0:64, 0:1], ACT.Exp), s.exp_done)
            b = ring.to_read()
            step(A(attT[:, :, SEQ:TOK], b[:, 0:32].rearrange("p (b g) -> p g b", g=HG), ACT.Copy), s.aring_free)
            act.sem_inc(s.att_done, 1)
            empty(ex, slice(0, 48), func=ACT.Exp)
            act.sem_inc(s.ex_ready, 1)
            for ch in range(NT):
                if ch >= 2:
                    act.wait_ge(s.L_ready, ch - 1)
                empty(E1[:, ch % 2, :], func=ACT.Exp)
                empty(E2[:, ch % 2, :], func=ACT.Exp)
                act.sem_inc(s.E_ready, 1)
            act.wait_ge(s.out_small, 64)
            for lv in range(1, 7):
                for ch in range(NT):
                    empty(A2[:, ch, :])
                    act.sem_inc(s.a2_ready, 1)
            for ch in range(NT):
                empty(E1[:, 1, :])
                act.sem_inc(s.qs_ready, 1)
                empty(E2[:, 0, :])
                act.sem_inc(s.vn_ready, 1)
                act.wait_ge(s.o_ready, ch + 1)
                step(A(rms4, rms4, ACT.Sqrt, bias=eps, scale=1.0 / P), s.orms_ready)
            b = ring.to_read()
            step(A(sdv[0], b[:, 0:32], ACT.Exp))
            step(A(sdv[1], b[:, 32:64], ACT.Copy), s.aring_free)
            act.sem_inc(s.sa_ready, 1)
            empty(sdv[2], slice(0, 32), func=ACT.Sqrt, bias=eps, scale=1.0 / P)
            act.sem_inc(s.sa_ready, 1)

            def norm(i):
                t = i // 2 if i < 2 * (NT + 1) else i - 2 * (NT + 1)
                r = slice(0, ROWS[t])
                act.wait_ge(s.ms_ready, i + 1)
                step(A(rstd[r, 0:1], ssx[r, 0:1], ACT.Sqrt, bias=eps[r, :], scale=1.0 / D), s.mr_ready)

            def transposed(t):
                for g in range(2):
                    empty(h2T[t > 0][:, 4 * g:4 * g + 4, max(t - 1, 0) * P:max(t, 1) * P])

            def scores(n):
                rows = ROWS[n]
                if n >= 2:
                    act.wait_ge(s.topk_done, PH * (n - 1))
                for g in range(4):
                    empty(sc[n % 2][0:rows, g * 512:(g + 1) * 512], rows=slice(0, rows))
                act.sem_inc(s.sc_ready, 1)

            def best_exp(count, jobs):
                for i, (n, h) in enumerate(jobs):
                    r, lane = slice(0, ROWS[n]), lanes[i]
                    act.wait_ge(s.best_ready, count + (i + 1))
                    A(lane.gexp[r, :], lane.best[r, :], ACT.Exp, bias=lane.nbest[r, :],
                      accum_out=lane.gsum[r, :]).then_inc(s.gexp_ready, 1)

            for i in range(2 * NT):
                norm(i)
            transposed(0)
            act.sem_inc(s.h2T_ready, 1)
            for m in range(B_QRY):
                if m in (0, 3):
                    norm(2 * NT + m // 3)
                empty(qryT[0][:, m, :], slice(0, P))
                if m % 4 == 3:
                    act.sem_inc(s.qry_ready, 1)
                    if m == 3:
                        act.wait_ge(s.h2_ready, NT + 1)
                    empty(sc[0][:, (m // 4) * 512:(m // 4 + 1) * 512])
                    if m in (7, B_QRY - 1):
                        act.sem_inc(s.sc_ready, 1)
                if m == 11:
                    best_exp(0, [(0, 0)])
            for t in range(1, NT):
                transposed(t)
            empty(h2T[1][:, :, SEQ - P:], slice(0, KT * NB))
            act.sem_inc(s.h2T_ready, 1)
            late, late_banks = ring.n, [ring.banks[(ring.n + i) % 2] for i in range(2)]

            def query(h, a):
                act.wait_ge(s.aring_full, h * 2 + (late + a + 1))
                b, m = late_banks[a], bass.ds(h * 2 + a, 1)
                A(qryT[1][:, m, :], b[:, 0:P].unsqueeze(1), ACT.Copy).then_inc(s.act_step, 1)
                A(qryT[2][:, m, :], b[:, P:TOK - P].unsqueeze(1), ACT.Copy).then_inc(s.aring_free, 1)

            def weigh(r, a, base):
                act.wait_ge(u_used[SLOTS - 1], r + 1)
                A(act8[:, a, :], act8[:, a, :], ACT.Gelu).then_inc(s.gelu_ready, 1)
                act.wait_ge(s.w_ready, r + 1)
                for j in range(SLOTS):
                    if not (isinstance(r, int) and r == 0):
                        act.wait_ge(v_used[j], r)
                    A(diag[:, j, 0:base.shape[1]], base, ACT.Copy, scale=w8[:, a, j:j + 1]).then_inc(s.diag_ready, 1)

            for t in range(NT):
                if 0 < t < NT - 1:
                    scores(t + 1)

                def head(h):
                    weigh(h * 2 + 2 * PH * t, 0, ident)
                    if next_heads(t, h):
                        best_exp(searched(t, h) + (1 if t < NT - 1 else 2), next_heads(t, h))
                    if t and isinstance(h, int) and h == 0:
                        norm(2 * (NT + 1) + t - 1)
                    if t == 0 and isinstance(h, int) and h == 0:
                        query(0, 0)
                        query(0, 1)
                    if t == 0 and not (isinstance(h, int) and h == PH - 1):
                        query(h + 1, 0)
                    weigh(h * 2 + (2 * PH * t + 1), 1, ident)
                    if t == 0 and not (isinstance(h, int) and h == PH - 1):
                        query(h + 1, 1)
                head(0)
                with act.Fori(1, PH - 1) as h:
                    head(h)
                if t == 0:
                    ring.n += B_QRY
                    step.n[s.aring_free.name] += B_QRY
                    step.n[s.act_step.name] += B_QRY
                    act.wait_ge(s.aring_free, step.n[s.aring_free.name])
                    act.wait_ge(s.act_step, step.n[s.act_step.name])
                    act.sem_inc(s.qry_ready, 1)
                    scores(1)
                if t == NT - 2:
                    scores(NT)
                head(PH - 1)
            weigh(2 * PH * NT, 0, consts[:, C_TK:C_TK + NB])
            norm(3 * (NT + 1) - 2)
            norm(3 * (NT + 1) - 1)

        filled = {}

        @block.tensor
        def _(pe):
            dring = Ring(pe, dbank, s.dring_full, s.dring_free)
            aring = Ring(pe, abank, s.aring_full, s.aring_free)
            stream = [0]

            def mm(out, lhsT, rhs, first=True, last=True):
                return pe.matmul(out, lhsT, rhs, start=first, stop=last)

            def weights():
                n = stream[0]
                pe.wait_ge(w_full[PLACE[n]], 16 * loads(n))
                stream[0] += 1
                return wplace[PLACE[n]].rearrange("p (k m) -> p k m", m=P)

            def block_before_used(ins):
                if stream[0] > 1:
                    ins.then_inc(s.w_used, 1)

            def project(x, parts=PARTS):
                w = weights()
                for i, (lo, hi) in enumerate(parts):
                    b = aring.to_fill()
                    for k in range(KT):
                        last = mm(b[:, 0:hi - lo], w[:, k, :], x[:, k, lo:hi], k == 0, k == KT - 1)
                        if i == 0 and k == 0:
                            block_before_used(last)
                    last.then_inc(s.aring_full, 1)

            mod_at, mod_bank = [0], [None]

            def modulation(blocks):
                for _ in range(blocks):
                    q = mod_at[0] % CHUNK
                    mod_at[0] += 1
                    if q == 0:
                        mod_bank[0] = dring.to_fill()
                    w = weights().rearrange("p k m -> p (k m)")
                    for e in range(2):
                        last = mm(mod_bank[0][0:NCOND, :], cT[:, 2 * q + e, :], w[:, e * 512:(e + 1) * 512],
                                  q == 0 and e == 0, q == CHUNK - 1 and e == 1)
                        if e == 0:
                            block_before_used(last)
                    if q == CHUNK - 1:
                        last.then_inc(s.dring_full, 1)

            pe.wait_ge(s.silu_c, 1)
            modulation(B_ADA1)
            pe.wait_ge(s.consts_in, 32)
            pe.wait_ge(s.mrow_ready, 4)
            b = dring.to_fill()
            for k in range(2 * KT):
                last = pe.transpose(b[:, NCOND * k:NCOND * (k + 1)], mrow1[:, k * P:(k + 1) * P], consts[0:NCOND, 0:NCOND])
            last.then_inc(s.dring_full, 1)
            pe.wait_ge(s.xn_ready, NT + 1)
            for k in range(KT):
                b = dring.to_fill()
                for t in range(NT):
                    last = pe.transpose(b[:, t * P:(t + 1) * P], x_t[:, t, k * P:(k + 1) * P], ident)
                last.then_inc(s.dring_full, 1)
            b = dring.to_fill()
            for k in range(KT):
                last = pe.transpose(b[:, k * NB:(k + 1) * NB], x_t[0:NB, NT, k * P:(k + 1) * P], consts[0:NB, 0:NB])
            last.then_inc(s.dring_full, 1)
            pe.wait_ge(s.hT_ready, KT + 1)
            for m in range(CT_N):
                project(hT)
                modulation(BEHIND[m])
            pe.wait_ge(s.wnat_in, 16)
            for t in range(NT + 1):
                b = aring.to_fill()
                for k in range(KT):
                    last = mm(b[0:ROWS[t], 0:NAT_W], hT[:, k, tcols(t)], wnat[:, k, :], k == 0, k == KT - 1)
                last.then_inc(s.aring_full, 1)
            for m in range(B_Q):
                project(hT)
                modulation(BEHIND[B_CONV + m])
            pe.wait_ge(s.nat_ready, NT)
            b = aring.to_fill()
            for t in range(NT):
                last = pe.transpose(b[:, t * P:(t + 1) * P], nat[:, t, 0:P], ident)
            last.then_inc(s.aring_full, 1)
            pe.wait_ge(s.rels_ready, 1)
            b = aring.to_fill()
            mm(b[0:HQ, 0:384], relx[:, :], onehot[:, :]).then_inc(s.aring_full, 1)
            for m in range(2 * DH):
                pe.wait_ge(s.sq_ready, m + 1)
                for lo, hi in PARTS:
                    b = aring.to_fill()
                    mm(b[:, 0:hi - lo], ones, sqb[:, m % 2, lo:hi]).then_inc(s.aring_full, 1)
                modulation(AHEAD[m])
                project(hT)
            pe.wait_ge(s.qT_ready, 1)
            pe.wait_ge(s.kT_ready, 1)
            for blk in range(NT):
                lo = 0 if blk else P
                for i in range(HQ // 2):
                    b = dring.to_fill()
                    for e in range(2):
                        h = 2 * i + e
                        g, rows = h % HG, slice(64 * (h // HG), 64 * (h // HG) + 64)
                        last = mm(b[:, e * 256 + lo:e * 256 + 256], qT[rows, g, blk * P:(blk + 1) * P],
                                  kT[rows, (blk - 1) * P + lo:(blk + 1) * P])
                    last.then_inc(s.dring_full, 1)
                project(hT)
                project(hT)
                pe.wait_ge(s.prob_ready, blk + 1)
                parts = [(h, c) for h in range(HQ) for c in ((1,) if blk == 0 else (0, 1))]
                for i in range(len(parts) // 4):
                    b = aring.to_fill()
                    for e, (h, c) in enumerate(parts[4 * i:4 * i + 4]):
                        last = pe.transpose(b[:, e * P:(e + 1) * P], prob[:, h, c * P:(c + 1) * P], ident)
                    last.then_inc(s.aring_full, 1)
                project(hT)
                pe.wait_ge(s.probT_ready, blk + 1)
                b = aring.to_fill()
                for i, (h, c) in enumerate(parts):
                    half = 64 * (h // HG)
                    last = mm(b[half:half + 64, (h % HG) * P:(h % HG + 1) * P],
                              nat[:, blk - 1 + c, P + half:P + half + 64], probT[:, i, :],
                              blk == 0 or c == 0, c == 1)
                last.then_inc(s.aring_full, 1)
            pe.wait_ge(s.keyc_in, 16)
            for i in range(2):
                b = aring.to_fill()
                for e in range(4):
                    last = pe.transpose(b[:, e * P:(e + 1) * P], keyc[:, 4 * i + e, :], ident)
                last.then_inc(s.aring_full, 1)
            pe.wait_ge(s.kTs_ready, 1)
            for kv in range(2):
                b = dring.to_fill()
                rows = slice(64 * kv, 64 * kv + 64)
                for q in range(NB):
                    last = mm(b[:, q * HG:(q + 1) * HG], probT[rows, q, :], qT[rows, :, SEQ + q])
                last.then_inc(s.dring_full, 1)
            b = dring.to_fill()
            mm(b[0:64, 0:P], rels[:, :], onehot[:, P:2 * P]).then_inc(s.dring_full, 1)
            pe.wait_ge(s.lt_ready, 1)
            b = dring.to_fill()
            pe.transpose(b[0:64, 0:P], lt64, ident).then_inc(s.dring_full, 1)
            pe.wait_ge(s.prob_ready, NT + 1)
            b = dring.to_fill()
            pe.transpose(b[:, 0:64], prob[0:64, 0, 0:P], consts[0:64, 0:64]).then_inc(s.dring_full, 1)
            pe.wait_ge(s.lt_ready, 2)
            pe.wait_ge(s.valc_in, 16)
            b = aring.to_fill()
            for q in range(NB):
                for kv in range(2):
                    last = mm(b[64 * kv:64 * kv + 64, q * HG:(q + 1) * HG], valc[:, q, 64 * kv:64 * kv + 64],
                              lt64[:, q * HQ + kv * HG:q * HQ + kv * HG + HG])
            last.then_inc(s.aring_full, 1)
            pe.wait_ge(s.g_ready, 1)
            b = aring.to_fill()
            for i, tri in enumerate((le, gt, ones)):
                last = mm(b[:, 16 * i:16 * i + 16], tri, gg[:, 0:NT, :])
            last.then_inc(s.aring_full, 1)
            pe.wait_ge(s.l2_done, 2 * DH)
            for ch in range(NT):
                for first in (DH, 2 * DH):
                    b = dring.to_fill()
                    for h in range(DH):
                        last = pe.transpose(b[:, h * P:(h + 1) * P], ct[:, first + h, ch * P:(ch + 1) * P], ident)
                    last.then_inc(s.dring_full, 1)
            for ch in range(NT):
                here = slice(ch * P, (ch + 1) * P)
                pe.wait_ge(s.mg_ready, ch + 1)
                b = aring.to_fill()
                mm(b[:, :], le, mgt[:, ch % 2, :]).then_inc(s.aring_full, 1)
                b = aring.to_fill()
                for h in range(DH):
                    last = mm(b[:, h * P:(h + 1) * P], mgt[:, ch % 2, h * P:(h + 1) * P], le)
                last.then_inc(s.aring_full, 1)
                for right in (DH, 0):
                    b = dring.to_fill()
                    for h in range(DH):
                        last = mm(b[:, h * P:(h + 1) * P], ct[:, DH + h, here], ct[:, right + h, here])
                    last.then_inc(s.dring_full, 1)
            for ch in range(NT):
                pe.wait_ge(s.lm_ready, ch + 1)
                b = dring.to_fill()
                for h in range(DH):
                    last = pe.transpose(b[:, h * P:(h + 1) * P], Lm[:, ch, h * P:(h + 1) * P], ident)
                last.then_inc(s.dring_full, 1)
            for lv in range(1, 7):
                for ch in range(NT):
                    pe.wait_ge(s.lm_ready, NT * lv + ch + 1)
                    pe.wait_ge(s.wt_ready, NT * (lv - 1) + ch + 1)
                    b = aring.to_fill()
                    for h in range(DH):
                        hs = slice(h * P, (h + 1) * P)
                        last = mm(b[:, hs], Lm[:, ch, hs], Wc[:, ch, hs])
                    last.then_inc(s.aring_full, 1)
                for ch in range(NT):
                    pe.wait_ge(s.a2_ready, NT * (lv - 1) + ch + 1)
                    for left, right in ((Tc, A2), (A2, Tc)) if lv < 6 else ((Tc, A2),):
                        b = dring.to_fill()
                        for h in range(DH):
                            hs = slice(h * P, (h + 1) * P)
                            last = mm(b[:, hs], left[:, ch, hs], right[:, ch, hs])
                        last.then_inc(s.dring_full, 1)
            pe.wait_ge(s.wt_ready, NT * 7)
            def outputs(ch):
                pe.wait_ge(s.on_ready, ch + 1)
                b = dring.to_fill()
                for h in range(DH):
                    last = pe.transpose(b[:, h * P:(h + 1) * P], E2[:, 1, h * P:(h + 1) * P], ident)
                last.then_inc(s.dring_full, 1)

            for ch in range(NT):
                def per_head(ring, full, left, right):
                    b = ring.to_fill()
                    for h in range(DH):
                        last = mm(b[:, h * P:(h + 1) * P], left(h), right[:, h * P:(h + 1) * P])
                    last.then_inc(full, 1)
                here = slice(ch * P, (ch + 1) * P)
                pe.wait_ge(s.S_ready, ch + 1)
                per_head(dring, s.dring_full, lambda h: ct[:, DH + h, here], delta)
                per_head(aring, s.aring_full, lambda h: ct[:, h, here], delta)
                if ch:
                    outputs(ch - 1)
                pe.wait_ge(s.r_ready, ch + 1)
                per_head(aring, s.aring_full, lambda h: Wc[:, ch, h * P:(h + 1) * P], E1[:, 0, :])
                pe.wait_ge(s.vn_ready, ch + 1)
                per_head(dring, s.dring_full, lambda h: kdec[:, ch, h * P:(h + 1) * P], E2[:, 0, :])
                per_head(dring, s.dring_full, lambda h: ATc[:, ch, h * P:(h + 1) * P], E2[:, 0, :])
            outputs(NT - 1)
            pe.wait_ge(s.sg_ready, 1)
            b = aring.to_fill()
            mm(b[:, 0:64], consts[0:NB, C_ONE:C_ONE + P], at(E0 + 1832 + 32 * 3, 64)[0:NB, :]).then_inc(s.aring_full, 1)
            pe.wait_ge(s.sdel_in, 16)
            b = dring.to_fill()
            for h in range(DH):
                for q in range(NB):
                    c0 = 2 * (h * NB + q)
                    last = mm(b[:, c0:c0 + 2], sdel[:, h, q, :], ct[:, h:h + DH + 1:DH, SEQ + q])
            last.then_inc(s.dring_full, 1)
            pe.wait_ge(s.sp_ready, 1)
            b = dring.to_fill()
            mm(b[:, 0:32], ones, sdv[5]).then_inc(s.dring_full, 1)
            b = dring.to_fill()
            for h in range(DH):
                last = pe.transpose(b[0:NB, h * P:(h + 1) * P], sdv[12][:, h * NB:(h + 1) * NB], ident)
            last.then_inc(s.dring_full, 1)
            pe.wait_ge(s.sn_ready, 1)
            b = dring.to_fill()
            for h in range(DH):
                last = pe.transpose(b[0:NB, h * P:(h + 1) * P], sdv[8][:, h * NB:(h + 1) * NB], ident)
            last.then_inc(s.dring_full, 1)
            pe.wait_ge(s.sn_ready, 2)
            b = aring.to_fill()
            mm(b[:, 0:32], ones, sdv[10]).then_inc(s.aring_full, 1)
            pe.wait_ge(s.att_done, 1)
            pe.wait_ge(s.od_done, NT + 1)
            for m in range(B_BR):
                w = weights()
                for lo, hi in PARTS:
                    for k0, x in ((0, attT), (4, odT)):
                        b = dring.to_fill()
                        for k in range(4):
                            last = mm(b[:, 0:hi - lo], w[:, k0 + k, :], x[:, k, lo:hi], k == 0, k == 3)
                            if lo == 0 and k0 == 0 and k == 0:
                                block_before_used(last)
                        last.then_inc(s.dring_full, 1)
                if m < DH:
                    pe.wait_ge(s.vd_ready, m + 1)
                    for g in range(2):
                        b = dring.to_fill()
                        mm(b[:, :], kn8[:, m * P:(m + 1) * P], at(R0 + 1024 * (m % 2), 1024)[0:NB, g * 512:(g + 1) * 512]).then_inc(s.dring_full, 1)

            def mix(t):
                for g in range(2):
                    b = dring.to_fill()
                    for k in range(KT):
                        last = mm(b[0:ROWS[t], :], gaT[:, k, tcols(t)], wout[:, k, g * 512:(g + 1) * 512], k == 0, k == KT - 1)
                    last.then_inc(s.dring_full, 1)

            def transposed(t):
                pe.wait_ge(s.h2_ready, t + 1)
                for g in range(2):
                    b = aring.to_fill()
                    for j in range(4):
                        last = pe.transpose(b[:, j * P:(j + 1) * P], h2[:, t, (4 * g + j) * P:(4 * g + j + 1) * P], ident)
                    last.then_inc(s.aring_full, 1)

            def scores(n, groups=range(4)):
                q, lo = qryT[min(n, 2)], max(COL[n] - CUT, 0)
                for g in groups:
                    b = aring.to_fill()
                    for e in range(4):
                        m = 4 * g + e
                        last = mm(b[0:ROWS[n], e * P:(e + 1) * P], q[:, m, lo:lo + ROWS[n]], skt[:, m % 2, :])
                    last.then_inc(s.aring_full, 1)

            pe.wait_ge(s.merged_ready, KT)
            pe.wait_ge(s.wout_in, 16)
            for t in range(NT + 1):
                mix(t)
            transposed(0)
            pe.wait_ge(s.h2T_ready, 1)
            pe.wait_ge(s.skt_in, 16)
            for m in range(B_QRY):
                project(h2T[0], ((0, P),))
                filled[stream[0] - 1] = aring.n
                if m % 4 == 3:
                    pe.wait_ge(s.qry_ready, m // 4 + 1)
                    scores(0, [m // 4])
            for t in range(1, NT):
                transposed(t)
            pe.wait_ge(s.h2_ready, NT + 1)
            b = aring.to_fill()
            for k in range(KT):
                last = pe.transpose(b[:, k * NB:(k + 1) * NB], h2s[0:NB, k * P:(k + 1) * P], consts[0:NB, 0:NB])
            last.then_inc(s.aring_full, 1)
            pe.wait_ge(s.h2T_ready, 2)

            late, late_banks = aring.n, [aring.banks[(aring.n + i) % 2] for i in range(2)]

            def query(h, a):
                w = wplace[2 + a].rearrange("p (k m) -> p k m", m=P)
                pe.wait_ge(w_full[2 + a], h * 16 + 16 * loads(N_FIRST + a))
                pe.wait_ge(s.aring_free, h * 2 + (late + a - 1))
                for k in range(KT):
                    last = mm(late_banks[a][:, 0:TOK - P], w[:, k, :], h2T[1][:, k, :], k == 0, k == KT - 1)
                    if k == 0:
                        block_before_used(last)
                last.then_inc(s.aring_full, 1)

            filled.update((N_FIRST + m, late + m + 1) for m in range(B_QRY))
            query(0, 0)
            query(0, 1)

            def clear(n):
                if n == 1:
                    pe.wait_ge(s.dring_free, dring.n)
                if n >= 2:
                    pe.wait_ge(s.f_read, n - 1)
                for g in range(2):
                    pe.matmul(fsum[n % 2][g][:, :], zeros[:, :], consts[:, 0:512], start=True, stop=False, skip_group_check=True)

            def add_round(n, r, cols_):
                for j in range(SLOTS):
                    pe.wait_ge(s.diag_ready, r * SLOTS + (j + 1))
                    pe.wait_ge(v_in[j], r * 16 + 16)
                    for g in range(2):
                        last = pe.matmul(fsum[n % 2][g][0:cols_, :], diag[:, j, 0:cols_], vring[j][:, g * 512:(g + 1) * 512],
                                         start=False, stop=False, skip_group_check=True)
                    last.then_inc(v_used[j], 1)

            for t in range(NT):
                if 0 < t < NT - 1:
                    scores(t + 1)
                clear(t)

                def head(h):
                    for a in range(2):
                        add_round(t, h * 2 + (2 * PH * t + a), P)
                        if t == 0 and not (isinstance(h, int) and h == PH - 1):
                            query(h + 1, a)
                with pe.Fori(0, PH - 1) as h:
                    head(h)
                if t == 0:
                    aring.n += B_QRY
                    pe.wait_ge(s.qry_ready, 5)
                    scores(1)
                if t == NT - 2:
                    scores(NT)
                head(PH - 1)
                if t == 0:
                    for g in range(2):
                        b = dring.to_fill()
                        mm(b[:, :], consts[0:NB, C_KT:C_KT + P], h2s[0:NB, g * 512:(g + 1) * 512]).then_inc(s.dring_full, 1)
            clear(NT)
            add_round(NT, 2 * PH * NT, NB)

        @block.sync
        def _(sp):
            for n, place in enumerate(PLACE):
                if n > N_FIRST:
                    sp.wait_ge(s.aring_full, filled[n - 2])
                elif place in PLACE[:n]:
                    sp.wait_ge(s.w_used, n - PLACE[:n][::-1].index(place))
                if n == N_FIRST - B_QRY:
                    sp.wait_ge(s.od_done, NT + 1)
                    sp.dma_start(wout, I["wout"]).then_inc(s.wout_in, 16)
                sp.dma_start(wplace[place], I["wstream"][n if n < N_FIRST else n - B_QRY]).then_inc(w_full[place], 16)
            for t in range(NT + 1):
                if t == NT - 1:
                    sp.wait_ge(s.topk_done, PH * (NT + 1))
                    for src, tmp in ((eidx, "sidx"), (gate, "sgate")):
                        sp.dma_start(I[tmp], src[0:NB, NT % 2, :]).then_inc(s.sel_out, 16)
                    sp.wait_ge(s.sel_out, 32)
                    for dst, tmp in ((sidx, "sidx"), (sgate, "sgate")):
                        for b in range(NB):
                            sp.dma_start(dst[b * TOPK:(b + 1) * TOPK, :],
                                           I[tmp][b, :].rearrange("(h k) -> k h", k=TOPK), allow_slow_non_contiguous=True).then_inc(s.sel_in, 16)
                sp.wait_ge(s.y_ready, t + 1)
                out = O["yp"][t * P:(t + 1) * P, :] if t < NT else O["ys"]
                sp.dma_start(out, x_t[0:ROWS[t], t, :]).then_inc(s.out_y, 16)
            sp.wait_ge(s.out_y, 16 * (NT + 1))

        @block.vector
        def _(dve):
            step = Steps(dve, s.dve_step)
            ring = Ring(dve, dbank, s.dring_full, s.dring_free)
            TT, TS, STT, TTR = dve.tensor_tensor, dve.tensor_scalar, dve.scalar_tensor_tensor, dve.tensor_tensor_reduce
            copy, recip = dve.tensor_copy, dve.reciprocal

            def bc(v, axis, n):
                shape = list(v.shape)
                shape.insert(axis, n)
                return v.unsqueeze(axis).to_broadcast(shape)

            def three(v, q=P):
                return v.rearrange("p (a q) -> p a q", q=q)

            step(dve.memset(ubuf, 0.0))
            step(dve.memset(eps, EPS))
            step(dve.memset(eps128, EPS * P))
            step(dve.memset(nat[:, NT, :], 0.0))
            step(dve.memset(zeros[:, :], 0.0))
            step(dve.memset(relx[32:33, :], NEG))
            dve.wait_ge(s.x_in, 32)
            for t in range(NT + 1):
                r = slice(0, ROWS[t])
                step(TTR(junk[r, :], x_t[r, t, :], x_t[r, t, :], 1.0, 0.0, ALU.mult, ALU.add, ssx[r, t:t + 1]), s.ss_ready)
            for t in range(NT + 1):
                dve.wait_ge(s.rms_ready, t + 1)
                step(recip(rstd[0:ROWS[t], t:t + 1], rstd[0:ROWS[t], t:t + 1]), s.rstd_ready)

            def modulation(c):
                v, half = c // 2, slice(512 * c, 512 * (c + 1))
                out, bias_ = (mrow1[:, half], brow1[:, half]) if v < 2 else (
                    mrow2[:, 512 * (c - 4):512 * (c - 3)], brow2[:, 512 * (c - 4):512 * (c - 3)])
                gain = {1: 0, 2: 1, 4: 2, 5: 3}.get(v)
                done = s.mrow_ready if v < 2 else s.mrows_ready
                b = ring.to_read()
                if gain is None:
                    step(TT(out, b[0:NCOND, :], bias_, ALU.add), s.dring_free)
                    dve.sem_inc(done, 1)
                else:
                    g = grow[:, gain * D + 512 * (c % 2):gain * D + 512 * (c % 2) + 512]
                    step(TT(out, b[0:NCOND, :], bias_, ALU.add), s.dring_free)
                    step(STT(out, out, 1.0 if v in (1, 4) else 0.0, g, ALU.add, ALU.mult), done)

            dve.wait_ge(s.rows_in, 32)
            for c in range(4):
                modulation(c)
            b = ring.to_read()
            step(copy(adaT[:, :, :], b[:, 0:2 * KT * NCOND].rearrange("p (k c) -> p k c", c=NCOND)), s.dring_free)
            for k in range(KT):
                b = ring.to_read()
                step(TS(hT[:, k, 0:SEQ], b[:, :], adaT[:, KT + k, 0:1], adaT[:, k, 0:1], ALU.mult, ALU.add), s.dring_free)
                dve.sem_inc(s.hT_ready, 1)
            b = ring.to_read()
            step(TT(hT[:, :, SEQ:TOK], three(b[:, 0:KT * NB], NB), adaT[:, KT:2 * KT, 1:9], ALU.mult), s.dring_free)
            step(TT(hT[:, :, SEQ:TOK], hT[:, :, SEQ:TOK], adaT[:, 0:KT, 1:9], ALU.add), s.hT_ready)
            dve.wait_ge(s.cols_in, 32)
            step(copy(rels[:, :].rearrange("p (b h) -> p b h", h=HQ), bc(relx[:, :], 1, NB)), s.rels_ready)
            dve.wait_ge(s.cst_in, 16)
            dve.wait_ge(s.brow_in, 16)
            for m in range(CT_N):
                if m in (5, 9):
                    modulation(4 + m // 8)
                dve.wait_ge(s.conv_in, m + 1)
                u = ubuf[:, m % 2, :]
                us = u[:, 515:547].rearrange("p (b i) -> p b i", i=4)
                step(copy(us[:, :, 0:3], cst[:, m, :, :]))
                step(copy(cpo[:, m, :], u[:, SEQ:SEQ + 3]))
                step(copy(cso[:, m, :, :], us[:, :, 1:4]))
                for i in range(4):
                    w = cols[:, K_CONV + 4 * m + i:K_CONV + 4 * m + i + 1]
                    for out, src in ((ct[:, m, 0:SEQ], u[:, i:i + SEQ]), (ct[:, m, SEQ:TOK], us[:, :, i])):
                        if i == 0:
                            step(TS(out, src, w, None, ALU.mult))
                        elif i < 3 or out.shape[1] == SEQ:
                            step(STT(out, src, w, out, ALU.mult, ALU.add))
                        else:
                            step(STT(out, src, w, out, ALU.mult, ALU.add), s.conv_out)
            modulation(6)
            for m in range(2 * DH + 1):
                if m < 2 * DH:
                    dve.wait_ge(s.silu_out, m + 1)
                    step(TT(sqb[:, m % 2, :], ct[:, m, :], ct[:, m, :], ALU.mult), s.sq_ready)
                if m == 1:
                    modulation(7)
                    modulation(8)
                if m >= 1:
                    dve.wait_ge(s.rn_ready, m)
                    r = rnb[:, (m - 1) % 2, :]
                    step(recip(r, r))
                    step(TT(ct[:, m - 1, :], ct[:, m - 1, :], r, ALU.mult), s.l2_done)
            for c in range(9, 12):
                modulation(c)
            dve.wait_ge(s.nat_ready, NT + 1)
            step(TT(gtmp, nat[:, :, 256:260], bc(cols[:, K_DT:K_DT + 4], 1, NT + 1), ALU.add), s.gx_ready)
            dve.wait_ge(s.beta_ready, 1)
            step(STT(gg, gtmp, 0.0, gtmp2, ALU.max, ALU.add))
            step(STT(gg, gg, -1.0, bc(ealog, 1, NT + 1), ALU.mult, ALU.mult), s.g_ready)
            dve.wait_ge(s.bias_in, 16)
            for blk in range(NT):
                lo = 0 if blk else P
                if blk:
                    dve.wait_ge(s.probT_ready, blk)
                for i in range(HQ // 2):
                    b = ring.to_read()
                    step(STT(prob[:, 2 * i:2 * i + 2, lo:256], three(b[:, :], 256)[:, :, lo:256], HD ** -0.5,
                             bias[:, 2 * i:2 * i + 2, lo:256], ALU.mult, ALU.add), s.dring_free)
                step(dve.tensor_reduce(mx8, prob[:, :, lo:256], AX.X, ALU.max))
                step(TT(mx8, mx8, cols[:, K_SINK:K_SINK + 8], ALU.max))
                step(TT(es8, cols[:, K_SINK:K_SINK + 8], mx8, ALU.subtract))
                step(TS(nm8, mx8, -1.0, None, ALU.mult), s.nm_ready)
                dve.wait_ge(s.exp_done, blk + 1)
                step(TT(sm8, sm8, es8, ALU.add))
                step(recip(sm8, sm8))
                step(TT(prob[:, :, lo:256], prob[:, :, lo:256], bc(sm8, 2, 256 - lo), ALU.mult), s.prob_ready)
            dve.wait_ge(s.probT_ready, NT)
            for kv in range(2):
                b = ring.to_read()
                step(TS(lt64.rearrange("p (q v g) -> p q v g", v=2, g=HG)[:, :, kv, :], three(b[:, 0:NB * HG], HG), HD ** -0.5, None, ALU.mult), s.dring_free)
            dve.sem_inc(s.lt_ready, 1)
            q0 = prob[0:64, 0, 0:P]
            b = ring.to_read()
            step(copy(q0, b[0:64, 0:P]), s.dring_free)
            b = ring.to_read()
            step(TT(q0, b[0:64, 0:P], q0, ALU.add), s.dring_free)
            mx, nm, sm_, es, sink = mx8[0:64, 0:1], nm8[0:64, 0:1], sm8[0:64, 0:1], es8[0:64, 0:1], cols[0:64, K_SINKS:K_SINKS + 1]
            step(dve.tensor_reduce(mx, q0, AX.X, ALU.max))
            step(TT(mx, mx, sink, ALU.max))
            step(TT(es, sink, mx, ALU.subtract))
            step(TS(nm, mx, -1.0, None, ALU.mult), s.nm_ready)
            dve.wait_ge(s.exp_done, NT + 1)
            step(TT(sm_, sm_, es, ALU.add))
            step(recip(sm_, sm_))
            step(TS(q0, q0, sm_, None, ALU.mult), s.prob_ready)
            b = ring.to_read()
            step(copy(lt64, b[:, 0:64]), s.dring_free)
            dve.sem_inc(s.lt_ready, 1)
            step(copy(three(svv, NB), ct[:, 2 * DH:3 * DH, SEQ:TOK]))
            dve.wait_ge(s.ex_ready, 1)
            for ch in range(NT):
                b = ring.to_read()
                step(TT(three(kdec[:, ch, :]), three(b[:, :]), bc(ex[:, 16 + 4 * ch:20 + 4 * ch], 2, P), ALU.mult), s.dring_free)
                b = ring.to_read()
                step(TT(three(vb[:, ch, :]), three(b[:, :]), bc(beta[:, ch, :], 2, P), ALU.mult), s.dring_free)
            step(STT(three(nbeg, DH), three(ex[:, 0:16], DH), -1.0, beta[:, 0:NT, :], ALU.mult, ALU.mult))

            def spread(ch):
                step(TT(three(mgt[:, ch % 2, :]), bc(gt, 1, DH), bc(gg[:, ch, :], 2, P), ALU.mult), s.mg_ready)

            spread(0)
            for ch in range(NT):
                if ch + 1 < NT:
                    spread(ch + 1)
                dve.wait_ge(s.E_ready, ch + 1)
                e1, e2 = three(E1[:, ch % 2, :]), three(E2[:, ch % 2, :])
                step(TT(e1, e1, bc(gt, 1, DH), ALU.mult))
                step(TT(e1, e1, bc(beta[:, ch, :], 2, P), ALU.mult))
                b = ring.to_read()
                step(TT(Lc[:, ch, :], b[:, :], E1[:, ch % 2, :], ALU.mult), s.dring_free)
                step(TT(e2, e2, bc(le, 1, DH), ALU.mult))
                b = ring.to_read()
                step(TT(ATc[:, ch, :], b[:, :], E2[:, ch % 2, :], ALU.mult), s.dring_free)
                dve.sem_inc(s.L_ready, 1)
            def masked(lv, ch):
                mask = consts[:, C_LVL + lv * P:C_LVL + (lv + 1) * P]
                step(TT(three(Lm[:, ch, :]), three(Lc[:, ch, :]), bc(mask, 1, DH), ALU.mult), s.lm_ready)

            for ch in range(NT):
                masked(0, ch)
            for lv in range(7):
                for ch in range(NT):
                    if lv == 0:
                        step(TT(three(Tc[:, ch, :]), bc(ident, 1, DH), three(Lm[:, ch, :]), ALU.subtract))
                        b = ring.to_read()
                        step(TT(three(Wc[:, ch, :]), bc(ident, 1, DH), three(b[:, :]), ALU.subtract), s.dring_free)
                    else:
                        b = ring.to_read()
                        step(TT(Wc[:, ch, :], Wc[:, ch, :], b[:, :], ALU.subtract), s.dring_free)
                        if lv < 6:
                            b = ring.to_read()
                            step(TT(Tc[:, ch, :], Tc[:, ch, :], b[:, :], ALU.subtract), s.dring_free)
                    dve.sem_inc(s.wt_ready, 1)
                    if lv < 6:
                        masked(lv + 1, ch)
            R, qs, o = E1[:, 0, :], E1[:, 1, :], E2[:, 1, :]
            def gated(ch):
                here = slice(ch * P, (ch + 1) * P)
                b = ring.to_read()
                step(STT(odT[:, :, here], three(b[:, :]), cols[:, K_DN:K_DN + 1], zT[:, :, here], ALU.mult, ALU.mult), s.dring_free)
                dve.sem_inc(s.od_done, 1)

            step(dve.memset(delta[:, :], 0.0), s.S_ready)
            for ch in range(NT):
                cs = slice(4 * ch, 4 * ch + 4)
                b = ring.to_read()
                step(TT(three(R), three(b[:, :]), bc(nbeg[:, cs], 2, P), ALU.mult), s.dring_free)
                step(TT(R, R, vb[:, ch, :], ALU.add), s.r_ready)
                if ch:
                    gated(ch - 1)
                dve.wait_ge(s.qs_ready, ch + 1)
                step(TT(three(o), three(qs), bc(ex[:, cs], 2, P), ALU.mult))
                step(TT(three(delta[:, :]), three(delta[:, :]), bc(ex[:, 32 + 4 * ch:36 + 4 * ch], 2, P), ALU.mult))
                b = ring.to_read()
                step(TT(delta[:, :], delta[:, :], b[:, :], ALU.add), s.dring_free)
                dve.sem_inc(s.S_ready, 1)
                b = ring.to_read()
                step(TT(o, o, b[:, :], ALU.add), s.dring_free)
                step(TT(R, o, o, ALU.mult))
                step(dve.tensor_reduce(rms4, three(R), AX.X, ALU.add), s.o_ready)
                dve.wait_ge(s.orms_ready, ch + 1)
                step(recip(rms4, rms4))
                step(TT(three(o), three(o), bc(rms4, 2, P), ALU.mult), s.on_ready)
            gated(NT - 1)
            eg, be, rr, sgx, prod, ks_, qs_, vn, oo, oo2 = sdv[0], sdv[1], sdv[2], at(E0 + 1832 + 96, 64), sdv[5], sdv[6], sdv[7], sdv[8], sdv[9], sdv[10]
            i8 = consts[0:NB, 0:NB]
            for i, v in enumerate((gg, beta)):
                step(TT(three(sgx[0:NB, 32 * i:32 * i + 32], NB), bc(v[0:NB, NT, :], 2, NB), bc(i8, 1, DH), ALU.mult), s.dve_step if i == 0 else s.sg_ready)
            step(copy(three(sdv[12], NB), ct[:, DH:2 * DH, SEQ:TOK]))
            step(TT(three(prod, NB), ct[:, 0:DH, SEQ:TOK], three(sdv[12], NB), ALU.mult), s.sp_ready)
            dve.wait_ge(s.sa_ready, 1)
            b = ring.to_read()
            kq = b[:, 0:64].rearrange("p (c z) -> p c z", z=2)
            step(TT(ks_, kq[:, :, 1], eg, ALU.mult))
            step(TT(qs_, kq[:, :, 0], eg, ALU.mult), s.dring_free)
            step(TT(vn, svv, ks_, ALU.subtract))
            step(TT(vn, vn, be, ALU.mult), s.sn_ready)
            b = ring.to_read()
            step(TT(oo, b[:, 0:32], vn, ALU.mult), s.dring_free)
            step(TT(oo, oo, qs_, ALU.add))
            step(TT(oo2, oo, oo, ALU.mult), s.sn_ready)
            b = ring.to_read()
            step(copy(kn8, b[0:NB, :]), s.dring_free)
            b = ring.to_read()
            step(copy(vn8, b[0:NB, :]), s.dring_free)
            dve.wait_ge(s.sa_ready, 2)
            step(recip(rr, rr))
            step(TT(oo, oo, rr, ALU.mult))
            step(STT(odT[:, :, SEQ:TOK], three(oo, NB), cols[:, K_DN:K_DN + 1], zT[:, :, SEQ:TOK], ALU.mult, ALU.mult), s.od_done)
            def state(h):
                vd = at(R0 + 1024 * (h % 2), NB, P)[0:NB]
                step(TT(vd, bc(vn8[:, h * P:(h + 1) * P], 1, NB), bc(i8, 2, P), ALU.mult), s.vd_ready)
                for g in range(2):
                    st = sdel[:, h, 4 * g:4 * g + 4, :]
                    step(TT(st, st, bc(eg[:, h * NB + 4 * g:h * NB + 4 * g + 4], 2, P), ALU.mult))

            def state_sum(h):
                for g in range(2):
                    st = sdel[:, h, 4 * g:4 * g + 4, :]
                    b = ring.to_read()
                    step(TT(st, st, three(b[:, :]), ALU.add), s.dring_free)
                if h == DH - 1:
                    dve.sem_inc(s.sd_ready, 1)

            for m in range(KT):
                if m < DH:
                    state(m)
                for lo, hi in PARTS:
                    for g in (gaT, gbT):
                        v = g[:, m, lo:hi]
                        b = ring.to_read()
                        step(TT(v, v, b[:, 0:hi - lo], ALU.mult), s.dring_free)
                step(TT(gaT[:, m, :], gaT[:, m, :], gbT[:, m, :], ALU.add), s.merged_ready)
                if m < DH:
                    state_sum(m)
            dve.wait_ge(s.out_small, 64)
            dve.wait_ge(s.mod_in, 128)

            def mean_square(src, r, k):
                step(TTR(t2[r, :], src, src, 1.0, 0.0, ALU.mult, ALU.add, ssx[r, 0:1]), s.ms_ready)
                dve.wait_ge(s.mr_ready, k)
                step(recip(rstd[r, 0:1], rstd[r, 0:1]))

            dve.wait_ge(s.xr_in, 32)

            def residual(t):
                r = slice(0, ROWS[t])
                g1, a2, s2 = (v_g1, v_a2, v_s2) if t < NT else (s_g1, s_a2, s_s2)
                h = h2[r, t, :] if t < NT else h2s[r, :]
                for g in range(2):
                    b = ring.to_read()
                    step(copy(t1[r, g * 512:(g + 1) * 512], b[r, :]), s.dring_free)
                mean_square(t1[r, :], r, 2 * t + 1)
                step(STT(t1[r, :], t1[r, :], rstd[r, 0:1], g1[r, :], ALU.mult, ALU.mult))
                step(TT(x_t[r, t, :], x_t[r, t, :], t1[r, :], ALU.add))
                mean_square(x_t[r, t, :], r, 2 * t + 2)
                step(STT(h, x_t[r, t, :], rstd[r, 0:1], a2[r, :], ALU.mult, ALU.mult))
                step(TT(h, h, s2[r, :], ALU.add), s.h2_ready)

            def search(jobs, count, base):
                looped = not isinstance(base, int)
                steps_done = [0]
                last = {}

                def after(*keys, bare=False):
                    dve.wait_ge(s.dve_step, base + max(last.get(k, 0) for k in keys))
                    if bare and looped:
                        dve.sem_inc(s.dve_turn, 1)

                def did(key, ins):
                    ins.then_inc(s.dve_step, 1)
                    steps_done[0] += 1
                    last[key] = steps_done[0]

                def sixteen(chains):
                    for key, val, idx, src, spare in chains:
                        after(key, bare=True)
                        did(key, dve.max(val[:, 0:8], src))
                    for key, val, idx, src, spare in chains:
                        after(key, bare=True)
                        did(key, dve.max_index(idx[:, 0:8], val[:, 0:8], src))
                    for key, val, idx, src, spare in chains:
                        after(key, bare=True)
                        did(key, dve.match_replace(spare, val[:, 0:8], src, -3e38))
                    for key, val, idx, src, spare in chains:
                        after(key, bare=True)
                        did(key, dve.max(val[:, 8:16], spare))
                    for key, val, idx, src, spare in chains:
                        after(key, bare=True)
                        did(key, dve.max_index(idx[:, 8:16], val[:, 8:16], spare))

                H = [(i, n, slice(0, ROWS[n]), h, lanes[i]) for i, (n, h) in enumerate(jobs)]
                for i, n, r, h, q in H:
                    after(i)
                    did(i, copy(q.s_in[r].rearrange("p a q -> p (a q)"), sc[n % 2][r, bass.ds(h * (2 * NKEY), 2 * NKEY)]))
                    last[i, 0] = last[i, 1] = last[i]
                sixteen([((i, p), q.sv[r, p, :], q.si[r, p, :], q.s_in[r, p, :], q.s_out[r, p, :]) for i, n, r, h, q in H for p in range(2)])
                for i, n, r, h, q in H:
                    after((i, 0), (i, 1))
                    did(i, TT(three(q.cand[r, :], TOPK), bc(q.sv[r, 0, :], 2, TOPK), bc(q.sv[r, 1, :], 1, TOPK), ALU.add))
                sixteen([(i, q.best[r, :], q.pos[r, :], q.cand[r, :], q.cand2[r, :]) for i, n, r, h, q in H])
                for i, n, r, h, q in H:
                    after(i)
                    TS(q.nbest[r, :], q.best[r, 0:1], -1.0, None, ALU.mult).then_inc(s.best_ready, 1)
                for i, n, r, h, q in H:
                    did(i, copy(q.sif[r], q.si[r]))
                    did((i, 0), TS(q.pint[r, 0, :], q.pos[r, :], 4, None, ALU.logical_shift_right))
                    did((i, 1), TS(q.pint[r, 1, :], q.pos[r, :], 15, None, ALU.bitwise_and))
                for i, n, r, h, q in H:
                    after((i, 0), (i, 1))
                    did((i, 0), copy(q.pf[r], q.pint[r]))
                for i, n, r, h, q in H:
                    after((i, 0))
                    did((i, 0), TT(q.hit[r].rearrange("p a k i -> p (a k) i"), bc(q.pf[r].rearrange("p a k -> p (a k)"), 2, TOPK),
                                   bc(consts[r, C_IOTA:C_IOTA + TOPK], 1, 2 * TOPK), ALU.is_equal))
                for i, n, r, h, q in H:
                    after((i, 0))
                    did((i, 0), TT(q.hit[r], q.hit[r], bc(q.sif[r], 2, TOPK), ALU.mult))
                for i, n, r, h, q in H:
                    after((i, 0))
                    did((i, 0), dve.tensor_reduce(q.ee[r], q.hit[r], AX.X, ALU.add))
                for i, n, r, h, q in H:
                    after((i, 0))
                    did((i, 0), STT(q.ef[r, :], q.ee[r, 0, :], float(NKEY), q.ee[r, 1, :], ALU.mult, ALU.add))
                for i, n, r, h, q in H:
                    dve.wait_ge(s.gexp_ready, count + (i + 1))
                    did(i, recip(q.gsum[r, :], q.gsum[r, :]))
                for i, n, r, h, q in H:
                    after((i, 0))
                    did((i, 0), copy(eidx[r, n % 2, bass.ds(h * TOPK, TOPK)], q.ef[r, :]))
                for i, n, r, h, q in H:
                    after(i, (i, 0))
                    TS(gate[r, n % 2, bass.ds(h * TOPK, TOPK)], q.gexp[r, :], q.gsum[r, 0:1], None, ALU.mult).then_inc(s.topk_done, 1)
                dve.wait_ge(s.topk_done, count + len(jobs))
                return steps_done[0]

            def dots(r, a, x, g):
                for j in range(SLOTS):
                    dve.wait_ge(u_in[j], r * 16 + 16)
                    TTR(uring[j], uring[j], x, 1.0, 0.0, ALU.mult, ALU.add, act8[:, a, j:j + 1]).then_inc(u_used[j], 1)
                dve.wait_ge(s.gelu_ready, r + 1)
                TT(w8[:, a, :], act8[:, a, :], g, ALU.mult).then_inc(s.w_ready, 1)

            steps = [0]

            def next_step(ins):
                ins.then_inc(s.dve_step, 1)
                steps[0] += 1
                dve.wait_ge(s.dve_step, steps[0])

            def finish(t, g2):
                r = slice(0, ROWS[t])
                dve.wait_ge(v_used[SLOTS - 1], 2 * PH * (t + 1) if t < NT else 2 * PH * NT + 1)
                next_step(copy(t1[r, 0:512], fsum[t % 2][0][r, :]))
                step(copy(t1[r, 512:1024], fsum[t % 2][1][r, :]), s.f_read)
                step(TTR(t2[r, :], t1[r, :], t1[r, :], 1.0, 0.0, ALU.mult, ALU.add, ssx[r, 0:1]), s.ms_ready)
                dve.wait_ge(s.mr_ready, 2 * (NT + 1) + t + 1)
                next_step(recip(rstd[r, 0:1], rstd[r, 0:1]))
                next_step(STT(t1[r, :], t1[r, :], rstd[r, 0:1], g2[r, :], ALU.mult, ALU.mult))
                step(TT(x_t[r, t, :], x_t[r, t, :], t1[r, :], ALU.add), s.y_ready)

            for t in range(NT + 1):
                residual(t)
            dve.wait_ge(s.sc_ready, 1)
            steps[0] = step.n[s.dve_step.name]
            steps[0] += search([(0, 0)], 0, steps[0])

            for t in range(NT):
                lanes_in_use = 1 + (t == NT - 1)

                def head(h, base):
                    for a in range(2):
                        r = h * 2 + (2 * PH * t + a)
                        if not (isinstance(r, int) and r == 0):
                            dve.wait_ge(s.w_ready, r)
                        copy(gcur[:, :], gate[:, t % 2, bass.ds(h * TOPK + a * SLOTS, SLOTS)]).then_inc(s.gc_ready, 1)
                        dve.wait_ge(s.gc_ready, r + 1)
                        dots(r, a, h2[:, t, :], gcur[:, :])
                        if a == 0 and isinstance(h, int) and h == PH - 1 and t < NT - 1:
                            dve.wait_ge(s.sc_ready, (3, 4, NT + 2)[t])
                        if a == 0 and next_heads(t, h):
                            done = search(next_heads(t, h), searched(t, h) + lanes_in_use, base)
                            assert done == N_SEARCH * len(next_heads(t, h))
                            if isinstance(h, int):
                                steps[0] += done
                            if t and isinstance(h, int) and h == 0:
                                finish(t - 1, v_g2)
                head(0, steps[0])
                if t == 0:
                    dve.wait_ge(s.sc_ready, 2)
                per_head = N_SEARCH * lanes_in_use
                with dve.Fori(1, PH - 1) as h:
                    head(h, h * per_head + (steps[0] - per_head))
                steps[0] += (PH - 2) * per_head
                head(PH - 1, steps[0])
                if t == 0:
                    for g in range(2):
                        b = ring.to_read()
                        step(copy(h2sb[:, g * 512:(g + 1) * 512], b[:, :]), s.dring_free)
            dve.wait_ge(s.sel_in, 2 * 16 * NB)
            dots(2 * PH * NT, 0, h2sb, sgate)
            finish(NT - 1, v_g2)
            finish(NT, s_g2)


def layout(a):
    f = lambda v: np.ascontiguousarray(v, dtype=np.float32)
    blocks = lambda w: w.reshape(KT, P, -1, P).transpose(2, 1, 0, 3)
    w_in, w_ada = a["w_in"][0], a["w_ada"][0]
    aq, ak, av, conv, dec, bb, z, g_a, g_b = np.split(w_in, np.cumsum([512, 128, 128, 1536, 4, 4, 512, 1024]), axis=1)
    pair = [h * HD + i for g in range(HG) for h in (g, g + HG) for i in range(HD)]
    ada = w_ada.reshape(KT // 2, 2, P, -1, 512).transpose(3, 0, 2, 1, 4).reshape(-1, P, KT, P)
    branch = np.concatenate([a["w_att_out"][0][pair], a["w_delta_out"][0]], axis=0)
    projected = np.concatenate([blocks(conv), blocks(aq[:, pair]), blocks(z), blocks(g_a), blocks(g_b)])
    order, later = [], iter(ada[B_ADA1:])
    counts = [(0, n) for n in BEHIND] + [(n, 0) for n in AHEAD]
    for i, block in enumerate(projected):
        before, behind = counts[i] if i < len(counts) else (0, 0)
        order += [next(later) for _ in range(before)] + [block] + [next(later) for _ in range(behind)]
    wstream = np.concatenate([ada[:B_ADA1], np.stack(order), blocks(branch), blocks(a["w_query"][0])], axis=0)
    tile = lambda v: v.reshape(-1, P).T
    cols = np.concatenate(
        [
         a["w_conv"][0].reshape(4, CT_N, P).transpose(2, 1, 0).reshape(P, -1), tile(a["delta_norm"][0]),
         np.broadcast_to(a["attn_sinks"][0], (P, 8)), np.broadcast_to(a["a_log"][0], (P, 4)), np.broadcast_to(a["dt_bias"][0], (P, 4)),
         np.tile(a["attn_sinks"][0], 16)[:, None]], axis=1)
    c = np.concatenate([a["c_prompt"], a["c_sample"]], axis=0)
    return {
        "cT": f(c.T.reshape(KT, P, 1 + NB).transpose(1, 0, 2)),
        "x": f(a["x_prompt"][0]), "xs": f(a["x_sample"][:, 0]),
        "wstream": f(wstream), "wnat": f(np.concatenate([ak, av, dec, bb], axis=1).reshape(KT, P, NAT_W).transpose(1, 0, 2)),
        "wout": f(a["w_out"][0].reshape(KT, P, D).transpose(1, 0, 2)),
        "cols": f(cols), "rel": f(a["rel_bias"]),
        "rows": f(np.concatenate([a["b_ada"][0], a["g_pre_mix"][0], a["g_post_mix"][0], a["g_pre_ffn"][0], a["g_post_ffn"][0]]))[None],
        "cst": f(a["state_conv"][0].reshape(NB, 3, CT_N, P).transpose(3, 2, 0, 1)),
        "kc": f(a["cache_swa_k"][0].reshape(NB, WIN, P)), "vc": f(a["cache_swa_v"][0].reshape(NB, WIN, P)),
        "sdel": f(a["state_delta"][0].transpose(2, 1, 0, 3)),
        "skt": f(a["sub_keys"][0].transpose(2, 0, 1)),
        "eu": f(a["expert_u"][0]), "ev": f(a["expert_v"][0]),
    }


def constants():
    r, c = np.arange(P)[:, None], np.arange(P)[None, :]
    out = [r == c, r <= c, r > c, np.ones((P, P))]
    for lv in range(7):
        m = 1 << lv
        out.append((r // (2 * m) == c // (2 * m)) & (r % (2 * m) >= m) & (c % (2 * m) < m))
    out.append(np.broadcast_to(np.arange(TOPK), (P, TOPK)))
    out.append(r // TOPK == c[:, 0:NB])
    out.append((c // TOPK == r) & (r < NB))
    onehot = np.zeros((33, 384), np.float32)
    for i in range(384):
        d = 255 - i
        if 0 <= d < WIN:
            big = 16 + int(np.log(np.float32(max(d, 1)) / np.float32(16)) / np.float32(np.log(8.0)) * np.float32(16))
            onehot[d if d < 16 else min(big, 31), i] = 1.0
        else:
            onehot[32, i] = 1.0
    return {"consts": np.concatenate([np.asarray(o, np.float32) for o in out], axis=1), "onehot": onehot}


OUTS = {"yp": (SEQ, D), "ys": (NB, D), "kp": (WIN, P), "vp": (WIN, P), "convp": (P, CT_N, 3), "deltap": (P, 512),
        "ks": (NB, WIN, P), "vs": (NB, WIN, P), "convs": (P, CT_N, NB, 3), "deltas": (P, DH, NB, P)}


def kernel(**inputs):
    import concourse.bacc as bacc
    from concourse.bass_utils import run_bass_kernel_spmd

    nc = bacc.Bacc("TRN2", target_bir_lowering=False, num_devices=1)
    arrays = layout({k: np.asarray(v) for k, v in inputs.items()})
    arrays.update(constants())
    ins = {k: nc.dram_tensor("in_" + k, v.shape, F32, kind="ExternalInput").ap() for k, v in arrays.items()}
    ins["skew"] = nc.dram_tensor("skew", (HQ, P, 384), F32, kind="Internal").ap()
    ins["mod"] = nc.dram_tensor("mod", (NCOND, 4 * D), F32, kind="Internal").ap()
    ins["sidx"] = nc.dram_tensor("sidx", (NB, P), U32, kind="Internal").ap()
    ins["sgate"] = nc.dram_tensor("sgate", (NB, P), F32, kind="Internal").ap()
    outs = {k: nc.dram_tensor("out_" + k, v, F32, kind="ExternalOutput").ap() for k, v in OUTS.items()}
    build(nc, ins, outs)
    got = run_bass_kernel_spmd(nc, [{"in_" + k: v for k, v in arrays.items()}], core_ids=[0]).results[0]
    o = {k: got["out_" + k] for k in OUTS}
    win = lambda v: v.reshape(1, -1, WIN, 2, HD)
    return (o["yp"].reshape(1, SEQ, D), o["ys"].reshape(NB, 1, D), win(o["kp"]), win(o["vp"]),
            np.ascontiguousarray(o["convp"].transpose(2, 1, 0)).reshape(1, 1, 3, CT_N * P),
            np.ascontiguousarray(o["deltap"].reshape(P, DH, P).transpose(1, 0, 2)).reshape(1, 1, DH, P, P),
            win(o["ks"]), win(o["vs"]),
            np.ascontiguousarray(o["convs"].transpose(2, 3, 1, 0)).reshape(1, NB, 3, CT_N * P),
            np.ascontiguousarray(o["deltas"].transpose(2, 1, 0, 3)).reshape(1, NB, DH, P, P))
```
